# Optimizing a Trainium2 kernel written in Bass

```python
import jax, jax.numpy as jnp
from jax import lax
import numpy as np

D_MODEL = 1024
BATCH = 1
SEQ = 128
DEPTH = 1
DEC_BATCH = 1
DEC_SEQ = 512
PAST_LEN = 128

GRID_W = 64
D_MIX = D_MODEL
GLA_HEADS = 4
GLA_WIDTH = D_MIX // 2
GLA_DV = GLA_WIDTH // GLA_HEADS
GLA_DK = GLA_DV // 2
GLA_LOWRANK = 16
GLA_GATE_NORM = 16.0
GLA_CHUNK = 64
SGU_WIDTH = D_MIX - GLA_WIDTH
SGU_GROUPS = 4
SGU_CH = SGU_WIDTH // SGU_GROUPS
SGU_CHUNK = 128
N_EXPERTS = 16
EC_CAPACITY_FACTOR = 2
D_EXPERT = 2048
EPS = 1e-6

QK_W = GLA_HEADS * GLA_DK
OFF_Q = 0
OFF_K = OFF_Q + QK_W
OFF_V = OFF_K + QK_W
OFF_G = OFF_V + GLA_WIDTH
OFF_AF = OFF_G + GLA_WIDTH
OFF_AB = OFF_AF + GLA_LOWRANK
OFF_U = OFF_AB + GLA_LOWRANK
OFF_SV = OFF_U + SGU_WIDTH
D_IN = OFF_SV + SGU_WIDTH

kernel_name = "hybrid_gla_sgu_ecmoe_diffusion_step"

def rmsnorm(x, w):
    xf = x.astype(jnp.float32)
    y = xf * lax.rsqrt(jnp.mean(xf * xf, axis=-1, keepdims=True) + EPS)
    return (y * w.astype(jnp.float32)).astype(x.dtype)

def grid_sincos(n_tokens, dtype):
    rows = n_tokens // GRID_W
    r = jnp.broadcast_to(jnp.arange(rows, dtype=jnp.float32)[:, None], (rows, GRID_W)).reshape(-1)
    col = jnp.broadcast_to(jnp.arange(GRID_W, dtype=jnp.float32)[None, :], (rows, GRID_W)).reshape(-1)
    nf = D_MODEL // 4
    omega = 1.0 / (10000.0 ** (jnp.arange(nf, dtype=jnp.float32) / nf))
    def emb(p):
        a = p[:, None] * omega[None, :]
        return jnp.concatenate([jnp.sin(a), jnp.cos(a)], axis=-1)
    return jnp.concatenate([emb(r), emb(col)], axis=-1).astype(dtype)

def gla_chunked(q, k, v, log_a, s0):
    b, T, H, DK = q.shape
    DV = v.shape[-1]
    n = T // GLA_CHUNK
    f32 = jnp.float32
    q = q.astype(f32).reshape(b, n, GLA_CHUNK, H, DK)
    k = k.astype(f32).reshape(b, n, GLA_CHUNK, H, DK)
    v32 = v.astype(f32).reshape(b, n, GLA_CHUNK, H, DV)
    cum = jnp.cumsum(log_a.astype(f32).reshape(b, n, GLA_CHUNK, H, DK), axis=2)
    qe = q * jnp.exp(cum)
    ke = k * jnp.exp(-cum)
    mask = jnp.tril(jnp.ones((GLA_CHUNK, GLA_CHUNK), dtype=bool))
    att = jnp.einsum('bnihd,bnjhd->bnhij', qe, ke)
    att = jnp.where(mask[None, None, None], att, 0.0)
    o_intra = jnp.einsum('bnhij,bnjhe->bnihe', att, v32)
    last = cum[:, :, -1]
    kd = k * jnp.exp(last[:, :, None] - cum)
    ds = jnp.einsum('bnjhd,bnjhe->bnhde', kd, v32)
    def step(S, inp):
        dec, d = inp
        return dec[..., None] * S + d, S
    s_fin, s_starts = lax.scan(step, s0.astype(f32),
                               (jnp.moveaxis(jnp.exp(last), 1, 0), jnp.moveaxis(ds, 1, 0)))
    o_inter = jnp.einsum('bnihd,nbhde->bnihe', qe, s_starts)
    out = (o_intra + o_inter).reshape(b, T, H, DV)
    return out.astype(v.dtype), s_fin.astype(v.dtype)

def sgu_chunked(u_in, v_in, norm_w, ws, bs):
    b, T, _ = u_in.shape
    u = jax.nn.gelu(u_in)
    v = rmsnorm(jax.nn.gelu(v_in).reshape(b, T, SGU_GROUPS, SGU_CH), norm_w.reshape(SGU_GROUPS, SGU_CH))
    v = v.reshape(b, T // SGU_CHUNK, SGU_CHUNK, SGU_GROUPS, SGU_CH)
    vm = jnp.einsum('gpq,bnqgc->bnpgc', ws, v) + bs.T[None, None, :, :, None]
    return u * vm.reshape(b, T, SGU_WIDTH)

def ec_moe(x, router_w, w1, w3, w2):
    b, T, D = x.shape
    N = b * T
    xf = x.reshape(N, D)
    probs = jax.nn.softmax(jnp.matmul(xf.astype(jnp.float32), router_w.astype(jnp.float32)), axis=-1)
    cap = EC_CAPACITY_FACTOR * N // N_EXPERTS
    gates, idx = lax.top_k(probs.T, cap)
    xe = xf[idx]
    h = jax.nn.silu(jnp.einsum('ecd,edf->ecf', xe, w1)) * jnp.einsum('ecd,edf->ecf', xe, w3)
    ye = jnp.einsum('ecf,efd->ecd', h, w2) * gates[..., None].astype(x.dtype)
    out = jnp.zeros_like(xf).at[idx.reshape(-1)].add(ye.reshape(-1, D))
    return out.reshape(b, T, D)

def trunk_layer(x, mod, s0_f, s0_b, norm1_w, w_in, wa2_f, ba_f, wa2_b, ba_b, gla_norm_w,
                sgu_norm_w, sgu_ws, sgu_bs, w_out, norm2_w, router_w, w1, w3, w2):
    b, T, _ = x.shape
    shift1, scale1, gate1, shift2, scale2, gate2 = jnp.split(mod[:, None, :].astype(x.dtype), 6, axis=-1)
    h = rmsnorm(x, norm1_w) * (1.0 + scale1) + shift1
    p = jnp.matmul(h, w_in)
    q = p[..., OFF_Q:OFF_Q + QK_W].reshape(b, T, GLA_HEADS, GLA_DK) * (GLA_DK ** -0.5)
    k = p[..., OFF_K:OFF_K + QK_W].reshape(b, T, GLA_HEADS, GLA_DK)
    v = p[..., OFF_V:OFF_V + GLA_WIDTH].reshape(b, T, GLA_HEADS, GLA_DV)
    g = p[..., OFF_G:OFF_G + GLA_WIDTH]
    la_f = jax.nn.log_sigmoid((jnp.matmul(p[..., OFF_AF:OFF_AF + GLA_LOWRANK], wa2_f) + ba_f).astype(jnp.float32)) / GLA_GATE_NORM
    la_b = jax.nn.log_sigmoid((jnp.matmul(p[..., OFF_AB:OFF_AB + GLA_LOWRANK], wa2_b) + ba_b).astype(jnp.float32)) / GLA_GATE_NORM
    la_f = la_f.reshape(b, T, GLA_HEADS, GLA_DK)
    la_b = la_b.reshape(b, T, GLA_HEADS, GLA_DK)
    o_f, s_f = gla_chunked(q, k, v, la_f, s0_f)
    o_b, s_b = gla_chunked(jnp.flip(q, 1), jnp.flip(k, 1), jnp.flip(v, 1), jnp.flip(la_b, 1), s0_b)
    o = rmsnorm(o_f + jnp.flip(o_b, 1), gla_norm_w).reshape(b, T, GLA_WIDTH) * jax.nn.silu(g)
    s = sgu_chunked(p[..., OFF_U:OFF_U + SGU_WIDTH], p[..., OFF_SV:OFF_SV + SGU_WIDTH], sgu_norm_w, sgu_ws, sgu_bs)
    x = x + gate1 * jnp.matmul(jnp.concatenate([o, s], axis=-1), w_out)
    h2 = rmsnorm(x, norm2_w) * (1.0 + scale2) + shift2
    x = x + gate2 * ec_moe(h2, router_w, w1, w3, w2)
    return x, s_f, s_b

def setup_inputs(seed: int = 0) -> dict:
    key = jax.random.key(seed)
    ks = jax.random.split(key, 32)
    f32 = jnp.float32
    nrm = lambda i, shape, s: jax.random.normal(ks[i], shape, f32) * s
    st_shape = (DEC_BATCH, DEPTH, GLA_HEADS, GLA_DK, GLA_DV)
    return {
        "x_prompt": nrm(0, (BATCH, SEQ, D_MODEL), 1.0),
        "x_sample": nrm(1, (DEC_BATCH, DEC_SEQ, D_MODEL), 1.0),
        "state_gla_fwd": nrm(2, st_shape, 0.5),
        "state_gla_bwd": nrm(3, st_shape, 0.5),
        "c": nrm(4, (DEC_BATCH, D_MODEL), 1.0),
        "c_ctx": nrm(5, (D_MODEL,), 1.0),
        "ada_w": nrm(6, (DEPTH, D_MODEL, 6 * D_MODEL), 0.5 * D_MODEL ** -0.5),
        "ada_b": nrm(7, (DEPTH, 6 * D_MODEL), 0.02),
        "norm1_w": 1.0 + nrm(8, (DEPTH, D_MODEL), 0.02),
        "w_in": nrm(9, (DEPTH, D_MODEL, D_IN), D_MODEL ** -0.5),
        "gla_wa2_f": nrm(10, (DEPTH, GLA_LOWRANK, QK_W), GLA_LOWRANK ** -0.5),
        "gla_ba_f": nrm(11, (DEPTH, QK_W), 0.1),
        "gla_wa2_b": nrm(12, (DEPTH, GLA_LOWRANK, QK_W), GLA_LOWRANK ** -0.5),
        "gla_ba_b": nrm(13, (DEPTH, QK_W), 0.1),
        "gla_norm_w": 1.0 + nrm(14, (DEPTH, GLA_DV), 0.02),
        "sgu_norm_w": 1.0 + nrm(15, (DEPTH, SGU_WIDTH), 0.02),
        "sgu_ws": nrm(16, (DEPTH, SGU_GROUPS, SGU_CHUNK, SGU_CHUNK), SGU_CHUNK ** -0.5),
        "sgu_bs": 1.0 + nrm(17, (DEPTH, SGU_GROUPS, SGU_CHUNK), 0.02),
        "w_out": nrm(18, (DEPTH, D_MIX, D_MODEL), D_MIX ** -0.5),
        "norm2_w": 1.0 + nrm(19, (DEPTH, D_MODEL), 0.02),
        "router_w": nrm(20, (DEPTH, D_MODEL, N_EXPERTS), D_MODEL ** -0.5),
        "exp_w1": nrm(21, (DEPTH, N_EXPERTS, D_MODEL, D_EXPERT), D_MODEL ** -0.5),
        "exp_w3": nrm(22, (DEPTH, N_EXPERTS, D_MODEL, D_EXPERT), D_MODEL ** -0.5),
        "exp_w2": nrm(23, (DEPTH, N_EXPERTS, D_EXPERT, D_MODEL), D_EXPERT ** -0.5),
        "final_norm_w": 1.0 + nrm(24, (D_MODEL,), 0.02),
    }

def reference(x_prompt, x_sample, state_gla_fwd, state_gla_bwd, c, c_ctx, ada_w, ada_b, norm1_w, w_in,
              gla_wa2_f, gla_ba_f, gla_wa2_b, gla_ba_b, gla_norm_w, sgu_norm_w, sgu_ws, sgu_bs, w_out,
              norm2_w, router_w, exp_w1, exp_w3, exp_w2, final_norm_w):
    def layer_params(l):
        return (norm1_w[l], w_in[l], gla_wa2_f[l], gla_ba_f[l], gla_wa2_b[l], gla_ba_b[l], gla_norm_w[l],
                sgu_norm_w[l], sgu_ws[l], sgu_bs[l], w_out[l], norm2_w[l], router_w[l],
                exp_w1[l], exp_w3[l], exp_w2[l])

    xp = x_prompt
    zero_state = jnp.zeros((xp.shape[0], GLA_HEADS, GLA_DK, GLA_DV), xp.dtype)
    ctx_f, ctx_b = [], []
    for l in range(DEPTH):
        mod_ctx = (jnp.matmul(jax.nn.silu(c_ctx), ada_w[l]) + ada_b[l])[None, :]
        xp, s_f, s_b = trunk_layer(xp, mod_ctx, zero_state, zero_state, *layer_params(l))
        ctx_f.append(s_f)
        ctx_b.append(s_b)
    y_prompt = rmsnorm(xp, final_norm_w)
    new_state_gla_fwd = jnp.stack(ctx_f, axis=1)
    new_state_gla_bwd = jnp.stack(ctx_b, axis=1)

    xs = x_sample + grid_sincos(x_sample.shape[1], x_sample.dtype)[None]
    for l in range(DEPTH):
        mod = jnp.matmul(jax.nn.silu(c), ada_w[l]) + ada_b[l]
        xs, _, _ = trunk_layer(xs, mod, state_gla_fwd[:, l], state_gla_bwd[:, l], *layer_params(l))
    y_sample = rmsnorm(xs, final_norm_w)
    return (y_prompt, y_sample, new_state_gla_fwd, new_state_gla_bwd)


_drawn_inputs = setup_inputs


def setup_inputs(seed=0):
    import zlib

    import numpy as np

    out = dict(_drawn_inputs(seed))
    spreads = {}
    factors = {'state_gla_fwd': 8.0,
     'state_gla_bwd': 8.0,
     'gla_norm_w': 8.0,
     'sgu_norm_w': 8.0,
     'sgu_bs': 8.0,
     'norm2_w': 8.0,
     'final_norm_w': 2.873}
    for name, (base, spread) in spreads.items():
        noise = np.random.default_rng([zlib.crc32(name.encode()), seed]).standard_normal(out[name].shape)
        drawn = base * np.exp(spread * noise) if base else spread * noise
        out[name] = __import__('jax').numpy.asarray(drawn.astype(out[name].dtype))
    for name, factor in factors.items():
        out[name] = (out[name] * factor).astype(out[name].dtype)
    return out
```

```python
from contextlib import ExitStack

import numpy as np

import concourse.bass as bass
from concourse import mybir

ALU = mybir.AluOpType
ACT = mybir.ActivationFunctionType
F32 = mybir.dt.float32
I32 = mybir.dt.int32
AX_X = mybir.AxisListType.X

P = 128
D = 1024
KT = D // P
SAMPLE, PROMPT = 512, 128
TILES = (SAMPLE + PROMPT) // P
ST = SAMPLE // P
TOK = SAMPLE + PROMPT
HEADS, DK, DV = 4, 64, 128
CH = 64
CHUNKS = TOK // CH
SCH = SAMPLE // CH
LOWRANK = 16
GATE_NORM = 16.0
GROUPS = 4
EXPERTS = 16
FE = 2048
CAP_S, CAP_P = 2 * SAMPLE // EXPERTS, 2 * PROMPT // EXPERTS
SLOTS = CAP_S + CAP_P
GRID_W = 64
EPS = 1e-6
PAIRS = EXPERTS // 2

COL_QK, COL_V, COL_G, COL_A, COL_U, COL_SV = 0, 512, 1024, 1536, 1568, 2080

BANKS = 8
CHUNK_F = 4096
RING = 6
TRUNK_RING = 3

V_ADAB, V_C, V_CCTX, V_N1, V_N2, V_BS, V_BA, V_GLAW, V_ROWS = 0, 48, 56, 64, 72, 80, 84, 88, 89
SHIFT1, SCALE1, GATE1, SHIFT2, SCALE2, GATE2 = 0, 8, 16, 24, 32, 40


def shape_constants():
    j = np.arange(P)[:, None]
    i = np.arange(P)[None, :]
    same = (j // CH) == (i // CH)
    ident = np.eye(P, dtype=np.float32)
    fwd = (same & (j <= i)).astype(np.float32)
    bwd = (same & (j >= i)).astype(np.float32)
    keep = np.broadcast_to((np.arange(TOK) % CH != 0).astype(np.float32), (P, TOK))
    iota = np.broadcast_to(np.arange(CAP_S, dtype=np.float32), (P, CAP_S))
    table = np.concatenate([ident, fwd, bwd, keep, iota], axis=1).astype(np.float32)
    nf = D // 4
    omega = (1.0 / (np.float32(10000.0) ** (np.arange(nf, dtype=np.float32) / np.float32(nf)))).astype(np.float32)

    def emb(n):
        a = np.arange(n, dtype=np.float32)[:, None] * omega[None, :]
        return np.concatenate([np.sin(a), np.cos(a)], axis=-1).astype(np.float32)

    return table, emb(SAMPLE // GRID_W), emb(GRID_W)


def job_numbers():
    names = [("vec",), ("wsT",), ("ada", 0)]
    names += [("xT", k) for k in range(KT)] + [("xTp", h) for h in range(2)]
    names += [("qkP",)] + [("qkS", m) for m in range(4)]
    names += [("aS",), ("aP",)] + [("zS", h) for h in range(HEADS)] + [("zP",)]
    names += [("v", t) for t in range(TILES)] + [("g", t) for t in range(TILES)]
    names += [("kd", t) for t in range(TILES)] + [("ds", n) for n in range(CHUNKS)]
    names += [("u", t) for t in range(TILES)] + [("sv", t) for t in range(TILES)]
    names += [("mix", t) for t in range(TILES)]
    names += [("ada", 1), ("ada", 2)] + [("g1", q) for q in range(4)]
    for t in range(TILES + 2):
        if t < TILES:
            names += [("attF", t), ("attB", t)]
        if 1 <= t <= TILES:
            names += [("o", t - 1)]
        if t >= 2:
            names += [("mT", t - 2, 0), ("mT", t - 2, 1), ("out", t - 2, 0), ("out", t - 2, 1)]
    for t in range(TILES):
        names += [("hT", t, 0), ("hT", t, 1), ("logit", t)]
    names += [("pS",), ("pP",), ("ada", 3), ("rank",)]
    return {name: n for n, name in enumerate(names)}


JOB = job_numbers()
JOBS_TRUNK = len(JOB)

PAIR_JOBS = 40
X_S, X_P = lambda e: 2 * e, lambda e: 2 * e + 1
G_S, G_P = 4, 5
W1 = lambda e, f: 6 + 10 * e + 2 * f
W3 = lambda e, f: 7 + 10 * e + 2 * f
Y = lambda e, half: 14 + 10 * e + half
YT_S = lambda half: 26 + half
YT_P = lambda half: 28 + half
COMB = lambda t, half: 30 + 2 * t + half

TRUNK_CHUNKS = ([("ada", 512 * c) for c in range(4)]
                + [("in", c) for c in (COL_QK, COL_V, COL_G, COL_U, COL_SV)]
                + [("ada", 512 * c) for c in range(4, 10)]
                + [("out", 0), ("out", 512)]
                + [("ada", 512 * c) for c in range(10, 12)])
CHUNK_OF = {c: n for n, c in enumerate(TRUNK_CHUNKS)}
EXPERT_SLOT = [3, 4, 5, 1, 2, 0]
LOADS_BEFORE = [len([n for n in range(len(TRUNK_CHUNKS)) if n % TRUNK_RING == s]) if s < TRUNK_RING else 0
                for s in range(RING)]
PAIR_CHUNKS = 24
ADA_JOBS = [(0, [0, 1, 2, 3]), (1, [4, 5]), (2, [6, 7, 8, 9]), (3, [10, 11])]


def trunk_kernel(nc, x_prompt, x_sample, s0_f, s0_b, c, c_ctx, ada_w, ada_b, norm1_w, w_in, wa2_f, ba_f,
                 wa2_b, ba_b, gla_norm_w, sgu_norm_w, sgu_ws, sgu_bs, w_out, norm2_w, router_w, w1, w3, w2,
                 final_norm_w, table, pos_row, pos_col, y_prompt, y_sample, new_f, new_b):
    with ExitStack() as ctx:
        def sb(name, cols):
            return ctx.enter_context(nc.sbuf_tensor(name, [P, cols], F32))

        def sem(name):
            return ctx.enter_context(nc.semaphore(name))

        ring = sb("ring", RING * CHUNK_F)
        consts = sb("consts", 3 * P + TOK + CAP_S)
        ident = consts[:, 0:P]
        mask_f = consts[:, P:2 * P].bitcast(I32)
        mask_b = consts[:, 2 * P:3 * P].bitcast(I32)
        keep = consts[:, 3 * P:3 * P + TOK]
        iota = consts[:, 3 * P + TOK:3 * P + TOK + CAP_S]
        vecs = sb("vecs", 96)
        silu_c = sb("silu_c", 2 * KT)[:].rearrange("p (k w) -> p k w", w=2)
        mod = sb("mod", 96)[:].rearrange("p (k w) -> p k w", w=2)
        amp1 = sb("amp1", 2 * KT)[:].rearrange("p (k w) -> p k w", w=2)
        amp2 = sb("amp2", 2 * KT)[:].rearrange("p (k w) -> p k w", w=2)
        router = sb("router", KT * EXPERTS)[:].rearrange("p (k e) -> p k e", e=EXPERTS)
        router_amp = sb("router_amp", 2 * KT * EXPERTS)[:].rearrange("p (w k e) -> p w k e", w=2, e=EXPERTS)
        x = sb("x", TILES * D)[:].rearrange("p (t d) -> p t d", t=TILES)
        feat = sb("feat", TILES * D)
        hT = feat[:].rearrange("p (k n) -> p k n", k=KT)
        xn2 = feat[:].rearrange("p (t d) -> p t d", t=TILES)
        probs = sb("probs", TILES * 18)[:].rearrange("p (t e) -> p t e", t=TILES)
        rank = sb("rank", TILES * 18)[:].rearrange("p (t e) -> p t e", t=TILES)
        stats = sb("stats", 160)
        chunk_decay = sb("chunk_decay", HEADS * CHUNKS)[:].rearrange("p (h n) -> p h n", h=HEADS)

        up = TRUNK_RING * CHUNK_F
        q = ring[:, up:up + 2560].rearrange("p (h n) -> p h n", h=HEADS)
        k = ring[:, up + 2560:up + 5120].rearrange("p (h n) -> p h n", h=HEADS)
        v = ring[:, up + 5120:up + 7680].rearrange("p (t n) -> p t n", t=TILES)
        g = ring[:, up + 7680:up + 10240].rearrange("p (t n) -> p t n", t=TILES)
        att = ring[:, up + 10240:up + 12288].rearrange("p (b d h n) -> p b d h n", b=2, d=2, h=HEADS)
        pos_r = ring[:, up:up + 2048].rearrange("p (t n) -> p t n", t=ST)
        pos_c = ring[:, up + 2048:up + 2560]

        both = sb("both", 15872)
        z = both[:, 0:2560]
        cum = both[:, 2560:5120]
        rem = both[:, 5120:7680]
        states = both[:, 0:5120].rearrange("p (n h e) -> p n h e", n=CHUNKS, h=HEADS)
        xn = both[:, 0:5120].rearrange("p (t d) -> p t d", t=TILES)
        gate1_rows = both[:, 5120:7168].rearrange("p (w d) -> p w d", w=2)
        kd = both[:, 7680:10240].rearrange("p (t h d) -> p t h d", t=TILES, h=HEADS)
        a_up = both[0:2 * LOWRANK, 7680:8192].rearrange("p (h n) -> p h n", h=HEADS)
        aT = both[0:2 * LOWRANK, 8192:8832]
        w_a = both[:, 8832:9088].rearrange("p (k n) -> p k n", k=KT)
        vec_rows = both[:, 9088:9216]
        ws = both[:, 9216:9728].rearrange("p (g n) -> p g n", g=GROUPS)
        o_tok = both[:, 7680:8704].rearrange("p (b n) -> p b n", b=2)
        o_sq = both[:, 8704:9216]
        out_tmp = both[:, 9216:10240].rearrange("p (b n) -> p b n", b=2)
        s = both[:, 10240:12800].rearrange("p (t n) -> p t n", t=TILES)
        mixT = both[:, 12800:14848].rearrange("p (b k n) -> p b k n", b=2, k=KT)
        sgu_sq = both[:, 13824:14336]
        fin = both[:, 14336:14848].rearrange("p (h e) -> p h e", h=HEADS)
        wsT = both[:, 14848:15360].rearrange("p (g n) -> p g n", g=GROUPS)
        sgu_w = both[:, 15360:15872]
        top_work = both[0:EXPERTS, 10240:10880]
        top_mask = both[0:EXPERTS, 10880:11520]
        top_rank = both[0:EXPERTS, 11520:12160]
        top8 = both[0:EXPERTS, 12160:12168]

        xe = both[:, 0:1280].rearrange("p (e k n) -> p e k n", e=2, k=KT)
        h = both[:, 1280:3840].rearrange("p (e f n) -> p e f n", e=2, f=FE // P)
        yT_s = both[:, 3840:4864].rearrange("p (k n) -> p k n", k=KT)
        yT_p = both[:, 4864:5120].rearrange("p (k n) -> p k n", k=KT)
        y_s = both[:, 5120:6144]
        y_p = both[0:2 * CAP_P, 6144:7168]
        hot_s = both[:, 7168:7680].rearrange("p (t e n) -> p t e n", t=ST, e=2)
        hot_p = both[:, 7680:7712].rearrange("p (e n) -> p e n", e=2)
        gate_s = both[:, 7712:8224].rearrange("p (t e n) -> p t e n", t=ST, e=2)
        gate_p = both[:, 8224:8256].rearrange("p (e n) -> p e n", e=2)
        gT_s = both[:, 8256:8768]
        gT_p = both[0:2 * CAP_P, 8768:8896]
        silu_h = both[:, 8896:9536].rearrange("p (b n) -> p b n", b=2)
        comb_rk = both[:, 9536:9546].rearrange("p (t e) -> p t e", e=2)
        comb_pr = both[:, 9546:9556].rearrange("p (t e) -> p t e", e=2)
        final_w = both[:, 12288:13312]
        y_out = both[:, 9728:11776].rearrange("p (b d) -> p b d", b=2)

        def s_vn(t):
            return both[:, 7680 + 512 * t:8192 + 512 * t]

        psum = ctx.enter_context(nc.psum_tensor("psum", [P, BANKS, 512], F32))

        psum_filled = [sem(f"psum_filled{b}") for b in range(BANKS)]
        psum_stored = [sem(f"psum_stored{b}") for b in range(BANKS)]
        slot_loaded = [sem(f"slot_loaded{s}") for s in range(RING)]
        chunk_read = sem("chunk_read")
        w2_half_read = sem("w2_half_read")
        consts_loaded = sem("consts_loaded")
        vecs_loaded = sem("vecs_loaded")
        ws_loaded = sem("ws_loaded")
        x_loaded = [sem(f"x_loaded{t}") for t in range(TILES)]
        pos_loaded = sem("pos_loaded")
        wa_zeroed = sem("wa_zeroed")
        wa_loaded = sem("wa_loaded")
        router_loaded = sem("router_loaded")
        sguw_loaded = sem("sguw_loaded")
        s0_loaded = sem("s0_loaded")
        final_loaded = sem("final_loaded")
        pool_zeroed = sem("pool_zeroed")
        vec_step = sem("vec_step")
        act_step = sem("act_step")
        vec_pair_step = sem("vec_pair_step")
        vec_final_step = sem("vec_final_step")
        silu_c_ready = sem("silu_c_ready")
        x_pos_ready = sem("x_pos_ready")
        x_squared = sem("x_squared")
        x_recip = sem("x_recip")
        x_rs = sem("x_rs")
        xn_ready = sem("xn_ready")
        mod_ready = sem("mod_ready")
        z_ln = sem("z_ln")
        cum_ready = sem("cum_ready")
        rem_ready = sem("rem_ready")
        exp_cum = sem("exp_cum")
        exp_neg = sem("exp_neg")
        exp_rem = sem("exp_rem")
        decay_ready = sem("decay_ready")
        qe_ready = sem("qe_ready")
        kdT_ready = sem("kdT_ready")
        ke_ready = sem("ke_ready")
        ds_stored = sem("ds_stored")
        fin_ready = sem("fin_ready")
        sgu_recip = sem("sgu_recip")
        sgu_rs = sem("sgu_rs")
        sgu_vn_ready = sem("sgu_vn_ready")
        s_ready = sem("s_ready")
        o_recip = sem("o_recip")
        o_rs = sem("o_rs")
        o_ready = sem("o_ready")
        x1_ready = sem("x1_ready")
        x1_squared = sem("x1_squared")
        x1_recip = sem("x1_recip")
        x1_rs = sem("x1_rs")
        xn2_ready = sem("xn2_ready")
        router_amp_ready = sem("router_amp_ready")
        max_ready = sem("max_ready")
        exp_ready = sem("exp_ready")
        probs_ready = sem("probs_ready")
        rank_rows_ready = sem("rank_rows_ready")
        hot_ready = sem("hot_ready")
        y_squared = sem("y_squared")
        y_recip = sem("y_recip")
        y_rs = sem("y_rs")
        y_ready = sem("y_ready")
        y_saved = [sem(f"y_saved{b}") for b in range(2)]
        state_saved = sem("state_saved")

        def bank(n):
            return psum[:, n % BANKS, :]

        def wait_filled(eng, n, pair=None):
            eng.wait_ge(psum_filled[n % BANKS], n // BANKS + 1 + (0 if pair is None else pair * (PAIR_JOBS // BANKS)))

        def wait_stored(eng, n, pair=None):
            eng.wait_ge(psum_stored[n % BANKS], n // BANKS + 1 + (0 if pair is None else pair * (PAIR_JOBS // BANKS)))

        def wait_bank_free(pe, n, pair=None):
            if n >= BANKS:
                wait_stored(pe, n - BANKS, pair)

        def filled(ins, n):
            ins.then_inc(psum_filled[n % BANKS], 1)

        def stored(ins, n):
            ins.then_inc(psum_stored[n % BANKS], 1)

        def chunk(slot):
            return ring[:, slot * CHUNK_F:(slot + 1) * CHUNK_F]

        def wait_trunk_chunk(pe, n):
            pe.wait_ge(slot_loaded[n % TRUNK_RING], 16 * (n // TRUNK_RING + 1))
            return chunk(n % TRUNK_RING).rearrange("p (k n) -> p k n", k=KT)

        def wait_expert_chunk(pe, m, pair):
            slot = EXPERT_SLOT[m % RING]
            pe.wait_ge(slot_loaded[slot], 16 * (LOADS_BEFORE[slot] + m // RING + 1) + pair * (16 * PAIR_CHUNKS // RING))
            return chunk(slot)

        def wait_trunk_chunk_read(sp, n):
            name, col = TRUNK_CHUNKS[n]
            if name == "ada":
                inside = 0
                for i, part in ADA_JOBS:
                    if col // 512 == part[-1]:
                        return wait_filled(sp, JOB["ada", i])
                    if col // 512 in part:
                        return sp.wait_ge(chunk_read, inside + part.index(col // 512) + 1)
                    inside += len(part) - 1
            elif name == "in":
                last = {COL_QK: ("qkP",), COL_V: ("v", TILES - 1), COL_G: ("g", TILES - 1),
                        COL_U: ("u", TILES - 1), COL_SV: ("sv", TILES - 1)}[col]
                wait_filled(sp, JOB[last])
            else:
                wait_filled(sp, JOB["out", TILES - 1, col // 512])

        def wait_expert_chunk_read(sp, m, pair):
            back, m = (1, m + PAIR_CHUNKS) if m < 0 else (0, m)
            e, i = divmod(m, 12)
            when = pair - back
            if i < 8:
                wait_filled(sp, JOBS_TRUNK + (W1(e, i // 2) if i % 2 == 0 else W3(e, i // 2)), when)
            elif i in (8, 10):
                sp.wait_ge(w2_half_read, 2 * e + (i - 8) // 2 + 1 + when * 4)
            else:
                wait_filled(sp, JOBS_TRUNK + Y(e, (i - 9) // 2), when)

        sample_x = x_sample.rearrange("b (t p) d -> p (b t) d", p=P)
        prompt_x = x_prompt.rearrange("b p d -> p (b d)")
        ada_k = ada_w[0].rearrange("(k p) n -> p k n", p=P)
        in_k = w_in[0].rearrange("(k p) n -> p k n", p=P)
        out_k = w_out[0].rearrange("(k p) n -> p k n", p=P)

        block = ctx.enter_context(nc.Block())

        @block.sync
        def _(sp):
            sp.dma_start(consts[:], table).then_inc(consts_loaded, 16)
            for t in range(ST):
                sp.dma_start(x[:, t, :], sample_x[:, t, :]).then_inc(x_loaded[t], 16)
            sp.dma_start(x[:, ST, :], prompt_x).then_inc(x_loaded[ST], 16)
            for n, (name, col) in enumerate(TRUNK_CHUNKS):
                if n >= TRUNK_RING:
                    wait_trunk_chunk_read(sp, n - TRUNK_RING)
                src = {"ada": ada_k, "in": in_k, "out": out_k}[name][:, :, col:col + 512]
                sp.dma_start(chunk(n % TRUNK_RING).rearrange("p (k n) -> p k n", k=KT), src)\
                    .then_inc(slot_loaded[n % TRUNK_RING], 16)
                if n == 8:
                    sp.wait_ge(qe_ready, 1)
                    sp.wait_ge(ke_ready, 1)
                    sp.dma_start(states[0:DK, 0, :, :], s0_f[0, 0].rearrange("h d e -> d h e"))\
                        .then_inc(s0_loaded, 16)
                    sp.dma_start(states[DK:P, SCH - 1, :, :], s0_b[0, 0].rearrange("h d e -> d h e"))\
                        .then_inc(s0_loaded, 16)
                if n == 16:
                    sp.wait_ge(fin_ready, 1)
                    sp.dma_start(new_f[0, 0].rearrange("h d e -> d h e"), fin[0:DK, :, :]).then_inc(state_saved, 16)
                    sp.dma_start(new_b[0, 0].rearrange("h d e -> d h e"), fin[DK:P, :, :]).then_inc(state_saved, 16)

            def load_expert_chunk(m, pair):
                e, i = divmod(m, 12)
                slot = EXPERT_SLOT[m % RING]
                expert = 2 * pair + e
                if i < 8:
                    w = (w1, w3)[i % 2]
                    src = w[0, bass.ds(expert, 1)].rearrange("a (k p) n -> p (a k) n", p=P)[:, :, (i // 2) * 512:(i // 2) * 512 + 512]
                    dst = chunk(slot).rearrange("p (k n) -> p k n", k=KT)
                else:
                    src = w2[0, bass.ds(expert, 1)].rearrange("a (k p) n -> p (a k) n", p=P)[:, :, (i - 8) * 256:(i - 8) * 256 + 256]
                    dst = chunk(slot).rearrange("p (k n) -> p k n", k=FE // P)
                sp.dma_start(dst, src).then_inc(slot_loaded[slot], 16)

            wait_filled(sp, JOB["mT", TILES - 1, 1])
            sp.wait_ge(o_ready, TILES)
            for m in range(RING):
                if m >= 3:
                    wait_trunk_chunk_read(sp, {3: 16, 4: 17, 5: 18}[m])
                load_expert_chunk(m, 0)
            for m in range(RING, PAIR_CHUNKS):
                wait_expert_chunk_read(sp, m - RING, 0)
                load_expert_chunk(m, 0)
            with sp.Fori(1, PAIRS) as pair:
                for m in range(PAIR_CHUNKS):
                    wait_expert_chunk_read(sp, m - RING, pair)
                    load_expert_chunk(m, pair)

            for t in range(TILES):
                sp.wait_ge(y_ready, t + 1)
                dst = (y_sample.rearrange("b (t p) d -> p (b t) d", p=P)[:, t, :] if t < ST
                       else y_prompt.rearrange("b p d -> p (b d)"))
                sp.dma_start(dst, y_out[:, t % 2, :]).then_inc(y_saved[t % 2], 16)
            sp.wait_ge(y_saved[0], 16 * 3)
            sp.wait_ge(y_saved[1], 16 * 2)
            sp.wait_ge(state_saved, 32)

        @block.gpsimd
        def _(pool):
            rows = [(V_ADAB, ada_b.rearrange("a (k n) -> (a k) n", n=P)), (V_C, c.rearrange("a (k n) -> (a k) n", n=P)),
                    (V_CCTX, c_ctx.rearrange("(k n) -> k n", n=P)), (V_N1, norm1_w.rearrange("a (k n) -> (a k) n", n=P)),
                    (V_N2, norm2_w.rearrange("a (k n) -> (a k) n", n=P)), (V_BS, sgu_bs[0]), (V_GLAW, gla_norm_w)]
            for row, src in rows:
                pool.dma_start(vec_rows[row:row + src.shape[0], :], src).then_inc(vecs_loaded, 16)
            pool.dma_start(vec_rows[V_BA:V_BA + HEADS, 0:DK], ba_f.rearrange("a (h n) -> (a h) n", n=DK)).then_inc(vecs_loaded, 16)
            pool.dma_start(vec_rows[V_BA:V_BA + HEADS, DK:P], ba_b.rearrange("a (h n) -> (a h) n", n=DK)).then_inc(vecs_loaded, 16)
            for t in range(ST):
                for half in range(2):
                    pool.dma_start(pos_r[64 * half:64 * half + 64, t, :],
                                   pos_row[2 * t + half:2 * t + half + 1, :].to_broadcast([64, 512])).then_inc(pos_loaded, 16)
            for half in range(2):
                pool.dma_start(pos_c[64 * half:64 * half + 64, :], pos_col).then_inc(pos_loaded, 16)
            pool.dma_start(ws, sgu_ws[0].rearrange("g p q -> p g q")).then_inc(ws_loaded, 16)
            nc.gpsimd.memset(a_up, 0.0).then_inc(wa_zeroed, 1)
            nc.gpsimd.memset(att, 0.0).then_inc(pool_zeroed, 1)
            nc.gpsimd.memset(probs, 0.0).then_inc(pool_zeroed, 1)
            nc.gpsimd.memset(rank, 0.0).then_inc(pool_zeroed, 1)
            pool.wait_ge(wa_zeroed, 1)
            pool.dma_start(a_up[0:LOWRANK, :, 0:DK], wa2_f[0].rearrange("r (h n) -> r h n", n=DK)).then_inc(wa_loaded, 16)
            pool.dma_start(a_up[LOWRANK:2 * LOWRANK, :, DK:P], wa2_b[0].rearrange("r (h n) -> r h n", n=DK)).then_inc(wa_loaded, 16)
            pool.dma_start(w_a, in_k[:, :, COL_A:COL_A + 2 * LOWRANK]).then_inc(wa_loaded, 16)
            pool.dma_start(router, router_w[0].rearrange("(k p) e -> p k e", p=P)).then_inc(router_loaded, 16)
            pool.dma_start(sgu_w, sgu_norm_w.to_broadcast([P, 512])).then_inc(sguw_loaded, 16)
            wait_filled(pool, JOB["rank",])
            pool.dma_start(final_w, final_norm_w.rearrange("(a n) -> a n", a=1).to_broadcast([P, D])).then_inc(final_loaded, 16)

        @block.tensor
        def _(pe):
            def ada(i, parts):
                n = JOB["ada", i]
                wait_bank_free(pe, n)
                for at, c4 in enumerate(parts):
                    w = wait_trunk_chunk(pe, CHUNK_OF["ada", 512 * c4])
                    for j in range(4):
                        col = 2 * (4 * at + j)
                        for kt in range(KT):
                            mm = nc.tensor.matmul(bank(n)[:, col:col + 2], w[:, kt, j * P:(j + 1) * P], silu_c[:, kt, :],
                                                  start=(kt == 0), stop=(kt == KT - 1))
                    if c4 == parts[-1]:
                        filled(mm, n)
                    else:
                        mm.then_inc(chunk_read, 1)

            def project(name, col):
                w = wait_trunk_chunk(pe, CHUNK_OF["in", col])
                for t in range(TILES):
                    n = JOB[name, t]
                    wait_bank_free(pe, n)
                    for kt in range(KT):
                        mm = nc.tensor.matmul(bank(n), hT[:, kt, t * P:(t + 1) * P], w[:, kt, :],
                                              start=(kt == 0), stop=(kt == KT - 1))
                    filled(mm, n)

            pe.wait_ge(consts_loaded, 16)
            pe.wait_ge(vecs_loaded, 16 * 9)
            n = JOB["vec",]
            filled(nc.tensor.transpose(bank(n)[:, 0:V_ROWS], vec_rows[0:V_ROWS, :], ident[0:V_ROWS, 0:V_ROWS]), n)
            pe.wait_ge(ws_loaded, 16)
            n = JOB["wsT",]
            for gr in range(GROUPS):
                mm = nc.tensor.transpose(bank(n)[:, gr * P:(gr + 1) * P], ws[:, gr, :], ident)
            filled(mm, n)
            pe.wait_ge(silu_c_ready, 1)
            ada(0, ADA_JOBS[0][1])
            pe.wait_ge(xn_ready, TILES)
            for kt in range(KT):
                n = JOB["xT", kt]
                wait_bank_free(pe, n)
                for t in range(ST):
                    mm = nc.tensor.transpose(bank(n)[:, t * P:(t + 1) * P], xn[:, t, kt * P:(kt + 1) * P], ident)
                filled(mm, n)
            for half in range(2):
                n = JOB["xTp", half]
                wait_bank_free(pe, n)
                for j in range(4):
                    kt = 4 * half + j
                    mm = nc.tensor.transpose(bank(n)[:, j * P:(j + 1) * P], xn[:, ST, kt * P:(kt + 1) * P], ident)
                filled(mm, n)
            for kt in range(KT):
                wait_stored(pe, JOB["xT", kt])
            for half in range(2):
                wait_stored(pe, JOB["xTp", half])
            w = wait_trunk_chunk(pe, CHUNK_OF["in", COL_QK])
            nP = JOB["qkP",]
            wait_bank_free(pe, nP)
            for m in range(4):
                n = JOB["qkS", m]
                wait_bank_free(pe, n)
                for kt in range(KT):
                    mm = nc.tensor.matmul(bank(n), w[:, kt, m * P:(m + 1) * P], hT[:, kt, 0:SAMPLE],
                                          start=(kt == 0), stop=(kt == KT - 1))
                    mp = nc.tensor.matmul(bank(nP)[:, m * P:(m + 1) * P], w[:, kt, m * P:(m + 1) * P], hT[:, kt, SAMPLE:TOK],
                                          start=(kt == 0), stop=(kt == KT - 1))
                filled(mm, n)
            filled(mp, nP)
            pe.wait_ge(wa_loaded, 48)
            for name, lo, hi in (("aS", 0, SAMPLE), ("aP", SAMPLE, TOK)):
                n = JOB[name,]
                wait_bank_free(pe, n)
                for kt in range(KT):
                    mm = nc.tensor.matmul(bank(n)[0:2 * LOWRANK, 0:hi - lo], w_a[:, kt, :], hT[:, kt, lo:hi],
                                          start=(kt == 0), stop=(kt == KT - 1))
                filled(mm, n)
            wait_stored(pe, JOB["aS",])
            wait_stored(pe, JOB["aP",])
            for hd in range(HEADS):
                n = JOB["zS", hd]
                wait_bank_free(pe, n)
                filled(nc.tensor.matmul(bank(n), a_up[:, hd, :], aT[:, 0:SAMPLE], start=True, stop=True), n)
            n = JOB["zP",]
            wait_bank_free(pe, n)
            for hd in range(HEADS):
                mm = nc.tensor.matmul(bank(n)[:, hd * P:(hd + 1) * P], a_up[:, hd, :], aT[:, SAMPLE:TOK], start=True, stop=True)
            filled(mm, n)
            project("v", COL_V)
            project("g", COL_G)
            pe.wait_ge(kdT_ready, 1)
            kdT = rem.rearrange("p (h n) -> p h n", h=HEADS)
            for t in range(TILES):
                n = JOB["kd", t]
                wait_bank_free(pe, n)
                for hd in range(HEADS):
                    mm = nc.tensor.transpose(bank(n)[:, hd * P:(hd + 1) * P], kdT[:, hd, t * P:(t + 1) * P], ident)
                filled(mm, n)
            for ck in range(CHUNKS):
                n = JOB["ds", ck]
                t, lo = ck // 2, (ck % 2) * CH
                if ck % 2 == 0:
                    wait_stored(pe, JOB["v", t])
                    wait_stored(pe, JOB["kd", t])
                wait_bank_free(pe, n)
                for hd in range(HEADS):
                    mm = nc.tensor.matmul(bank(n)[:, hd * P:(hd + 1) * P], kd[lo:lo + CH, t, hd, :],
                                          v[lo:lo + CH, t, hd * P:(hd + 1) * P], start=True, stop=True)
                filled(mm, n)
            project("u", COL_U)
            project("sv", COL_SV)
            wait_stored(pe, JOB["wsT",])
            for t in range(TILES):
                n = JOB["mix", t]
                pe.wait_ge(sgu_vn_ready, t + 1)
                wait_bank_free(pe, n)
                for gr in range(GROUPS):
                    mm = nc.tensor.matmul(bank(n)[:, gr * P:(gr + 1) * P], wsT[:, gr, :],
                                          s_vn(t)[:, gr * P:(gr + 1) * P], start=True, stop=True)
                filled(mm, n)
            ada(1, ADA_JOBS[1][1])
            ada(2, ADA_JOBS[2][1])
            wait_stored(pe, JOB["ada", 1])
            for qd in range(4):
                n = JOB["g1", qd]
                wait_bank_free(pe, n)
                for j in range(4):
                    mm = nc.tensor.matmul(bank(n)[:, j * P:(j + 1) * P],
                                          mod[:, GATE1 + 4 * (qd % 2) + j, qd // 2:qd // 2 + 1].to_broadcast([P, P]), ident,
                                          start=True, stop=True)
                filled(mm, n)

            def attention(t):
                for d, name in ((0, "attF"), (1, "attB")):
                    n = JOB[name, t]
                    wait_bank_free(pe, n)
                    for hd in range(HEADS):
                        mm = nc.tensor.matmul(bank(n)[:, hd * P:(hd + 1) * P], k[d * DK:(d + 1) * DK, hd, t * P:(t + 1) * P],
                                              q[d * DK:(d + 1) * DK, hd, t * P:(t + 1) * P], start=True, stop=True)
                    filled(mm, n)

            def gla_out(t):
                n = JOB["o", t]
                wait_bank_free(pe, n)
                wait_stored(pe, JOB["attF", t])
                wait_stored(pe, JOB["attB", t])
                for hd in range(HEADS):
                    o = bank(n)[:, hd * P:(hd + 1) * P]
                    vh = v[:, t, hd * P:(hd + 1) * P]
                    nc.tensor.matmul(o, att[:, t % 2, 0, hd, :], vh, start=True, stop=False, skip_group_check=True)
                    nc.tensor.matmul(o, att[:, t % 2, 1, hd, :], vh, start=False, stop=False, skip_group_check=True)
                    for half in range(2):
                        ck = 2 * t + half
                        mm = nc.tensor.matmul(o[half * CH:(half + 1) * CH, :], q[:, hd, ck * CH:(ck + 1) * CH],
                                              states[:, ck, hd, :], start=False, stop=True, skip_group_check=True)
                filled(mm, n)

            def mix_turn(t):
                pe.wait_ge(o_ready, t + 1)
                pe.wait_ge(s_ready, TILES)
                for half in range(2):
                    n = JOB["mT", t, half]
                    wait_bank_free(pe, n)
                    src = o_tok[:, t % 2, :] if half == 0 else s[:, t, :]
                    for j in range(4):
                        mm = nc.tensor.transpose(bank(n)[:, j * P:(j + 1) * P], src[:, j * P:(j + 1) * P], ident)
                    filled(mm, n)
                wait_stored(pe, JOB["mT", t, 0])
                wait_stored(pe, JOB["mT", t, 1])
                for half in range(2):
                    w = wait_trunk_chunk(pe, CHUNK_OF["out", 512 * half])
                    n = JOB["out", t, half]
                    wait_bank_free(pe, n)
                    for kt in range(KT):
                        mm = nc.tensor.matmul(bank(n), mixT[:, t % 2, kt, :], w[:, kt, :], start=(kt == 0), stop=(kt == KT - 1))
                    filled(mm, n)

            pe.wait_ge(qe_ready, 1)
            pe.wait_ge(ke_ready, 1)
            pe.wait_ge(fin_ready, 1)
            for t in range(TILES + 2):
                if t < TILES:
                    attention(t)
                if 1 <= t <= TILES:
                    gla_out(t - 1)
                if t >= 2:
                    mix_turn(t - 2)
            pe.wait_ge(router_amp_ready, 1)
            for t in range(TILES):
                pe.wait_ge(xn2_ready, t + 1)
                for half in range(2):
                    n = JOB["hT", t, half]
                    wait_bank_free(pe, n)
                    for j in range(4):
                        kt = 4 * half + j
                        mm = nc.tensor.transpose(bank(n)[:, j * P:(j + 1) * P], xn2[:, t, kt * P:(kt + 1) * P], ident)
                    filled(mm, n)
                w = 0 if t < ST else 1
                n = JOB["logit", t]
                wait_bank_free(pe, n)
                for kt in range(KT):
                    nc.tensor.matmul(bank(n)[:, 0:EXPERTS], mod[:, SHIFT2 + kt, w:w + 1].to_broadcast([P, P]), router[:, kt, :],
                                     start=(kt == 0), stop=False)
                wait_stored(pe, JOB["hT", t, 0])
                wait_stored(pe, JOB["hT", t, 1])
                for kt in range(KT):
                    mm = nc.tensor.matmul(bank(n)[:, 0:EXPERTS], mixT[:, t % 2, kt, :], router_amp[:, w, kt, :],
                                          start=False, stop=(kt == KT - 1))
                filled(mm, n)
            pe.wait_ge(probs_ready, TILES)
            n = JOB["pS",]
            wait_bank_free(pe, n)
            for t in range(ST):
                mm = nc.tensor.transpose(bank(n)[0:EXPERTS, t * P:(t + 1) * P], probs[:, t, 0:EXPERTS], ident)
            filled(mm, n)
            n = JOB["pP",]
            wait_bank_free(pe, n)
            filled(nc.tensor.transpose(bank(n)[0:EXPERTS, 0:P], probs[:, ST, 0:EXPERTS], ident), n)
            ada(3, ADA_JOBS[3][1])
            pe.wait_ge(rank_rows_ready, 1)
            n = JOB["rank",]
            wait_bank_free(pe, n)
            for t in range(TILES):
                mm = nc.tensor.transpose(bank(n)[:, t * EXPERTS:(t + 1) * EXPERTS], top_rank[:, t * P:(t + 1) * P],
                                         ident[0:EXPERTS, 0:EXPERTS])
            filled(mm, n)

            with pe.Fori(0, PAIRS) as pair:
                J = JOBS_TRUNK
                pe.wait_ge(hot_ready, 4 + pair * 4)
                for e in range(2):
                    n = J + X_S(e)
                    wait_bank_free(pe, n, pair)
                    for kt in range(KT):
                        for t in range(ST):
                            mm = nc.tensor.matmul(bank(n)[:, kt * CAP_S:(kt + 1) * CAP_S], xn2[:, t, kt * P:(kt + 1) * P],
                                                  hot_s[:, t, e, :], start=(t == 0), stop=(t == ST - 1))
                    filled(mm, n)
                    n = J + X_P(e)
                    wait_bank_free(pe, n, pair)
                    for kt in range(KT):
                        mm = nc.tensor.matmul(bank(n)[:, kt * CAP_P:(kt + 1) * CAP_P], xn2[:, ST, kt * P:(kt + 1) * P],
                                              hot_p[:, e, :], start=True, stop=True)
                    filled(mm, n)
                n = J + G_S
                wait_bank_free(pe, n, pair)
                for t in range(ST):
                    mm = nc.tensor.transpose(bank(n)[:, t * P:(t + 1) * P], gate_s[:, t, :, :], ident)
                filled(mm, n)
                n = J + G_P
                wait_bank_free(pe, n, pair)
                filled(nc.tensor.transpose(bank(n)[0:2 * CAP_P, 0:P], gate_p, ident), n)
                for e in range(2):
                    wait_stored(pe, J + X_S(e), pair)
                    wait_stored(pe, J + X_P(e), pair)
                    for f4 in range(4):
                        for which, job in ((0, W1), (1, W3)):
                            n = J + job(e, f4)
                            w = wait_expert_chunk(pe, 12 * e + 2 * f4 + which, pair).rearrange("p (k n) -> p k n", k=KT)
                            wait_bank_free(pe, n, pair)
                            for j in range(4):
                                for kt in range(KT):
                                    mm = nc.tensor.matmul(bank(n)[:, j * SLOTS:(j + 1) * SLOTS], w[:, kt, j * P:(j + 1) * P],
                                                          xe[:, e, kt, :], start=(kt == 0), stop=(kt == KT - 1))
                            filled(mm, n)
                    for f4 in range(4):
                        wait_stored(pe, J + W3(e, f4), pair)
                    for quarter in range(4):
                        w = wait_expert_chunk(pe, 12 * e + 8 + quarter, pair).rearrange("p (f n) -> p f n", f=FE // P)
                        n = J + Y(e, quarter // 2)
                        if quarter % 2 == 0:
                            wait_bank_free(pe, n, pair)
                        for j in range(2):
                            col = (2 * (quarter % 2) + j) * SLOTS
                            for f in range(FE // P):
                                mm = nc.tensor.matmul(bank(n)[:, col:col + SLOTS], w[:, f, j * P:(j + 1) * P], h[:, e, f, :],
                                                      start=(f == 0), stop=(f == FE // P - 1))
                        if quarter % 2 == 0:
                            mm.then_inc(w2_half_read, 1)
                        else:
                            filled(mm, n)
                for half in range(2):
                    wait_stored(pe, J + Y(0, half), pair)
                    wait_stored(pe, J + Y(1, half), pair)
                for half in range(2):
                    n = J + YT_S(half)
                    wait_bank_free(pe, n, pair)
                    for j in range(4):
                        mm = nc.tensor.transpose(bank(n)[:, j * P:(j + 1) * P], yT_s[:, 4 * half + j, :], ident)
                    filled(mm, n)
                for half in range(2):
                    n = J + YT_P(half)
                    wait_bank_free(pe, n, pair)
                    for j in range(4):
                        mm = nc.tensor.transpose(bank(n)[0:2 * CAP_P, j * P:(j + 1) * P], yT_p[:, 4 * half + j, :], ident)
                    filled(mm, n)
                wait_stored(pe, J + G_S, pair)
                wait_stored(pe, J + G_P, pair)
                for t in range(TILES):
                    for half in range(2):
                        n = J + COMB(t, half)
                        wait_bank_free(pe, n, pair)
                        if t < ST:
                            wait_stored(pe, J + YT_S(half), pair)
                            mm = nc.tensor.matmul(bank(n), gT_s[:, t * P:(t + 1) * P], y_s[:, half * 512:(half + 1) * 512],
                                                  start=True, stop=True)
                        else:
                            wait_stored(pe, J + YT_P(half), pair)
                            mm = nc.tensor.matmul(bank(n), gT_p, y_p[:, half * 512:(half + 1) * 512], start=True, stop=True)
                        filled(mm, n)

        @block.scalar
        def _(act):
            steps = [0]

            def link(ins):
                steps[0] += 1
                ins.then_inc(act_step, 1)
                act.wait_ge(act_step, steps[0])

            wait_stored(act, JOB["vec",])
            nc.scalar.activation(silu_c, vecs[:, V_C:V_C + 16].rearrange("p (w k) -> p k w", w=2), ACT.Silu).then_inc(silu_c_ready, 1)
            for t in range(TILES):
                if t < ST:
                    act.wait_ge(x_pos_ready, t + 1)
                else:
                    act.wait_ge(x_loaded[ST], 16)
                nc.scalar.activation(xn[:, t, :], x[:, t, :], ACT.Square, accum_out=stats[:, t:t + 1]).then_inc(x_squared, 1)
            act.wait_ge(x_recip, 1)
            nc.scalar.activation(stats[:, 10:15], stats[:, 5:10], ACT.Sqrt).then_inc(x_rs, 1)
            n = JOB["wsT",]
            wait_filled(act, n)
            stored(nc.scalar.copy(wsT, bank(n).rearrange("p (g n) -> p g n", g=GROUPS)), n)
            act.wait_ge(mod_ready, 1)
            for kt in range(0, KT, 2):
                n = JOB["xT", kt]
                wait_filled(act, n)
                stored(nc.scalar.activation(hT[:, kt, 0:SAMPLE], bank(n), ACT.Identity, bias=mod[:, SHIFT1 + kt, 0:1],
                                            scale=amp1[:, kt, 0:1]), n)
            n = JOB["xTp", 0]
            wait_filled(act, n)
            for j in range(4):
                ins = nc.scalar.activation(hT[:, j, SAMPLE:TOK], bank(n)[:, j * P:(j + 1) * P], ACT.Identity,
                                           bias=mod[:, SHIFT1 + j, 1:2], scale=amp1[:, j, 1:2])
            stored(ins, n)
            for m in range(5):
                n = JOB["qkS", m] if m < 4 else JOB["qkP",]
                wait_filled(act, n)
                for mm in ([m] if m < 4 else range(4)):
                    dst, scale = (q, DK ** -0.5) if mm < 2 else (k, 1.0)
                    for hh in range(2):
                        for half in range(2):
                            src = bank(n)[hh * DK:(hh + 1) * DK, :] if m < 4 else bank(n)[hh * DK:(hh + 1) * DK, mm * P:(mm + 1) * P]
                            hd = 2 * (mm % 2) + hh
                            lo, hi = (0, SAMPLE) if m < 4 else (SAMPLE, TOK)
                            ins = nc.scalar.activation(dst[half * DK:(half + 1) * DK, hd, lo:hi], src, ACT.Copy, scale=scale)
                stored(ins, n)
            wait_stored(act, JOB["zP",])
            link(nc.scalar.activation(rem, z, ACT.Abs))
            link(nc.scalar.activation(rem, rem, ACT.Exp, scale=-1.0))
            nc.scalar.activation(rem, rem, ACT.Ln, bias=1.0).then_inc(z_ln, 1)

            def store_v(t):
                n = JOB["v", t]
                wait_filled(act, n)
                stored(nc.scalar.copy(v[:, t, :], bank(n)), n)

            for t in range(TILES):
                store_v(t)
            act.wait_ge(cum_ready, 1)
            nc.scalar.activation(z, cum, ACT.Exp, scale=1.0 / GATE_NORM).then_inc(exp_cum, 1)
            act.wait_ge(rem_ready, 1)
            nc.scalar.activation(rem, rem, ACT.Exp, scale=1.0 / GATE_NORM).then_inc(exp_rem, 1)
            act.wait_ge(exp_cum, 1)
            nc.scalar.activation(cum, cum, ACT.Exp, scale=-1.0 / GATE_NORM).then_inc(exp_neg, 1)
            nc.scalar.activation(chunk_decay, stats[:, 40:80].rearrange("p (h n) -> p h n", h=HEADS), ACT.Exp,
                                 scale=1.0 / GATE_NORM).then_inc(decay_ready, 1)
            for t in range(TILES):
                n = JOB["g", t]
                wait_filled(act, n)
                stored(nc.scalar.activation(g[:, t, :], bank(n), ACT.Silu), n)
            for t in range(TILES):
                n = JOB["kd", t]
                wait_filled(act, n)
                stored(nc.scalar.copy(kd[:, t, :, :], bank(n).rearrange("p (h n) -> p h n", h=HEADS)), n)
            act.wait_ge(qe_ready, 1)
            act.wait_ge(ke_ready, 1)
            for ck in range(CHUNKS):
                n = JOB["ds", ck]
                wait_filled(act, n)
                src = bank(n).rearrange("p (h e) -> p h e", h=HEADS)
                if ck < SCH:
                    moves = [(slice(0, DK), ck + 1)] * (ck + 1 < SCH) + [(slice(DK, P), ck - 1)] * (ck > 0)
                    dsts = [(rows, states[rows, to, :, :]) for rows, to in moves]
                elif ck == SCH:
                    dsts = [(slice(0, DK), states[0:DK, SCH + 1, :, :]), (slice(DK, P), fin[DK:P, :, :])]
                else:
                    dsts = [(slice(0, DK), fin[0:DK, :, :]), (slice(DK, P), states[DK:P, SCH, :, :])]
                for rows, dst in dsts:
                    ins = nc.scalar.copy(dst, src[rows])
                stored(ins, n)
            for t in range(TILES):
                n = JOB["u", t]
                wait_filled(act, n)
                stored(nc.scalar.activation(s[:, t, :], bank(n), ACT.Gelu_apprx_tanh), n)
            for t in range(TILES):
                n = JOB["sv", t]
                wait_filled(act, n)
                stored(nc.scalar.activation(s_vn(t), bank(n), ACT.Gelu_apprx_tanh), n)
            for t in range(TILES):
                act.wait_ge(sgu_recip, t + 1)
                nc.scalar.activation(stats[:, 84:88], stats[:, 80:84], ACT.Sqrt).then_inc(sgu_rs, 1)
            for qd in range(4):
                n = JOB["g1", qd]
                wait_filled(act, n)
                stored(nc.scalar.copy(gate1_rows[:, qd // 2, (qd % 2) * 512:(qd % 2) * 512 + 512], bank(n)), n)

            def mix_store(t):
                n = JOB["mT", t, 0]
                wait_filled(act, n)
                if t == 1:
                    act.wait_ge(state_saved, 32)
                if t >= 2:
                    wait_filled(act, JOB["out", t - 2, 1])
                stored(nc.scalar.activation(mixT[:, t % 2, 0:4, :], bank(n).rearrange("p (k n) -> p k n", k=4), ACT.Identity,
                                            bias=0.0, scale=vecs[:, V_GLAW:V_GLAW + 1]), n)
                n = JOB["mT", t, 1]
                wait_filled(act, n)
                stored(nc.scalar.copy(mixT[:, t % 2, 4:8, :], bank(n).rearrange("p (k n) -> p k n", k=4)), n)

            def norm2(t):
                act.wait_ge(x1_ready, t + 1)
                nc.scalar.activation(xn2[:, t, :], x[:, t, :], ACT.Square, accum_out=stats[:, 96:97]).then_inc(x1_squared, 1)
                act.wait_ge(x1_recip, t + 1)
                nc.scalar.activation(stats[:, 98:99], stats[:, 97:98], ACT.Sqrt).then_inc(x1_rs, 1)

            for t in range(TILES + 2):
                if 1 <= t <= TILES:
                    n = JOB["o", t - 1]
                    wait_filled(act, n)
                    if t - 1 >= 2:
                        wait_filled(act, JOB["mT", t - 3, 0])
                    stored(nc.scalar.copy(o_tok[:, (t - 1) % 2, :], bank(n)), n)
                    act.wait_ge(o_recip, t)
                    nc.scalar.activation(stats[:, 108:112], stats[:, 104:108], ACT.Sqrt).then_inc(o_rs, 1)
                if t >= 2:
                    mix_store(t - 2)
                    norm2(t - 2)
            for t in range(TILES):
                n = JOB["hT", t, 0]
                wait_filled(act, n)
                if t >= 2:
                    wait_filled(act, JOB["logit", t - 2])
                stored(nc.scalar.copy(mixT[:, t % 2, 0:4, :], bank(n).rearrange("p (k n) -> p k n", k=4)), n)
                n = JOB["logit", t]
                act.wait_ge(max_ready, t + 1)
                stored(nc.scalar.activation(probs[:, t, 0:EXPERTS], bank(n)[:, 0:EXPERTS], ACT.Exp,
                                            bias=stats[:, 112 + t:113 + t], accum_out=stats[:, 120 + t:121 + t]), n)

            with act.Fori(0, PAIRS) as pair:
                J = JOBS_TRUNK
                n = J + G_S
                wait_filled(act, n, pair)
                stored(nc.scalar.copy(gT_s, bank(n)), n)
                n = J + G_P
                wait_filled(act, n, pair)
                stored(nc.scalar.copy(gT_p, bank(n)[0:2 * CAP_P, 0:P]), n)
                for e in range(2):
                    for f4 in range(4):
                        i = 4 * e + f4
                        n = J + W1(e, f4)
                        wait_filled(act, n, pair)
                        if i >= 2:
                            wait_stored(act, J + W3((i - 2) // 4, (i - 2) % 4), pair)
                        stored(nc.scalar.activation(silu_h[:, i % 2, :], bank(n)[:, 0:4 * SLOTS], ACT.Silu), n)
                for half in range(2):
                    n = J + YT_S(half)
                    wait_filled(act, n, pair)
                    stored(nc.scalar.copy(y_s[:, half * 512:(half + 1) * 512], bank(n)), n)
                for half in range(2):
                    n = J + YT_P(half)
                    wait_filled(act, n, pair)
                    stored(nc.scalar.copy(y_p[:, half * 512:(half + 1) * 512], bank(n)[0:2 * CAP_P, :]), n)
            for t in range(TILES):
                wait_stored(act, JOBS_TRUNK + PAIR_JOBS * (PAIRS - 1) + COMB(t, 1))
                if t >= 2:
                    act.wait_ge(y_saved[t % 2], 16 * (t // 2))
                nc.scalar.activation(y_out[:, t % 2, :], x[:, t, :], ACT.Square, accum_out=stats[:, 130:131]).then_inc(y_squared, 1)
                act.wait_ge(y_recip, t + 1)
                nc.scalar.activation(stats[:, 132:133], stats[:, 131:132], ACT.Sqrt).then_inc(y_rs, 1)

        @block.vector
        def _(dve):
            steps = [0]

            def link(ins):
                steps[0] += 1
                ins.then_inc(vec_step, 1)
                dve.wait_ge(vec_step, steps[0])

            def mean_recip(out, sums, width, then, own=link):
                own(nc.vector.tensor_scalar(out, sums, 1.0 / width, EPS, ALU.mult, ALU.add))
                nc.vector.reciprocal(out, out).then_inc(then, 1)

            n = JOB["vec",]
            wait_filled(dve, n)
            stored(nc.vector.tensor_copy(vecs[:, 0:V_ROWS], bank(n)[:, 0:V_ROWS]), n)
            dve.wait_ge(pos_loaded, 160)
            for t in range(ST):
                dve.wait_ge(x_loaded[t], 16)
                nc.vector.tensor_tensor(x[:, t, 0:512], x[:, t, 0:512], pos_r[:, t, :], ALU.add)
                nc.vector.tensor_tensor(x[:, t, 512:D], x[:, t, 512:D], pos_c, ALU.add).then_inc(x_pos_ready, 1)
            dve.wait_ge(x_pos_ready, ST)
            dve.wait_ge(x_loaded[ST], 16)
            dve.wait_ge(x_squared, TILES)
            mean_recip(stats[:, 5:10], stats[:, 0:5], D, x_recip)
            dve.wait_ge(x_rs, 1)
            for t in range(TILES):
                nc.vector.tensor_scalar(xn[:, t, :], x[:, t, :], stats[:, 10 + t:11 + t], None, ALU.mult).then_inc(xn_ready, 1)

            def store_mod(i, first, count):
                n = JOB["ada", i]
                wait_filled(dve, n)
                stored(nc.vector.tensor_tensor(mod[:, first:first + count, :],
                                               bank(n)[:, 0:2 * count].rearrange("p (k w) -> p k w", w=2),
                                               vecs[:, V_ADAB + first:V_ADAB + first + count, None].to_broadcast([P, count, 2]),
                                               ALU.add), n)
                wait_stored(dve, n)

            store_mod(0, 0, 16)
            nc.vector.scalar_tensor_tensor(amp1, mod[:, SCALE1:SCALE1 + KT, :], 1.0,
                                           vecs[:, V_N1:V_N1 + KT, None].to_broadcast([P, KT, 2]), ALU.add, ALU.mult)\
                .then_inc(mod_ready, 1)
            dve.wait_ge(mod_ready, 1)
            for kt in range(1, KT, 2):
                n = JOB["xT", kt]
                wait_filled(dve, n)
                stored(nc.vector.tensor_scalar(hT[:, kt, 0:SAMPLE], bank(n), amp1[:, kt, 0:1], mod[:, SHIFT1 + kt, 0:1],
                                               ALU.mult, ALU.add), n)
            n = JOB["xTp", 1]
            wait_filled(dve, n)
            for j in range(4):
                ins = nc.vector.tensor_scalar(hT[:, 4 + j, SAMPLE:TOK], bank(n)[:, j * P:(j + 1) * P], amp1[:, 4 + j, 1:2],
                                              mod[:, SHIFT1 + 4 + j, 1:2], ALU.mult, ALU.add)
            stored(ins, n)
            for name, lo, hi in (("aS", 0, SAMPLE), ("aP", SAMPLE, TOK)):
                n = JOB[name,]
                wait_filled(dve, n)
                stored(nc.vector.tensor_copy(aT[:, lo:hi], bank(n)[0:2 * LOWRANK, 0:hi - lo]), n)
            z3 = z.rearrange("p (h n) -> p h n", h=HEADS)
            cum3 = cum.rearrange("p (h n) -> p h n", h=HEADS)
            for hd in range(HEADS):
                n = JOB["zS", hd]
                wait_filled(dve, n)
                stored(nc.vector.tensor_scalar(z3[:, hd, 0:SAMPLE], bank(n), vecs[:, V_BA + hd:V_BA + hd + 1], None, ALU.add), n)
            n = JOB["zP",]
            wait_filled(dve, n)
            for hd in range(HEADS):
                ins = nc.vector.tensor_scalar(z3[:, hd, SAMPLE:TOK], bank(n)[:, hd * P:(hd + 1) * P],
                                              vecs[:, V_BA + hd:V_BA + hd + 1], None, ALU.add)
            stored(ins, n)
            dve.wait_ge(z_ln, 1)
            link(nc.vector.scalar_tensor_tensor(z, z, 0.0, rem, ALU.min, ALU.subtract))
            for hd in range(HEADS):
                ins = nc.vector.tensor_tensor_scan(cum3[:, hd, :], keep, z3[:, hd, :], 0.0, ALU.mult, ALU.add)
            link(ins)
            cum4 = cum.rearrange("p (m n) -> p m n", n=CH)
            z4 = z.rearrange("p (m n) -> p m n", n=CH)
            rem4 = rem.rearrange("p (m n) -> p m n", n=CH)
            total = stats[:, 40:80]
            link(nc.vector.tensor_copy(total, cum4[:, :, CH - 1]))
            tot_b = stats[:, 40:80, None].to_broadcast([P, HEADS * CHUNKS, CH])
            link(nc.vector.tensor_tensor(cum4[DK:P], tot_b[DK:P], cum4[DK:P], ALU.subtract))
            nc.vector.tensor_tensor(cum4[DK:P], cum4[DK:P], z4[DK:P], ALU.add).then_inc(cum_ready, 1)
            dve.wait_ge(cum_ready, 1)
            nc.vector.tensor_tensor(rem4, tot_b, cum4, ALU.subtract).then_inc(rem_ready, 1)
            q2 = q.rearrange("p h n -> p (h n)")
            k2 = k.rearrange("p h n -> p (h n)")
            wait_stored(dve, JOB["qkP",])
            dve.wait_ge(exp_cum, 1)
            nc.vector.tensor_tensor(q2, q2, z, ALU.mult).then_inc(qe_ready, 1)
            dve.wait_ge(exp_rem, 1)
            nc.vector.tensor_tensor(rem, k2, rem, ALU.mult).then_inc(kdT_ready, 1)
            dve.wait_ge(exp_neg, 1)
            dve.wait_ge(kdT_ready, 1)
            nc.vector.tensor_tensor(k2, k2, cum, ALU.mult).then_inc(ke_ready, 1)
            dve.wait_ge(qe_ready, 1)
            dve.wait_ge(ke_ready, 1)
            link(nc.vector.memset(states[0:DK, SCH, :, :], 0.0))
            link(nc.vector.memset(states[DK:P, SCH + 1, :, :], 0.0))
            dve.wait_ge(s0_loaded, 32)
            dve.wait_ge(decay_ready, 1)
            for ck in range(CHUNKS):
                wait_stored(dve, JOB["ds", ck])

            def advance(rows, dst, src, ck):
                for hd in range(HEADS):
                    ins = nc.vector.scalar_tensor_tensor(dst[rows, hd, :], src[rows, hd, :], chunk_decay[rows, hd, ck:ck + 1],
                                                         dst[rows, hd, :], ALU.mult, ALU.add)
                return ins

            lower, upper = slice(0, DK), slice(DK, P)
            for i in range(SCH - 1):
                advance(lower, states[:, i + 1], states[:, i], i)
                link(advance(upper, states[:, SCH - 2 - i], states[:, SCH - 1 - i], SCH - 1 - i))
            advance(lower, fin, states[:, SCH + 1], SCH + 1)
            advance(upper, fin, states[:, SCH], SCH).then_inc(fin_ready, 1)
            for t in range(TILES):
                wait_stored(dve, JOB["sv", t])
                sv = s_vn(t)
                link(nc.vector.tensor_tensor(sgu_sq, sv, sv, ALU.mult))
                link(nc.vector.tensor_reduce(stats[:, 80:84], sgu_sq.rearrange("p (g n) -> p g n", g=GROUPS), AX_X, ALU.add))
                mean_recip(stats[:, 80:84], stats[:, 80:84], P, sgu_recip)
                dve.wait_ge(sgu_rs, t + 1)
                sv3 = sv.rearrange("p (g n) -> p g n", g=GROUPS)
                nc.vector.tensor_tensor(sv3, sv3, stats[:, 84:88, None].to_broadcast([P, GROUPS, P]), ALU.mult)\
                    .then_inc(sgu_vn_ready, 1)
            dve.wait_ge(sguw_loaded, 16)
            for t in range(TILES):
                n = JOB["mix", t]
                wait_filled(dve, n)
                stored(nc.vector.tensor_tensor(sgu_sq, bank(n), sgu_w, ALU.mult), n)
                wait_stored(dve, n)
                for gr in range(GROUPS):
                    cols = slice(gr * P, (gr + 1) * P)
                    ins = nc.vector.scalar_tensor_tensor(s[:, t, cols], sgu_sq[:, cols], vecs[:, V_BS + gr:V_BS + gr + 1],
                                                         s[:, t, cols], ALU.add, ALU.mult)
                ins.then_inc(s_ready, 1)
                dve.wait_ge(s_ready, t + 1)
            store_mod(1, GATE1, 8)
            store_mod(2, SHIFT2, 16)
            link(nc.vector.scalar_tensor_tensor(amp2, mod[:, SCALE2:SCALE2 + KT, :], 1.0,
                                                vecs[:, V_N2:V_N2 + KT, None].to_broadcast([P, KT, 2]), ALU.add, ALU.mult))
            dve.wait_ge(router_loaded, 16)
            for w in range(2):
                ins = nc.vector.tensor_tensor(router_amp[:, w], router, amp2[:, :, w:w + 1].to_broadcast([P, KT, EXPERTS]), ALU.mult)
            ins.then_inc(router_amp_ready, 1)

            def mask(t):
                for d, name, m in ((0, "attF", mask_f), (1, "attB", mask_b)):
                    n = JOB[name, t]
                    wait_filled(dve, n)
                    if t >= 2:
                        wait_filled(dve, JOB["o", t - 2])
                    stored(nc.vector.copy_predicated(att[:, t % 2, d, :, :], m[:, None, :].to_broadcast([P, HEADS, P]),
                                                     bank(n).rearrange("p (h n) -> p h n", h=HEADS)), n)

            def head_norm(t):
                ot = o_tok[:, t % 2, :]
                wait_stored(dve, JOB["o", t])
                link(nc.vector.tensor_tensor(o_sq, ot, ot, ALU.mult))
                link(nc.vector.tensor_reduce(stats[:, 104:108], o_sq.rearrange("p (g n) -> p g n", g=HEADS), AX_X, ALU.add))
                mean_recip(stats[:, 104:108], stats[:, 104:108], DV, o_recip)
                dve.wait_ge(o_rs, t + 1)
                o3 = ot.rearrange("p (g n) -> p g n", g=HEADS)
                link(nc.vector.tensor_tensor(o3, o3, stats[:, 108:112, None].to_broadcast([P, HEADS, P]), ALU.mult))
                nc.vector.tensor_tensor(ot, ot, g[:, t, :], ALU.mult).then_inc(o_ready, 1)

            def residual(t):
                w = 0 if t < ST else 1
                for half in range(2):
                    n = JOB["out", t, half]
                    cols = slice(half * 512, (half + 1) * 512)
                    wait_filled(dve, n)
                    stored(nc.vector.tensor_tensor(out_tmp[:, half, :], bank(n), gate1_rows[:, w, cols], ALU.mult), n)
                    wait_stored(dve, n)
                    ins = nc.vector.tensor_tensor(x[:, t, cols], x[:, t, cols], out_tmp[:, half, :], ALU.add)
                    if half == 1:
                        ins.then_inc(x1_ready, 1)
                dve.wait_ge(x1_squared, t + 1)
                mean_recip(stats[:, 97:98], stats[:, 96:97], D, x1_recip)
                dve.wait_ge(x1_rs, t + 1)
                nc.vector.tensor_scalar(xn2[:, t, :], x[:, t, :], stats[:, 98:99], None, ALU.mult).then_inc(xn2_ready, 1)

            dve.wait_ge(pool_zeroed, 3)
            for qd in range(4):
                wait_stored(dve, JOB["g1", qd])
            for t in range(TILES + 2):
                if t < TILES:
                    mask(t)
                if 1 <= t <= TILES:
                    head_norm(t - 1)
                if t >= 2:
                    residual(t - 2)
            for t in range(TILES):
                n = JOB["hT", t, 1]
                wait_filled(dve, n)
                if t >= 2:
                    wait_filled(dve, JOB["logit", t - 2])
                stored(nc.vector.tensor_copy(mixT[:, t % 2, 4:8, :], bank(n).rearrange("p (k n) -> p k n", k=4)), n)
                n = JOB["logit", t]
                wait_filled(dve, n)
                nc.vector.tensor_reduce(stats[:, 112 + t:113 + t], bank(n)[:, 0:EXPERTS], AX_X, ALU.max, negate=True)\
                    .then_inc(max_ready, 1)
                wait_stored(dve, n)
                link(nc.vector.reciprocal(stats[:, 125:126], stats[:, 120 + t:121 + t]))
                nc.vector.tensor_scalar(probs[:, t, 0:EXPERTS], probs[:, t, 0:EXPERTS], stats[:, 125:126], None, ALU.mult)\
                    .then_inc(probs_ready, 1)
                dve.wait_ge(probs_ready, t + 1)
            for name, lo, hi, rounds in (("pS", 0, SAMPLE, CAP_S // 8), ("pP", SAMPLE, TOK, CAP_P // 8)):
                n = JOB[name,]
                wait_filled(dve, n)
                work = top_work[:, lo:hi]
                stored(nc.vector.tensor_copy(work, bank(n)[0:EXPERTS, 0:hi - lo]), n)
                wait_stored(dve, n)
                for _ in range(rounds):
                    link(nc.vector.max(top8, work))
                    link(nc.vector.match_replace(out=work, in_to_replace=top8, in_values=work, imm_value=-1.0))
                link(nc.vector.tensor_scalar(top_mask[:, lo:hi], work, 0.0, None, ALU.is_lt))
            store_mod(3, GATE2, 8)
            link(nc.vector.memset(top_work, 1.0))
            link(nc.vector.tensor_tensor_scan(top_rank[:, 0:SAMPLE], top_work[:, 0:SAMPLE], top_mask[:, 0:SAMPLE], 0.0, ALU.mult, ALU.add))
            link(nc.vector.tensor_tensor_scan(top_rank[:, SAMPLE:TOK], top_work[:, SAMPLE:TOK], top_mask[:, SAMPLE:TOK], 0.0, ALU.mult, ALU.add))
            nc.vector.tensor_tensor(top_rank, top_rank, top_mask, ALU.mult).then_inc(rank_rows_ready, 1)
            n = JOB["rank",]
            wait_filled(dve, n)
            stored(nc.vector.tensor_scalar(rank[:, :, 0:EXPERTS], bank(n)[:, 0:TILES * EXPERTS].rearrange("p (t e) -> p t e", t=TILES),
                                           -1.0, None, ALU.add), n)
            wait_stored(dve, n)

            def one_hots(first, own):
                own(nc.vector.tensor_copy(comb_rk, rank[:, :, bass.ds(first, 2)]))
                own(nc.vector.tensor_copy(comb_pr, probs[:, :, bass.ds(first, 2)]))
                hs = hot_s.rearrange("p t e n -> p (t e) n")
                gs = gate_s.rearrange("p t e n -> p (t e) n")
                rk = comb_rk.rearrange("p t e -> p (t e)")
                pr = comb_pr.rearrange("p t e -> p (t e)")
                nc.vector.tensor_tensor(hs, iota[:, None, :].to_broadcast([P, 2 * ST, CAP_S]),
                                        rk[:, 0:2 * ST, None].to_broadcast([P, 2 * ST, CAP_S]), ALU.is_equal).then_inc(hot_ready, 1)
                nc.vector.tensor_tensor(hot_p, iota[:, None, 0:CAP_P].to_broadcast([P, 2, CAP_P]),
                                        rk[:, 2 * ST:2 * TILES, None].to_broadcast([P, 2, CAP_P]), ALU.is_equal).then_inc(hot_ready, 1)
                return hs, gs, pr

            def gates(hs, gs, pr):
                nc.vector.tensor_tensor(gs, hs, pr[:, 0:2 * ST, None].to_broadcast([P, 2 * ST, CAP_S]), ALU.mult).then_inc(hot_ready, 1)
                nc.vector.tensor_tensor(gate_p, hot_p, pr[:, 2 * ST:2 * TILES, None].to_broadcast([P, 2, CAP_P]), ALU.mult)\
                    .then_inc(hot_ready, 1)

            parts = one_hots(0, link)
            dve.wait_ge(hot_ready, 2)
            gates(*parts)

            with dve.Fori(0, PAIRS) as pair:
                J = JOBS_TRUNK
                pair_steps = [0]
                PER_PAIR = 6

                def link_pair(ins):
                    pair_steps[0] += 1
                    ins.then_inc(vec_pair_step, 1)
                    dve.wait_ge(vec_pair_step, pair_steps[0] + pair * PER_PAIR)

                for e in range(2):
                    for n, w, lo, cap in ((J + X_S(e), 0, 0, CAP_S), (J + X_P(e), 1, CAP_S, CAP_P)):
                        wait_filled(dve, n, pair)
                        dst = xe[:, e, :, lo:lo + cap]
                        link_pair(nc.vector.tensor_tensor(dst, bank(n)[:, 0:KT * cap].rearrange("p (k n) -> p k n", k=KT),
                                                          amp2[:, :, w:w + 1].to_broadcast([P, KT, cap]), ALU.mult))
                        stored(nc.vector.tensor_tensor(dst, dst, mod[:, SHIFT2:SHIFT2 + KT, w:w + 1].to_broadcast([P, KT, cap]),
                                                       ALU.add), n)
                for e in range(2):
                    for f4 in range(4):
                        n = J + W3(e, f4)
                        wait_stored(dve, J + W1(e, f4), pair)
                        wait_filled(dve, n, pair)
                        stored(nc.vector.tensor_tensor(h[:, e, 4 * f4:4 * f4 + 4, :],
                                                       silu_h[:, (4 * e + f4) % 2, :].rearrange("p (f n) -> p f n", f=4),
                                                       bank(n)[:, 0:4 * SLOTS].rearrange("p (f n) -> p f n", f=4), ALU.mult), n)
                    for half in range(2):
                        n = J + Y(e, half)
                        wait_filled(dve, n, pair)
                        src = bank(n)[:, 0:4 * SLOTS].rearrange("p (k n) -> p k n", k=4)
                        ks = slice(4 * half, 4 * half + 4)
                        gk = slice(GATE2 + 4 * half, GATE2 + 4 * half + 4)
                        nc.vector.tensor_tensor(yT_s[:, ks, e * CAP_S:(e + 1) * CAP_S], src[:, :, 0:CAP_S],
                                                mod[:, gk, 0:1].to_broadcast([P, 4, CAP_S]), ALU.mult)
                        stored(nc.vector.tensor_tensor(yT_p[:, ks, e * CAP_P:(e + 1) * CAP_P], src[:, :, CAP_S:SLOTS],
                                                       mod[:, gk, 1:2].to_broadcast([P, 4, CAP_P]), ALU.mult), n)
                wait_filled(dve, J + G_P, pair)
                parts = one_hots(2 * pair + 2, link_pair)
                dve.wait_ge(hot_ready, 6 + pair * 4)
                gates(*parts)
                for t in range(TILES):
                    for half in range(2):
                        n = J + COMB(t, half)
                        cols = slice(half * 512, (half + 1) * 512)
                        wait_filled(dve, n, pair)
                        stored(nc.vector.tensor_tensor(x[:, t, cols], x[:, t, cols], bank(n), ALU.add), n)
                assert pair_steps[0] == PER_PAIR
            dve.wait_ge(final_loaded, 16)
            final_steps = [0]

            def link_final(ins):
                final_steps[0] += 1
                ins.then_inc(vec_final_step, 1)
                dve.wait_ge(vec_final_step, final_steps[0])

            for t in range(TILES):
                dve.wait_ge(y_squared, t + 1)
                mean_recip(stats[:, 131:132], stats[:, 130:131], D, y_recip, link_final)
                dve.wait_ge(y_rs, t + 1)
                nc.vector.scalar_tensor_tensor(y_out[:, t % 2, :], x[:, t, :], stats[:, 132:133], final_w, ALU.mult, ALU.mult)\
                    .then_inc(y_ready, 1)


_INS = ["x_prompt", "x_sample", "state_gla_fwd", "state_gla_bwd", "c", "c_ctx", "ada_w", "ada_b", "norm1_w", "w_in",
        "gla_wa2_f", "gla_ba_f", "gla_wa2_b", "gla_ba_b", "gla_norm_w", "sgu_norm_w", "sgu_ws", "sgu_bs", "w_out",
        "norm2_w", "router_w", "exp_w1", "exp_w3", "exp_w2", "final_norm_w"]
_OUTS = [(1, PROMPT, D), (1, SAMPLE, D), (1, 1, HEADS, DK, DV), (1, 1, HEADS, DK, DV)]


def kernel(**inputs):
    import numpy as _np
    import concourse.bacc as _bacc
    from concourse import mybir as _mybir
    from concourse.bass_utils import run_bass_kernel_spmd as _run

    nc = _bacc.Bacc("TRN2", target_bir_lowering=False, num_devices=1)
    arrays, args = {}, []
    named = [(name, _np.ascontiguousarray(inputs[name])) for name in _INS]
    named += list(zip(("table", "pos_row", "pos_col"), shape_constants()))
    for name, a in named:
        arrays[f"in_{name}_dram"] = a
        args.append(nc.dram_tensor(f"in_{name}_dram", a.shape, _mybir.dt.from_np(a.dtype), kind="ExternalInput").ap())
    for i, shape in enumerate(_OUTS):
        args.append(nc.dram_tensor(f"out_{i}_dram", shape, F32, kind="ExternalOutput").ap())
    trunk_kernel(nc, *args)
    r = _run(nc, [arrays], core_ids=[0])
    return tuple(r.results[0][f"out_{i}_dram"] for i in range(len(_OUTS)))
```

```python
from contextlib import ExitStack

import numpy as np

import concourse.bass as bass
from concourse import mybir

ALU = mybir.AluOpType
ACT = mybir.ActivationFunctionType
F32 = mybir.dt.float32
I32 = mybir.dt.int32
AX_X = mybir.AxisListType.X

P = 128
D = 1024
KT = D // P
SAMPLE, PROMPT = 512, 128
TILES = (SAMPLE + PROMPT) // P
ST = SAMPLE // P
TOK = SAMPLE + PROMPT
HEADS, DK, DV = 4, 64, 128
CH = 64
CHUNKS = TOK // CH
SCH = SAMPLE // CH
LOWRANK = 16
GATE_NORM = 16.0
GROUPS = 4
EXPERTS = 16
FE = 2048
CAP_S, CAP_P = 2 * SAMPLE // EXPERTS, 2 * PROMPT // EXPERTS
SLOTS = CAP_S + CAP_P
GRID_W = 64
EPS = 1e-6
PAIRS = EXPERTS // 2

COL_QK, COL_V, COL_G, COL_A, COL_U, COL_SV = 0, 512, 1024, 1536, 1568, 2080

BANKS = 8
CHUNK_F = 4096
RING = 6
TRUNK_RING = 3

V_ADAB, V_C, V_CCTX, V_N1, V_N2, V_BS, V_BA, V_GLAW, V_ROWS = 0, 48, 56, 64, 72, 80, 84, 88, 89
SHIFT1, SCALE1, GATE1, SHIFT2, SCALE2, GATE2 = 0, 8, 16, 24, 32, 40


def shape_constants():
    j = np.arange(P)[:, None]
    i = np.arange(P)[None, :]
    same = (j // CH) == (i // CH)
    ident = np.eye(P, dtype=np.float32)
    fwd = (same & (j <= i)).astype(np.float32)
    bwd = (same & (j >= i)).astype(np.float32)
    keep = np.broadcast_to((np.arange(TOK) % CH != 0).astype(np.float32), (P, TOK))
    iota = np.broadcast_to(np.arange(CAP_S, dtype=np.float32), (P, CAP_S))
    table = np.concatenate([ident, fwd, bwd, keep, iota], axis=1).astype(np.float32)
    nf = D // 4
    omega = (1.0 / (np.float32(10000.0) ** (np.arange(nf, dtype=np.float32) / np.float32(nf)))).astype(np.float32)

    def emb(n):
        a = np.arange(n, dtype=np.float32)[:, None] * omega[None, :]
        return np.concatenate([np.sin(a), np.cos(a)], axis=-1).astype(np.float32)

    return table, emb(SAMPLE // GRID_W), emb(GRID_W)


GATHER_JOBS = [("XG_S", 0), ("XG_S", 1), ("XG_P", 0), ("XG_P", 1), ("XT_S", 0), ("XT_S", 1), ("XT_P",)]


def job_numbers():
    names = [("vec",), ("wsT",)]
    for c in range(5):
        names += [("adaR", c)] * (c < 4) + [("adaT", c - 1)] * (c > 0)
    names += [("xT", k) for k in range(KT)] + [("xTp", h) for h in range(2)]
    names += [("qkP",)] + [("qkS", m) for m in range(4)]
    names += [("adaR", 4), ("adaR", 5)]
    names += [("aS",), ("aP",)] + [("zS", h) for h in range(HEADS)] + [("zP",)]
    names += [("v", t) for t in range(TILES)]
    names += [("adaT", 4), ("adaT", 5), ("adaR", 6), ("adaR", 7)]
    names += [("g", t) for t in range(TILES)]
    names += [("adaT", 6), ("adaT", 7), ("adaR", 8), ("adaR", 9)]
    names += [("kd", t) for t in range(TILES)] + [("ds", n) for n in range(CHUNKS)]
    names += [("u", t) for t in range(TILES)]
    names += [("adaT", 8), ("adaT", 9), ("adaR", 10)]
    names += [("sv", t) for t in range(TILES)]
    names += [("adaT", 10), ("adaR", 11)]
    names += [("mix", t) for t in range(TILES)]
    names += [("adaT", 11)] + [("g1", q) for q in range(4)]
    for t in range(TILES + 3):
        if t < TILES:
            names += [("attF", t), ("attB", t)]
        if 1 <= t <= TILES:
            names += [("o", t - 1)]
        if 2 <= t < TILES + 2:
            names += [("mT", t - 2, 0), ("mT", t - 2, 1), ("out", t - 2, 0), ("out", t - 2, 1)]
        if t >= 3:
            names += [("hT", t - 3, 0), ("hT", t - 3, 1), ("logit", t - 3)]
    names += [("g2", q) for q in range(4)] + [("pS",), ("pP",), ("rank",)]
    names += GATHER_JOBS
    return {name: n for n, name in enumerate(names)}


JOB = job_numbers()
JOBS_TRUNK = len(JOB)

PAIR_JOBS = 40
R1 = lambda e, r: (0, 12)[e] + ((0, 2, 6), (0, 2, 5))[e][r]
R3 = lambda e, r: R1(e, r) + 1
T = lambda e, r: ((4, 8, 11), (16, 19, 22))[e][r]
G_S = 5
Y = lambda e, i: (9, 20)[e] + i
NEXT_GATHER = dict(zip(GATHER_JOBS, (23, 24, 25, 26, 33, 34, 35)))
COMB_ORDER = [ST] + list(range(ST))
COMB_AHEAD = 3


def COMB(t, half, last):
    i = 2 * COMB_ORDER.index(t) + half
    return (23 if last else 27 if i < 2 * COMB_AHEAD else 30) + i


PART = 32
PADDED = 3 * PART
ROUNDS = [[(0, 0), (0, 1), (0, 2), (1, 2)], [(1, 0), (1, 1), (2, 0), (2, 1)], [(3, 0), (3, 1), (3, 2), (2, 2)]]
EXPERT_CHUNKS = [(0, 0), (0, 1), (1, 0), (1, 1), (0, 2), (1, 2), (0, 3), (1, 3)]
LAST_ROUND = [0, 1, 2, 2]

ADA = [("ada", 512 * c) for c in range(12)]
TRUNK_CHUNKS = (ADA[0:4] + [("in", COL_QK)] + ADA[4:6] + [("in", COL_V)] + ADA[6:8] + [("in", COL_G)] + ADA[8:10]
                + [("in", COL_U)] + ADA[10:11] + [("in", COL_SV)] + ADA[11:12] + [("out", 0), ("out", 512)])
CHUNK_OF = {c: n for n, c in enumerate(TRUNK_CHUNKS)}
EXPERT_SLOT = [3, 4, 5, 1, 2, 0]
LOADS_BEFORE = [len([n for n in range(len(TRUNK_CHUNKS)) if n % TRUNK_RING == s]) if s < TRUNK_RING else 0
                for s in range(RING)]
PAIR_CHUNKS = 24

def trunk_kernel(nc, x_prompt, x_sample, s0_f, s0_b, c, c_ctx, ada_w, ada_b, norm1_w, w_in, wa2_f, ba_f,
                 wa2_b, ba_b, gla_norm_w, sgu_norm_w, sgu_ws, sgu_bs, w_out, norm2_w, router_w, w1, w3, w2,
                 final_norm_w, table, pos_row, pos_col, y_prompt, y_sample, new_f, new_b):
    with ExitStack() as ctx:
        def sb(name, cols):
            return ctx.enter_context(nc.sbuf_tensor(name, [P, cols], F32))

        def sem(name):
            return ctx.enter_context(nc.semaphore(name))

        ring = sb("ring", RING * CHUNK_F)
        consts = sb("consts", 3 * P + TOK + CAP_S)
        ident = consts[:, 0:P]
        mask_f = consts[:, P:2 * P].bitcast(I32)
        mask_b = consts[:, 2 * P:3 * P].bitcast(I32)
        keep = consts[:, 3 * P:3 * P + TOK]
        iota = consts[:, 3 * P + TOK:3 * P + TOK + CAP_S]
        vecs = sb("vecs", 96)
        silu_c = sb("silu_c", PART * KT)[:].rearrange("p (k w) -> p k w", w=PART)
        mod = sb("mod", 96)[:].rearrange("p (k w) -> p k w", w=2)
        amp1 = sb("amp1", 2 * KT)[:].rearrange("p (k w) -> p k w", w=2)
        amp2 = sb("amp2", 2 * KT)[:].rearrange("p (k w) -> p k w", w=2)
        router = sb("router", KT * EXPERTS)[:].rearrange("p (k e) -> p k e", e=EXPERTS)
        router_amp = sb("router_amp", 2 * KT * EXPERTS)[:].rearrange("p (w k e) -> p w k e", w=2, e=EXPERTS)
        x = sb("x", TILES * D)[:].rearrange("p (t d) -> p t d", t=TILES)
        feat = sb("feat", TILES * D)
        hT = feat[:].rearrange("p (k n) -> p k n", k=KT)
        xn2 = feat[:].rearrange("p (t d) -> p t d", t=TILES)
        probs = sb("probs", TILES * EXPERTS)[:].rearrange("p (t e) -> p t e", t=TILES)
        rank = sb("rank", TILES * EXPERTS)[:].rearrange("p (t e) -> p t e", t=TILES)
        stats = sb("stats", 160)
        logits = sb("logits", TILES * EXPERTS)[:].rearrange("p (t e) -> p t e", t=TILES)
        chunk_decay = sb("chunk_decay", HEADS * CHUNKS)[:].rearrange("p (h n) -> p h n", h=HEADS)

        up = TRUNK_RING * CHUNK_F
        q = ring[:, up:up + 2560].rearrange("p (h n) -> p h n", h=HEADS)
        k = ring[:, up + 2560:up + 5120].rearrange("p (h n) -> p h n", h=HEADS)
        v = ring[:, up + 5120:up + 7680].rearrange("p (t n) -> p t n", t=TILES)
        g = ring[:, up + 7680:up + 10240].rearrange("p (t n) -> p t n", t=TILES)
        att = ring[:, up + 10240:up + 12288].rearrange("p (b d h n) -> p b d h n", b=2, d=2, h=HEADS)
        pos_r = ring[:, up:up + 2048].rearrange("p (t n) -> p t n", t=ST)
        pos_c = ring[:, up + 2048:up + 2560]

        both = sb("both", 15872)
        z = both[:, 0:2560]
        cum = both[:, 2560:5120]
        rem = both[:, 5120:7680]
        states = both[:, 0:5120].rearrange("p (n h e) -> p n h e", n=CHUNKS, h=HEADS)
        xn = both[:, 0:5120].rearrange("p (t d) -> p t d", t=TILES)
        gate1_rows = both[:, 5120:7168].rearrange("p (w d) -> p w d", w=2)
        kd = both[:, 7680:10240].rearrange("p (t h d) -> p t h d", t=TILES, h=HEADS)
        a_up = both[0:2 * LOWRANK, 7680:8192].rearrange("p (h n) -> p h n", h=HEADS)
        aT = both[0:2 * LOWRANK, 8192:8832]
        w_a = both[:, 8832:9088].rearrange("p (k n) -> p k n", k=KT)
        vec_rows = both[:, 9088:9216]
        ws = both[:, 9216:9728].rearrange("p (g n) -> p g n", g=GROUPS)
        o_tok = both[:, 7680:8704].rearrange("p (b n) -> p b n", b=2)
        o_sq = both[:, 8704:9216]
        out_tmp = both[:, 9216:10240].rearrange("p (b n) -> p b n", b=2)
        s = both[:, 10240:12800].rearrange("p (t n) -> p t n", t=TILES)
        mixT = both[:, 12800:14848].rearrange("p (b k n) -> p b k n", b=2, k=KT)
        sgu_sq = both[:, 13824:14336]
        fin = both[:, 14336:14848].rearrange("p (h e) -> p h e", h=HEADS)
        ada_rows = both[:, 12800:13824].rearrange("p (b n) -> p b n", b=2)
        h2T = both[:, 14848:15872].rearrange("p (k n) -> p k n", k=KT)
        wsT = both[:, 14848:15360].rearrange("p (g n) -> p g n", g=GROUPS)
        sgu_w = both[:, 15360:15872]
        top_work = both[0:EXPERTS, 10240:10880]
        top_mask = both[0:EXPERTS, 10880:11520]
        top_rank = both[0:EXPERTS, 11520:12160]
        top8 = both[0:EXPERTS, 12160:12168]

        xe = both[:, 0:1536].rearrange("p (e k n) -> p e k n", e=2, k=KT)
        xg_s = both[:, 1536:2560]
        xg_p = both[0:2 * CAP_P, 2560:3584]
        h_rows = both[:, 3584:5120].rearrange("p (r n) -> p r n", r=3)
        h = both[:, 5120:6656].rearrange("p (f n) -> p f n", f=FE // P)
        silu_h = both[:, 6656:7680].rearrange("p (b n) -> p b n", b=2)
        hot_s = both[:, 7680:8192].rearrange("p (t e n) -> p t e n", t=ST, e=2)
        hot_p = both[:, 8192:8224].rearrange("p (e n) -> p e n", e=2)
        gate_s = both[:, 8224:8736].rearrange("p (t e n) -> p t e n", t=ST, e=2)
        gate_p = both[:, 8736:8800].rearrange("p (e n) -> p e n", e=2)
        gT_s = both[:, 8800:9312]
        gT_p = both[0:2 * PART, 9312:9440]
        comb_rk = both[:, 9440:9450].rearrange("p (t e) -> p t e", e=2)
        comb_pr = both[:, 9450:9460].rearrange("p (t e) -> p t e", e=2)
        gate2_0 = both[:, 12800:13312]
        gate2_1 = both[:, 13312:13824]
        y_s = both[:, 13824:14848]
        y_p = both[0:2 * PART, 14848:15872]
        y_half = both[:, 9460:9972]
        final_w = both[:, 0:1024]
        y_out = both[:, 3584:5632].rearrange("p (b d) -> p b d", b=2)

        def s_vn(t):
            return both[:, 7680 + 512 * t:8192 + 512 * t]

        psum = ctx.enter_context(nc.psum_tensor("psum", [P, BANKS, 512], F32))

        psum_filled = [sem(f"psum_filled{b}") for b in range(BANKS)]
        psum_stored = [sem(f"psum_stored{b}") for b in range(BANKS)]
        slot_loaded = [sem(f"slot_loaded{s}") for s in range(RING)]
        w2_read = sem("w2_read")
        silu_c_zeroed = sem("silu_c_zeroed")
        xe_zeroed = sem("xe_zeroed")
        mod_summed = sem("mod_summed")
        y_added = sem("y_added")
        ident_loaded = sem("ident_loaded")
        consts_loaded = sem("consts_loaded")
        vecs_loaded = sem("vecs_loaded")
        ws_loaded = sem("ws_loaded")
        x_loaded = [sem(f"x_loaded{t}") for t in range(TILES)]
        pos_loaded = sem("pos_loaded")
        wa_zeroed = sem("wa_zeroed")
        wa_loaded = sem("wa_loaded")
        router_loaded = sem("router_loaded")
        sguw_loaded = sem("sguw_loaded")
        s0_loaded = sem("s0_loaded")
        final_loaded = sem("final_loaded")
        pool_zeroed = sem("pool_zeroed")
        vec_step = sem("vec_step")
        act_step = sem("act_step")
        vec_pair_step = sem("vec_pair_step")
        vec_final_step = sem("vec_final_step")
        silu_c_ready = sem("silu_c_ready")
        x_pos_ready = sem("x_pos_ready")
        x_squared = sem("x_squared")
        x_recip = sem("x_recip")
        x_rs = sem("x_rs")
        xn_ready = sem("xn_ready")
        mod_ready = sem("mod_ready")
        z_ln = sem("z_ln")
        cum_ready = sem("cum_ready")
        rem_ready = sem("rem_ready")
        exp_cum = sem("exp_cum")
        exp_neg = sem("exp_neg")
        exp_rem = sem("exp_rem")
        decay_ready = sem("decay_ready")
        qe_ready = sem("qe_ready")
        kdT_ready = sem("kdT_ready")
        ke_ready = sem("ke_ready")
        ds_stored = sem("ds_stored")
        fin_ready = sem("fin_ready")
        sgu_recip = sem("sgu_recip")
        sgu_rs = sem("sgu_rs")
        sgu_vn_ready = sem("sgu_vn_ready")
        s_ready = sem("s_ready")
        o_recip = sem("o_recip")
        o_rs = sem("o_rs")
        o_ready = sem("o_ready")
        x1_ready = sem("x1_ready")
        x1_squared = sem("x1_squared")
        x1_recip = sem("x1_recip")
        x1_rs = sem("x1_rs")
        xn2_ready = sem("xn2_ready")
        router_amp_ready = sem("router_amp_ready")
        max_ready = sem("max_ready")
        exp_ready = sem("exp_ready")
        probs_ready = sem("probs_ready")
        rank_rows_ready = sem("rank_rows_ready")
        hot_ready = sem("hot_ready")
        y_squared = sem("y_squared")
        y_recip = sem("y_recip")
        y_rs = sem("y_rs")
        y_ready = sem("y_ready")
        y_saved = [sem(f"y_saved{b}") for b in range(2)]
        state_saved = sem("state_saved")

        def bank(n):
            return psum[:, n % BANKS, :]

        def wait_filled(eng, n, pair=None):
            eng.wait_ge(psum_filled[n % BANKS], n // BANKS + 1 + (0 if pair is None else pair * (PAIR_JOBS // BANKS)))

        def wait_stored(eng, n, pair=None):
            eng.wait_ge(psum_stored[n % BANKS], n // BANKS + 1 + (0 if pair is None else pair * (PAIR_JOBS // BANKS)))

        def wait_bank_free(pe, n, pair=None):
            if n >= BANKS:
                wait_stored(pe, n - BANKS, pair)

        def filled(ins, n):
            ins.then_inc(psum_filled[n % BANKS], 1)

        def stored(ins, n):
            ins.then_inc(psum_stored[n % BANKS], 1)

        def first_gather(*name):
            return JOB[name]

        def next_gather(*name):
            return JOBS_TRUNK + NEXT_GATHER[name]

        def chunk(slot):
            return ring[:, slot * CHUNK_F:(slot + 1) * CHUNK_F]

        def wait_trunk_chunk(pe, n):
            pe.wait_ge(slot_loaded[n % TRUNK_RING], 16 * (n // TRUNK_RING + 1))
            return chunk(n % TRUNK_RING).rearrange("p (k n) -> p k n", k=KT)

        def wait_expert_chunk(pe, m, pair):
            slot = EXPERT_SLOT[m % RING]
            pe.wait_ge(slot_loaded[slot], 16 * (LOADS_BEFORE[slot] + m // RING + 1) + pair * (16 * PAIR_CHUNKS // RING))
            return chunk(slot)

        def wait_trunk_chunk_read(sp, n):
            name, col = TRUNK_CHUNKS[n]
            if name == "ada":
                wait_filled(sp, JOB["adaR", col // 512])
            elif name == "in":
                last = {COL_QK: ("qkP",), COL_V: ("v", TILES - 1), COL_G: ("g", TILES - 1),
                        COL_U: ("u", TILES - 1), COL_SV: ("sv", TILES - 1)}[col]
                wait_filled(sp, JOB[last])
            else:
                wait_filled(sp, JOB["out", TILES - 1, col // 512])

        def wait_expert_chunk_read(sp, m, pair):
            back, m = (1, m + PAIR_CHUNKS) if m < 0 else (0, m)
            e, i = divmod(m, 12)
            when = pair - back
            if i < 8:
                which, f4 = EXPERT_CHUNKS[i]
                wait_filled(sp, JOBS_TRUNK + (R1, R3)[which](e, LAST_ROUND[f4]), when)
            elif i < 11:
                sp.wait_ge(w2_read, 3 * e + i - 7 + when * 6)
            else:
                wait_filled(sp, JOBS_TRUNK + Y(e, 1), when)

        sample_x = x_sample.rearrange("b (t p) d -> p (b t) d", p=P)
        prompt_x = x_prompt.rearrange("b p d -> p (b d)")
        ada_k = ada_w[0].rearrange("(k p) n -> p k n", p=P)
        in_k = w_in[0].rearrange("(k p) n -> p k n", p=P)
        out_k = w_out[0].rearrange("(k p) n -> p k n", p=P)

        block = ctx.enter_context(nc.Block())

        @block.sync
        def _(sp):
            sp.dma_start(ident, table[:, 0:P]).then_inc(ident_loaded, 16)
            for t in range(ST):
                sp.dma_start(x[:, t, :], sample_x[:, t, :]).then_inc(x_loaded[t], 16)
            sp.dma_start(x[:, ST, :], prompt_x).then_inc(x_loaded[ST], 16)
            sp.dma_start(consts[:, P:], table[:, P:]).then_inc(consts_loaded, 16)
            for n, (name, col) in enumerate(TRUNK_CHUNKS):
                if n >= TRUNK_RING:
                    wait_trunk_chunk_read(sp, n - TRUNK_RING)
                src = {"ada": ada_k, "in": in_k, "out": out_k}[name][:, :, col:col + 512]
                sp.dma_start(chunk(n % TRUNK_RING).rearrange("p (k n) -> p k n", k=KT), src)\
                    .then_inc(slot_loaded[n % TRUNK_RING], 16)
                if n == 13:
                    sp.wait_ge(qe_ready, 1)
                    sp.wait_ge(ke_ready, 1)
                    sp.dma_start(states[0:DK, 0, :, :], s0_f[0, 0].rearrange("h d e -> d h e"))\
                        .then_inc(s0_loaded, 16)
                    sp.dma_start(states[DK:P, SCH - 1, :, :], s0_b[0, 0].rearrange("h d e -> d h e"))\
                        .then_inc(s0_loaded, 16)
                if n == 16:
                    sp.wait_ge(fin_ready, 1)
                    sp.dma_start(new_f[0, 0].rearrange("h d e -> d h e"), fin[0:DK, :, :]).then_inc(state_saved, 16)
                    sp.dma_start(new_b[0, 0].rearrange("h d e -> d h e"), fin[DK:P, :, :]).then_inc(state_saved, 16)

            def load_expert_chunk(m, pair):
                e, i = divmod(m, 12)
                slot = EXPERT_SLOT[m % RING]
                expert = 2 * pair + e
                if i < 8:
                    which, f4 = EXPERT_CHUNKS[i]
                    src = (w1, w3)[which][0, bass.ds(expert, 1)].rearrange("a (k p) n -> p (a k) n", p=P)[:, :, f4 * 512:f4 * 512 + 512]
                    dst = chunk(slot).rearrange("p (k n) -> p k n", k=KT)
                else:
                    src = w2[0, bass.ds(expert, 1)].rearrange("a (k p) n -> p (a k) n", p=P)[:, (i - 8) * 4:(i - 8) * 4 + 4, :]
                    dst = chunk(slot).rearrange("p (k n) -> p k n", k=4)
                sp.dma_start(dst, src).then_inc(slot_loaded[slot], 16)

            wait_filled(sp, JOB["mT", TILES - 1, 1])
            sp.wait_ge(o_ready, TILES)
            for m in range(RING):
                if m >= 3:
                    wait_trunk_chunk_read(sp, {3: 16, 4: 17, 5: 18}[m])
                load_expert_chunk(m, 0)
            for m in range(RING, PAIR_CHUNKS):
                wait_expert_chunk_read(sp, m - RING, 0)
                load_expert_chunk(m, 0)
            with sp.Fori(1, PAIRS) as pair:
                for m in range(PAIR_CHUNKS):
                    wait_expert_chunk_read(sp, m - RING, pair)
                    load_expert_chunk(m, pair)

            for t in range(TILES):
                sp.wait_ge(y_ready, t + 1)
                dst = (y_sample.rearrange("b (t p) d -> p (b t) d", p=P)[:, t, :] if t < ST
                       else y_prompt.rearrange("b p d -> p (b d)"))
                sp.dma_start(dst, y_out[:, t % 2, :]).then_inc(y_saved[t % 2], 16)
            sp.wait_ge(y_saved[0], 16 * 3)
            sp.wait_ge(y_saved[1], 16 * 2)
            sp.wait_ge(state_saved, 32)

        @block.gpsimd
        def _(pool):
            nc.gpsimd.memset(silu_c, 0.0).then_inc(silu_c_zeroed, 1)
            for t in range(ST):
                for half in range(2):
                    pool.dma_start(pos_r[64 * half:64 * half + 64, t, :],
                                   pos_row[2 * t + half:2 * t + half + 1, :].to_broadcast([64, 512])).then_inc(pos_loaded, 16)
            for half in range(2):
                pool.dma_start(pos_c[64 * half:64 * half + 64, :], pos_col).then_inc(pos_loaded, 16)
            nc.gpsimd.memset(a_up, 0.0).then_inc(wa_zeroed, 1)
            nc.gpsimd.memset(att, 0.0).then_inc(pool_zeroed, 1)
            pool.wait_ge(wa_zeroed, 1)
            pool.dma_start(a_up[0:LOWRANK, :, 0:DK], wa2_f[0].rearrange("r (h n) -> r h n", n=DK)).then_inc(wa_loaded, 16)
            pool.dma_start(a_up[LOWRANK:2 * LOWRANK, :, DK:P], wa2_b[0].rearrange("r (h n) -> r h n", n=DK)).then_inc(wa_loaded, 16)
            pool.dma_start(w_a, in_k[:, :, COL_A:COL_A + 2 * LOWRANK]).then_inc(wa_loaded, 16)
            pool.dma_start(router, router_w[0].rearrange("(k p) e -> p k e", p=P)).then_inc(router_loaded, 16)
            pool.dma_start(sgu_w, sgu_norm_w.to_broadcast([P, 512])).then_inc(sguw_loaded, 16)
            wait_filled(pool, JOB["rank",])
            nc.gpsimd.memset(xe[:, :, :, SLOTS:PADDED], 0.0).then_inc(xe_zeroed, 1)
            wait_filled(pool, JOBS_TRUNK + R3(1, 2) + PAIR_JOBS * (PAIRS - 1))
            pool.dma_start(final_w, final_norm_w.rearrange("(a n) -> a n", a=1).to_broadcast([P, D])).then_inc(final_loaded, 16)

        @block.tensor
        def _(pe):
            def ada_product(c5):
                w = wait_trunk_chunk(pe, CHUNK_OF["ada", 512 * c5])
                n = JOB["adaR", c5]
                wait_bank_free(pe, n)
                for i in range(2):
                    for gr in range(4):
                        kt = 4 * i + gr
                        mm = nc.tensor.matmul(bank(n)[gr * PART:(gr + 1) * PART, :], silu_c[:, kt, :], w[:, kt, :],
                                              start=(i == 0), stop=(i == 1))
                filled(mm, n)

            def ada_turn(c5):
                wait_stored(pe, JOB["adaR", c5])
                n = JOB["adaT", c5]
                wait_bank_free(pe, n)
                for j in range(4):
                    mm = nc.tensor.transpose(bank(n)[:, j * P:(j + 1) * P], ada_rows[:, c5 % 2, j * P:(j + 1) * P], ident)
                filled(mm, n)

            def project(name, col):
                w = wait_trunk_chunk(pe, CHUNK_OF["in", col])
                for t in range(TILES):
                    n = JOB[name, t]
                    wait_bank_free(pe, n)
                    for kt in range(KT):
                        mm = nc.tensor.matmul(bank(n), hT[:, kt, t * P:(t + 1) * P], w[:, kt, :],
                                              start=(kt == 0), stop=(kt == KT - 1))
                    filled(mm, n)

            pe.wait_ge(ident_loaded, 16)
            pe.wait_ge(vecs_loaded, 16 * 9)
            n = JOB["vec",]
            filled(nc.tensor.transpose(bank(n)[:, 0:V_ROWS], vec_rows[0:V_ROWS, :], ident[0:V_ROWS, 0:V_ROWS]), n)
            pe.wait_ge(ws_loaded, 16)
            n = JOB["wsT",]
            for gr in range(GROUPS):
                mm = nc.tensor.transpose(bank(n)[:, gr * P:(gr + 1) * P], ws[:, gr, :], ident)
            filled(mm, n)
            pe.wait_ge(silu_c_ready, 1)
            for c5 in range(5):
                if c5 < 4:
                    ada_product(c5)
                if c5 > 0:
                    ada_turn(c5 - 1)
            pe.wait_ge(xn_ready, TILES)
            for kt in range(KT):
                n = JOB["xT", kt]
                wait_bank_free(pe, n)
                for t in range(ST):
                    mm = nc.tensor.transpose(bank(n)[:, t * P:(t + 1) * P], xn[:, t, kt * P:(kt + 1) * P], ident)
                filled(mm, n)
            for half in range(2):
                n = JOB["xTp", half]
                wait_bank_free(pe, n)
                for j in range(4):
                    kt = 4 * half + j
                    mm = nc.tensor.transpose(bank(n)[:, j * P:(j + 1) * P], xn[:, ST, kt * P:(kt + 1) * P], ident)
                filled(mm, n)
            for kt in range(KT):
                wait_stored(pe, JOB["xT", kt])
            for half in range(2):
                wait_stored(pe, JOB["xTp", half])
            w = wait_trunk_chunk(pe, CHUNK_OF["in", COL_QK])
            nP = JOB["qkP",]
            wait_bank_free(pe, nP)
            for m in range(4):
                n = JOB["qkS", m]
                wait_bank_free(pe, n)
                for kt in range(KT):
                    mm = nc.tensor.matmul(bank(n), w[:, kt, m * P:(m + 1) * P], hT[:, kt, 0:SAMPLE],
                                          start=(kt == 0), stop=(kt == KT - 1))
                    mp = nc.tensor.matmul(bank(nP)[:, m * P:(m + 1) * P], w[:, kt, m * P:(m + 1) * P], hT[:, kt, SAMPLE:TOK],
                                          start=(kt == 0), stop=(kt == KT - 1))
                filled(mm, n)
            filled(mp, nP)
            ada_product(4)
            ada_product(5)
            pe.wait_ge(wa_loaded, 48)
            for name, lo, hi in (("aS", 0, SAMPLE), ("aP", SAMPLE, TOK)):
                n = JOB[name,]
                wait_bank_free(pe, n)
                for kt in range(KT):
                    mm = nc.tensor.matmul(bank(n)[0:2 * LOWRANK, 0:hi - lo], w_a[:, kt, :], hT[:, kt, lo:hi],
                                          start=(kt == 0), stop=(kt == KT - 1))
                filled(mm, n)
            wait_stored(pe, JOB["aS",])
            wait_stored(pe, JOB["aP",])
            for hd in range(HEADS):
                n = JOB["zS", hd]
                wait_bank_free(pe, n)
                filled(nc.tensor.matmul(bank(n), a_up[:, hd, :], aT[:, 0:SAMPLE], start=True, stop=True), n)
            n = JOB["zP",]
            wait_bank_free(pe, n)
            for hd in range(HEADS):
                mm = nc.tensor.matmul(bank(n)[:, hd * P:(hd + 1) * P], a_up[:, hd, :], aT[:, SAMPLE:TOK], start=True, stop=True)
            filled(mm, n)
            project("v", COL_V)
            ada_turn(4)
            ada_turn(5)
            ada_product(6)
            ada_product(7)
            project("g", COL_G)
            ada_turn(6)
            ada_turn(7)
            ada_product(8)
            ada_product(9)
            pe.wait_ge(kdT_ready, 1)
            kdT = rem.rearrange("p (h n) -> p h n", h=HEADS)
            for t in range(TILES):
                n = JOB["kd", t]
                wait_bank_free(pe, n)
                for hd in range(HEADS):
                    mm = nc.tensor.transpose(bank(n)[:, hd * P:(hd + 1) * P], kdT[:, hd, t * P:(t + 1) * P], ident)
                filled(mm, n)
            for ck in range(CHUNKS):
                n = JOB["ds", ck]
                t, lo = ck // 2, (ck % 2) * CH
                if ck % 2 == 0:
                    wait_stored(pe, JOB["v", t])
                    wait_stored(pe, JOB["kd", t])
                wait_bank_free(pe, n)
                for hd in range(HEADS):
                    mm = nc.tensor.matmul(bank(n)[:, hd * P:(hd + 1) * P], kd[lo:lo + CH, t, hd, :],
                                          v[lo:lo + CH, t, hd * P:(hd + 1) * P], start=True, stop=True)
                filled(mm, n)
            project("u", COL_U)
            ada_turn(8)
            ada_turn(9)
            ada_product(10)
            project("sv", COL_SV)
            ada_turn(10)
            ada_product(11)
            wait_stored(pe, JOB["wsT",])
            for t in range(TILES):
                n = JOB["mix", t]
                pe.wait_ge(sgu_vn_ready, t + 1)
                wait_bank_free(pe, n)
                for gr in range(GROUPS):
                    mm = nc.tensor.matmul(bank(n)[:, gr * P:(gr + 1) * P], wsT[:, gr, :],
                                          s_vn(t)[:, gr * P:(gr + 1) * P], start=True, stop=True)
                filled(mm, n)
            ada_turn(11)

            def gate_rows(name, gate):
                for qd in range(4):
                    n = JOB[name, qd]
                    wait_bank_free(pe, n)
                    for j in range(4):
                        mm = nc.tensor.matmul(bank(n)[:, j * P:(j + 1) * P],
                                              mod[:, gate + 4 * (qd % 2) + j, qd // 2:qd // 2 + 1].to_broadcast([P, P]), ident,
                                              start=True, stop=True)
                    filled(mm, n)

            pe.wait_ge(mod_summed, 6)
            gate_rows("g1", GATE1)

            def attention(t):
                for d, name in ((0, "attF"), (1, "attB")):
                    n = JOB[name, t]
                    wait_bank_free(pe, n)
                    for hd in range(HEADS):
                        mm = nc.tensor.matmul(bank(n)[:, hd * P:(hd + 1) * P], k[d * DK:(d + 1) * DK, hd, t * P:(t + 1) * P],
                                              q[d * DK:(d + 1) * DK, hd, t * P:(t + 1) * P], start=True, stop=True)
                    filled(mm, n)

            def gla_out(t):
                n = JOB["o", t]
                wait_bank_free(pe, n)
                wait_stored(pe, JOB["attF", t])
                wait_stored(pe, JOB["attB", t])
                for hd in range(HEADS):
                    o = bank(n)[:, hd * P:(hd + 1) * P]
                    vh = v[:, t, hd * P:(hd + 1) * P]
                    nc.tensor.matmul(o, att[:, t % 2, 0, hd, :], vh, start=True, stop=False, skip_group_check=True)
                    nc.tensor.matmul(o, att[:, t % 2, 1, hd, :], vh, start=False, stop=False, skip_group_check=True)
                    for half in range(2):
                        ck = 2 * t + half
                        mm = nc.tensor.matmul(o[half * CH:(half + 1) * CH, :], q[:, hd, ck * CH:(ck + 1) * CH],
                                              states[:, ck, hd, :], start=False, stop=True, skip_group_check=True)
                filled(mm, n)

            def mix_turn(t):
                pe.wait_ge(o_ready, t + 1)
                pe.wait_ge(s_ready, TILES)
                for half in range(2):
                    n = JOB["mT", t, half]
                    wait_bank_free(pe, n)
                    src = o_tok[:, t % 2, :] if half == 0 else s[:, t, :]
                    for j in range(4):
                        mm = nc.tensor.transpose(bank(n)[:, j * P:(j + 1) * P], src[:, j * P:(j + 1) * P], ident)
                    filled(mm, n)
                wait_stored(pe, JOB["mT", t, 0])
                wait_stored(pe, JOB["mT", t, 1])
                for half in range(2):
                    w = wait_trunk_chunk(pe, CHUNK_OF["out", 512 * half])
                    n = JOB["out", t, half]
                    wait_bank_free(pe, n)
                    for kt in range(KT):
                        mm = nc.tensor.matmul(bank(n), mixT[:, t % 2, kt, :], w[:, kt, :], start=(kt == 0), stop=(kt == KT - 1))
                    filled(mm, n)

            pe.wait_ge(qe_ready, 1)
            pe.wait_ge(ke_ready, 1)
            pe.wait_ge(fin_ready, 1)
            def route(t):
                pe.wait_ge(xn2_ready, t + 1)
                for half in range(2):
                    n = JOB["hT", t, half]
                    wait_bank_free(pe, n)
                    for j in range(4):
                        kt = 4 * half + j
                        mm = nc.tensor.transpose(bank(n)[:, j * P:(j + 1) * P], xn2[:, t, kt * P:(kt + 1) * P], ident)
                    filled(mm, n)
                w = 0 if t < ST else 1
                n = JOB["logit", t]
                wait_bank_free(pe, n)
                for kt in range(KT):
                    nc.tensor.matmul(bank(n)[:, 0:EXPERTS], mod[:, SHIFT2 + kt, w:w + 1].to_broadcast([P, P]), router[:, kt, :],
                                     start=(kt == 0), stop=False)
                wait_stored(pe, JOB["hT", t, 0])
                wait_stored(pe, JOB["hT", t, 1])
                for kt in range(KT):
                    mm = nc.tensor.matmul(bank(n)[:, 0:EXPERTS], h2T[:, kt, :], router_amp[:, w, kt, :],
                                          start=False, stop=(kt == KT - 1))
                filled(mm, n)

            pe.wait_ge(router_amp_ready, 1)
            for t in range(TILES + 3):
                if t < TILES:
                    attention(t)
                if 1 <= t <= TILES:
                    gla_out(t - 1)
                if 2 <= t < TILES + 2:
                    mix_turn(t - 2)
                if t >= 3:
                    route(t - 3)
            pe.wait_ge(mod_summed, 12)
            gate_rows("g2", GATE2)
            pe.wait_ge(probs_ready, 1)
            n = JOB["pS",]
            wait_bank_free(pe, n)
            for t in range(ST):
                mm = nc.tensor.transpose(bank(n)[0:EXPERTS, t * P:(t + 1) * P], probs[:, t, 0:EXPERTS], ident)
            filled(mm, n)
            n = JOB["pP",]
            wait_bank_free(pe, n)
            filled(nc.tensor.transpose(bank(n)[0:EXPERTS, 0:P], probs[:, ST, 0:EXPERTS], ident), n)
            pe.wait_ge(rank_rows_ready, 1)
            n = JOB["rank",]
            wait_bank_free(pe, n)
            for t in range(TILES):
                mm = nc.tensor.transpose(bank(n)[:, t * EXPERTS:(t + 1) * EXPERTS], top_rank[:, t * P:(t + 1) * P],
                                         ident[0:EXPERTS, 0:EXPERTS])
            filled(mm, n)

            def gather(job, pair=None):
                for half in range(2):
                    n = job("XG_S", half)
                    wait_bank_free(pe, n, pair)
                    for t in range(ST):
                        mm = nc.tensor.matmul(bank(n), hot_s[:, t, :, :], xn2[:, t, half * 512:(half + 1) * 512],
                                              start=(t == 0), stop=(t == ST - 1))
                    filled(mm, n)
                for half in range(2):
                    n = job("XG_P", half)
                    wait_bank_free(pe, n, pair)
                    filled(nc.tensor.matmul(bank(n)[0:2 * CAP_P, :], hot_p, xn2[:, ST, half * 512:(half + 1) * 512],
                                            start=True, stop=True), n)

            def turn_gathered(job, pair=None):
                for half in range(2):
                    wait_stored(pe, job("XG_P", half), pair)
                wait_bank_free(pe, job("XT_P"), pair)
                for half in range(2):
                    n = job("XT_S", half)
                    wait_bank_free(pe, n, pair)
                    wait_stored(pe, job("XG_S", half), pair)
                    for j in range(4):
                        mm = nc.tensor.transpose(bank(n)[:, j * P:(j + 1) * P], xg_s[:, (4 * half + j) * P:(4 * half + j + 1) * P], ident)
                    filled(mm, n)
                n = job("XT_P")
                for kt in range(KT):
                    nc.tensor.transpose(bank(n)[:, kt * 2 * CAP_P:(kt + 1) * 2 * CAP_P], xg_p[:, kt * P:(kt + 1) * P],
                                        ident[0:2 * CAP_P, 0:2 * CAP_P])
                filled(nc.tensor.transpose(bank(n)[0:2 * PART, 256:256 + P], gate_p, ident), n)

            def wait_gathered(job, pair=None):
                for half in range(2):
                    wait_stored(pe, job("XT_S", half), pair)
                wait_stored(pe, job("XT_P"), pair)

            pe.wait_ge(hot_ready, 4)
            gather(first_gather)
            turn_gathered(first_gather)
            wait_gathered(first_gather)
            pe.wait_ge(xe_zeroed, 1)

            def pair_products(pair, last=False):
                J = JOBS_TRUNK

                def rounds(e, r):
                    for which, job in ((0, R1), (1, R3)):
                        n = J + job(e, r)
                        w = {f4: wait_expert_chunk(pe, 12 * e + EXPERT_CHUNKS.index((which, f4)), pair)
                             .rearrange("p (k n) -> p k n", k=KT) for f4 in sorted({f4 for f4, _ in ROUNDS[r]})}
                        wait_bank_free(pe, n, pair)
                        for kt in range(KT):
                            for gr, (f4, part) in enumerate(ROUNDS[r]):
                                mm = nc.tensor.matmul(bank(n)[gr * PART:(gr + 1) * PART, :],
                                                      xe[:, e, kt, part * PART:(part + 1) * PART], w[f4][:, kt, :],
                                                      start=(kt == 0), stop=(kt == KT - 1))
                        filled(mm, n)

                def turn_h(e, r):
                    n = J + T(e, r)
                    wait_bank_free(pe, n, pair)
                    wait_stored(pe, J + R3(e, r), pair)
                    for j in range(4):
                        mm = nc.tensor.transpose(bank(n)[:, j * P:(j + 1) * P], h_rows[:, r, j * P:(j + 1) * P], ident)
                    filled(mm, n)

                def down(e, i):
                    w = wait_expert_chunk(pe, 12 * e + 8 + i, pair).rearrange("p (k n) -> p k n", k=4)
                    n0, n1 = J + Y(e, 0), J + Y(e, 1)
                    for f in range(4):
                        ft = 4 * i + f
                        for gr, (half, part) in enumerate(((0, 0), (0, 1), (0, 2), (1, 2))):
                            m0 = nc.tensor.matmul(bank(n0)[gr * PART:(gr + 1) * PART, :], h[:, ft, part * PART:(part + 1) * PART],
                                                  w[:, f, half * 512:(half + 1) * 512], start=(ft == 0), stop=(ft == 15))
                    if i == 3:
                        filled(m0, n0)
                    for f in range(0, 4, 2):
                        for odd in range(2):
                            ft = 4 * i + f + odd
                            for part in range(2):
                                gr = 2 * odd + part
                                m1 = nc.tensor.matmul(bank(n1)[gr * PART:(gr + 1) * PART, :], h[:, ft, part * PART:(part + 1) * PART],
                                                      w[:, f + odd, 512:D], start=(ft < 2), stop=(ft >= 14))
                    if i == 3:
                        filled(m1, n1)
                    else:
                        m1.then_inc(w2_read, 1)

                for e in range(2):
                    rounds(e, 0)
                    rounds(e, 1)
                    turn_h(e, 0)
                    if e == 0:
                        n = J + G_S
                        wait_bank_free(pe, n, pair)
                        for t in range(ST):
                            mm = nc.tensor.transpose(bank(n)[:, t * P:(t + 1) * P], gate_s[:, t, :, :], ident)
                        filled(mm, n)
                    rounds(e, 2)
                    turn_h(e, 1)
                    wait_bank_free(pe, J + Y(e, 0), pair)
                    wait_bank_free(pe, J + Y(e, 1), pair)
                    wait_stored(pe, J + T(e, 0), pair)
                    down(e, 0)
                    turn_h(e, 2)
                    wait_stored(pe, J + T(e, 1), pair)
                    down(e, 1)
                    wait_stored(pe, J + T(e, 2), pair)
                    down(e, 2)
                    down(e, 3)
                if not last:
                    pe.wait_ge(hot_ready, 8 + pair * 4)
                    gather(next_gather, pair)
                wait_stored(pe, J + G_S, pair)
                wait_stored(pe, J + Y(1, 0), pair)
                pe.wait_ge(y_added, 2 + pair * 2)
                for i, t in enumerate(COMB_ORDER):
                    if i == COMB_AHEAD and not last:
                        turn_gathered(next_gather, pair)
                    for half in range(2):
                        n = J + COMB(t, half, last)
                        cols = slice(half * 512, (half + 1) * 512)
                        wait_bank_free(pe, n, pair)
                        if t < ST:
                            mm = nc.tensor.matmul(bank(n), gT_s[:, t * P:(t + 1) * P], y_s[:, cols], start=True, stop=True)
                        else:
                            mm = nc.tensor.matmul(bank(n), gT_p, y_p[:, cols], start=True, stop=True)
                        filled(mm, n)
                if not last:
                    wait_gathered(next_gather, pair)

            with pe.Fori(0, PAIRS - 1) as pair:
                pair_products(pair)
            pair_products(PAIRS - 1, last=True)

        @block.scalar
        def _(act):
            steps = [0]

            def link(ins):
                steps[0] += 1
                ins.then_inc(act_step, 1)
                act.wait_ge(act_step, steps[0])

            rows = [(V_ADAB, ada_b.rearrange("a (k n) -> (a k) n", n=P)), (V_C, c.rearrange("a (k n) -> (a k) n", n=P)),
                    (V_CCTX, c_ctx.rearrange("(k n) -> k n", n=P)), (V_N1, norm1_w.rearrange("a (k n) -> (a k) n", n=P)),
                    (V_N2, norm2_w.rearrange("a (k n) -> (a k) n", n=P)), (V_BS, sgu_bs[0]), (V_GLAW, gla_norm_w)]
            for row, src in rows:
                act.dma_start(vec_rows[row:row + src.shape[0], :], src).then_inc(vecs_loaded, 16)
            act.dma_start(vec_rows[V_BA:V_BA + HEADS, 0:DK], ba_f.rearrange("a (h n) -> (a h) n", n=DK)).then_inc(vecs_loaded, 16)
            act.dma_start(vec_rows[V_BA:V_BA + HEADS, DK:P], ba_b.rearrange("a (h n) -> (a h) n", n=DK)).then_inc(vecs_loaded, 16)
            act.dma_start(ws, sgu_ws[0].rearrange("g p q -> p g q")).then_inc(ws_loaded, 16)
            wait_stored(act, JOB["vec",])
            act.wait_ge(silu_c_zeroed, 1)
            nc.scalar.activation(silu_c[:, :, 0:2], vecs[:, V_C:V_C + 16].rearrange("p (w k) -> p k w", w=2), ACT.Silu).then_inc(silu_c_ready, 1)
            for t in range(TILES):
                if t < ST:
                    act.wait_ge(x_pos_ready, t + 1)
                else:
                    act.wait_ge(x_loaded[ST], 16)
                nc.scalar.activation(xn[:, t, :], x[:, t, :], ACT.Square, accum_out=stats[:, t:t + 1]).then_inc(x_squared, 1)
            act.wait_ge(x_recip, 1)
            nc.scalar.activation(stats[:, 10:15], stats[:, 5:10], ACT.Sqrt).then_inc(x_rs, 1)
            def store_ada_rows(first, end):
                for c5 in range(first, end):
                    n = JOB["adaR", c5]
                    wait_filled(act, n)
                    if c5 >= 2:
                        wait_filled(act, JOB["adaT", c5 - 2])
                    stored(nc.scalar.copy(ada_rows[:, c5 % 2, :], bank(n)), n)

            store_ada_rows(0, 4)
            n = JOB["wsT",]
            wait_filled(act, n)
            stored(nc.scalar.copy(wsT, bank(n).rearrange("p (g n) -> p g n", g=GROUPS)), n)
            act.wait_ge(mod_ready, 1)
            for kt in range(0, KT, 2):
                n = JOB["xT", kt]
                wait_filled(act, n)
                stored(nc.scalar.activation(hT[:, kt, 0:SAMPLE], bank(n), ACT.Identity, bias=mod[:, SHIFT1 + kt, 0:1],
                                            scale=amp1[:, kt, 0:1]), n)
            n = JOB["xTp", 0]
            wait_filled(act, n)
            for j in range(4):
                ins = nc.scalar.activation(hT[:, j, SAMPLE:TOK], bank(n)[:, j * P:(j + 1) * P], ACT.Identity,
                                           bias=mod[:, SHIFT1 + j, 1:2], scale=amp1[:, j, 1:2])
            stored(ins, n)
            for m in range(5):
                n = JOB["qkS", m] if m < 4 else JOB["qkP",]
                wait_filled(act, n)
                for mm in ([m] if m < 4 else range(4)):
                    dst, scale = (q, DK ** -0.5) if mm < 2 else (k, 1.0)
                    for hh in range(2):
                        for half in range(2):
                            src = bank(n)[hh * DK:(hh + 1) * DK, :] if m < 4 else bank(n)[hh * DK:(hh + 1) * DK, mm * P:(mm + 1) * P]
                            hd = 2 * (mm % 2) + hh
                            lo, hi = (0, SAMPLE) if m < 4 else (SAMPLE, TOK)
                            ins = nc.scalar.activation(dst[half * DK:(half + 1) * DK, hd, lo:hi], src, ACT.Copy, scale=scale)
                stored(ins, n)
            store_ada_rows(4, 6)
            wait_stored(act, JOB["zP",])
            link(nc.scalar.activation(rem, z, ACT.Abs))
            link(nc.scalar.activation(rem, rem, ACT.Exp, scale=-1.0))
            nc.scalar.activation(rem, rem, ACT.Ln, bias=1.0).then_inc(z_ln, 1)

            def store_v(t):
                n = JOB["v", t]
                wait_filled(act, n)
                stored(nc.scalar.copy(v[:, t, :], bank(n)), n)

            for t in range(TILES):
                store_v(t)
            store_ada_rows(6, 8)
            act.wait_ge(cum_ready, 1)
            nc.scalar.activation(z, cum, ACT.Exp, scale=1.0 / GATE_NORM).then_inc(exp_cum, 1)
            act.wait_ge(rem_ready, 1)
            nc.scalar.activation(rem, rem, ACT.Exp, scale=1.0 / GATE_NORM).then_inc(exp_rem, 1)
            act.wait_ge(exp_cum, 1)
            nc.scalar.activation(cum, cum, ACT.Exp, scale=-1.0 / GATE_NORM).then_inc(exp_neg, 1)
            nc.scalar.activation(chunk_decay, stats[:, 40:80].rearrange("p (h n) -> p h n", h=HEADS), ACT.Exp,
                                 scale=1.0 / GATE_NORM).then_inc(decay_ready, 1)
            for t in range(TILES):
                n = JOB["g", t]
                wait_filled(act, n)
                stored(nc.scalar.activation(g[:, t, :], bank(n), ACT.Silu), n)
            store_ada_rows(8, 10)
            for t in range(TILES):
                n = JOB["kd", t]
                wait_filled(act, n)
                stored(nc.scalar.copy(kd[:, t, :, :], bank(n).rearrange("p (h n) -> p h n", h=HEADS)), n)
            act.wait_ge(qe_ready, 1)
            act.wait_ge(ke_ready, 1)
            for ck in range(CHUNKS):
                n = JOB["ds", ck]
                wait_filled(act, n)
                src = bank(n).rearrange("p (h e) -> p h e", h=HEADS)
                if ck < SCH:
                    moves = [(slice(0, DK), ck + 1)] * (ck + 1 < SCH) + [(slice(DK, P), ck - 1)] * (ck > 0)
                    dsts = [(rows, states[rows, to, :, :]) for rows, to in moves]
                elif ck == SCH:
                    dsts = [(slice(0, DK), states[0:DK, SCH + 1, :, :]), (slice(DK, P), fin[DK:P, :, :])]
                else:
                    dsts = [(slice(0, DK), fin[0:DK, :, :]), (slice(DK, P), states[DK:P, SCH, :, :])]
                for rows, dst in dsts:
                    ins = nc.scalar.copy(dst, src[rows])
                stored(ins, n)
            for t in range(TILES):
                n = JOB["u", t]
                wait_filled(act, n)
                stored(nc.scalar.activation(s[:, t, :], bank(n), ACT.Gelu_apprx_tanh), n)
            store_ada_rows(10, 11)
            for t in range(TILES):
                n = JOB["sv", t]
                wait_filled(act, n)
                stored(nc.scalar.activation(s_vn(t), bank(n), ACT.Gelu_apprx_tanh), n)
            store_ada_rows(11, 12)
            for t in range(TILES):
                act.wait_ge(sgu_recip, t + 1)
                nc.scalar.activation(stats[:, 84:88], stats[:, 80:84], ACT.Sqrt).then_inc(sgu_rs, 1)
            for qd in range(4):
                n = JOB["g1", qd]
                wait_filled(act, n)
                stored(nc.scalar.copy(gate1_rows[:, qd // 2, (qd % 2) * 512:(qd % 2) * 512 + 512], bank(n)), n)

            def mix_store(t):
                n = JOB["mT", t, 0]
                wait_filled(act, n)
                if t == 1:
                    act.wait_ge(state_saved, 32)
                if t >= 2:
                    wait_filled(act, JOB["out", t - 2, 1])
                stored(nc.scalar.activation(mixT[:, t % 2, 0:4, :], bank(n).rearrange("p (k n) -> p k n", k=4), ACT.Identity,
                                            bias=0.0, scale=vecs[:, V_GLAW:V_GLAW + 1]), n)
                n = JOB["mT", t, 1]
                wait_filled(act, n)
                stored(nc.scalar.copy(mixT[:, t % 2, 4:8, :], bank(n).rearrange("p (k n) -> p k n", k=4)), n)

            def norm2(t):
                act.wait_ge(x1_ready, t + 1)
                nc.scalar.activation(xn2[:, t, :], x[:, t, :], ACT.Square, accum_out=stats[:, 96:97]).then_inc(x1_squared, 1)
                act.wait_ge(x1_recip, t + 1)
                nc.scalar.activation(stats[:, 98:99], stats[:, 97:98], ACT.Sqrt).then_inc(x1_rs, 1)

            for t in range(TILES + 3):
                if 1 <= t <= TILES:
                    n = JOB["o", t - 1]
                    wait_filled(act, n)
                    if t - 1 >= 2:
                        wait_filled(act, JOB["mT", t - 3, 0])
                    stored(nc.scalar.copy(o_tok[:, (t - 1) % 2, :], bank(n)), n)
                    act.wait_ge(o_recip, t)
                    nc.scalar.activation(stats[:, 108:112], stats[:, 104:108], ACT.Sqrt).then_inc(o_rs, 1)
                if 2 <= t < TILES + 2:
                    mix_store(t - 2)
                if t >= 3:
                    n = JOB["hT", t - 3, 0]
                    wait_filled(act, n)
                    if t > 3:
                        wait_filled(act, JOB["logit", t - 4])
                    stored(nc.scalar.copy(h2T[:, 0:4, :], bank(n).rearrange("p (k n) -> p k n", k=4)), n)
                if 2 <= t < TILES + 2:
                    norm2(t - 2)
            act.wait_ge(max_ready, 1)
            nc.scalar.activation(logits, logits, ACT.Exp).then_inc(exp_ready, 1)
            for qd, dst, rows in ((0, gate2_0, slice(0, CAP_S)), (1, gate2_1, slice(0, P)),
                                  (2, gate2_0, slice(CAP_S, CAP_S + PART)), (3, gate2_0, slice(CAP_S + PART, P))):
                n = JOB["g2", qd]
                wait_filled(act, n)
                stored(nc.scalar.copy(dst[rows], bank(n)[rows]), n)

            def store_gathered(job, pair=None):
                for half in range(2):
                    n = job("XG_S", half)
                    wait_filled(act, n, pair)
                    stored(nc.scalar.copy(xg_s[:, half * 512:(half + 1) * 512], bank(n)), n)
                for half in range(2):
                    n = job("XG_P", half)
                    wait_filled(act, n, pair)
                    stored(nc.scalar.copy(xg_p[:, half * 512:(half + 1) * 512], bank(n)[0:2 * CAP_P, :]), n)

            store_gathered(first_gather)

            def pair_work(pair, last=False):
                J = JOBS_TRUNK

                def store_h(e, r):
                    n = J + T(e, r)
                    wait_filled(act, n, pair)
                    src = bank(n).rearrange("p (j n) -> p j n", j=4)
                    moves = [[(0, 0, 0, PADDED), (PADDED, 1, 2 * PART, PART)],
                             [(0, 1, 0, 2 * PART), (2 * PART, 2, 0, 2 * PART)],
                             [(0, 3, 0, PADDED), (PADDED, 2, 2 * PART, PART)]][r]
                    for lo, f4, to, width in moves:
                        ins = nc.scalar.copy(h[:, 4 * f4:4 * f4 + 4, to:to + width], src[:, :, lo:lo + width])
                    stored(ins, n)

                def silu(e, r):
                    i = 3 * e + r
                    n = J + R1(e, r)
                    wait_filled(act, n, pair)
                    if i >= 2:
                        wait_stored(act, J + R3((i - 2) // 3, (i - 2) % 3), pair)
                    stored(nc.scalar.activation(silu_h[:, i % 2, :], bank(n), ACT.Silu), n)

                for e in range(2):
                    silu(e, 0)
                    silu(e, 1)
                    store_h(e, 0)
                    if e == 0:
                        n = J + G_S
                        wait_filled(act, n, pair)
                        stored(nc.scalar.copy(gT_s, bank(n)), n)
                    silu(e, 2)
                    store_h(e, 1)
                    store_h(e, 2)
                if not last:
                    store_gathered(next_gather, pair)

            with act.Fori(0, PAIRS - 1) as pair:
                pair_work(pair)
            pair_work(PAIRS - 1, last=True)
            for t in range(TILES):
                wait_stored(act, JOBS_TRUNK + PAIR_JOBS * (PAIRS - 1) + COMB(t, 1, True))
                if t >= 2:
                    act.wait_ge(y_saved[t % 2], 16 * (t // 2))
                nc.scalar.activation(y_out[:, t % 2, :], x[:, t, :], ACT.Square, accum_out=stats[:, 130:131]).then_inc(y_squared, 1)
                act.wait_ge(y_recip, t + 1)
                nc.scalar.activation(stats[:, 132:133], stats[:, 131:132], ACT.Sqrt).then_inc(y_rs, 1)

        @block.vector
        def _(dve):
            steps = [0]

            def link(ins):
                steps[0] += 1
                ins.then_inc(vec_step, 1)
                dve.wait_ge(vec_step, steps[0])

            def mean_recip(out, sums, width, then, own=link):
                own(nc.vector.tensor_scalar(out, sums, 1.0 / width, EPS, ALU.mult, ALU.add))
                nc.vector.reciprocal(out, out).then_inc(then, 1)

            n = JOB["vec",]
            wait_filled(dve, n)
            stored(nc.vector.tensor_copy(vecs[:, 0:V_ROWS], bank(n)[:, 0:V_ROWS]), n)
            dve.wait_ge(pos_loaded, 160)
            for t in range(ST):
                dve.wait_ge(x_loaded[t], 16)
                nc.vector.tensor_tensor(x[:, t, 0:512], x[:, t, 0:512], pos_r[:, t, :], ALU.add)
                nc.vector.tensor_tensor(x[:, t, 512:D], x[:, t, 512:D], pos_c, ALU.add).then_inc(x_pos_ready, 1)
            dve.wait_ge(x_pos_ready, ST)
            dve.wait_ge(x_loaded[ST], 16)
            dve.wait_ge(x_squared, TILES)
            mean_recip(stats[:, 5:10], stats[:, 0:5], D, x_recip)
            dve.wait_ge(x_rs, 1)
            for t in range(TILES):
                nc.vector.tensor_scalar(xn[:, t, :], x[:, t, :], stats[:, 10 + t:11 + t], None, ALU.mult).then_inc(xn_ready, 1)

            def store_mod(first, end):
                for c5 in range(first, end):
                    n = JOB["adaT", c5]
                    wait_filled(dve, n)
                    dst = mod[:, 4 * c5:4 * c5 + 4, :]
                    quarters = bank(n).rearrange("p (j q c) -> p j c q", j=4, q=4)[:, :, 0:2, :]
                    stored(nc.vector.tensor_reduce(dst, quarters, AX_X, ALU.add), n)
                    wait_stored(dve, n)
                    nc.vector.tensor_tensor(dst, dst, vecs[:, V_ADAB + 4 * c5:V_ADAB + 4 * c5 + 4, None].to_broadcast([P, 4, 2]),
                                            ALU.add).then_inc(mod_summed, 1)
                dve.wait_ge(mod_summed, end)

            store_mod(0, 4)
            nc.vector.scalar_tensor_tensor(amp1, mod[:, SCALE1:SCALE1 + KT, :], 1.0,
                                           vecs[:, V_N1:V_N1 + KT, None].to_broadcast([P, KT, 2]), ALU.add, ALU.mult)\
                .then_inc(mod_ready, 1)
            dve.wait_ge(mod_ready, 1)
            for kt in range(1, KT, 2):
                n = JOB["xT", kt]
                wait_filled(dve, n)
                stored(nc.vector.tensor_scalar(hT[:, kt, 0:SAMPLE], bank(n), amp1[:, kt, 0:1], mod[:, SHIFT1 + kt, 0:1],
                                               ALU.mult, ALU.add), n)
            n = JOB["xTp", 1]
            wait_filled(dve, n)
            for j in range(4):
                ins = nc.vector.tensor_scalar(hT[:, 4 + j, SAMPLE:TOK], bank(n)[:, j * P:(j + 1) * P], amp1[:, 4 + j, 1:2],
                                              mod[:, SHIFT1 + 4 + j, 1:2], ALU.mult, ALU.add)
            stored(ins, n)
            for name, lo, hi in (("aS", 0, SAMPLE), ("aP", SAMPLE, TOK)):
                n = JOB[name,]
                wait_filled(dve, n)
                stored(nc.vector.tensor_copy(aT[:, lo:hi], bank(n)[0:2 * LOWRANK, 0:hi - lo]), n)
            z3 = z.rearrange("p (h n) -> p h n", h=HEADS)
            cum3 = cum.rearrange("p (h n) -> p h n", h=HEADS)
            for hd in range(HEADS):
                n = JOB["zS", hd]
                wait_filled(dve, n)
                stored(nc.vector.tensor_scalar(z3[:, hd, 0:SAMPLE], bank(n), vecs[:, V_BA + hd:V_BA + hd + 1], None, ALU.add), n)
            n = JOB["zP",]
            wait_filled(dve, n)
            for hd in range(HEADS):
                ins = nc.vector.tensor_scalar(z3[:, hd, SAMPLE:TOK], bank(n)[:, hd * P:(hd + 1) * P],
                                              vecs[:, V_BA + hd:V_BA + hd + 1], None, ALU.add)
            stored(ins, n)
            dve.wait_ge(consts_loaded, 16)
            dve.wait_ge(z_ln, 1)
            link(nc.vector.scalar_tensor_tensor(z, z, 0.0, rem, ALU.min, ALU.subtract))
            for hd in range(HEADS):
                ins = nc.vector.tensor_tensor_scan(cum3[:, hd, :], keep, z3[:, hd, :], 0.0, ALU.mult, ALU.add)
            link(ins)
            cum4 = cum.rearrange("p (m n) -> p m n", n=CH)
            z4 = z.rearrange("p (m n) -> p m n", n=CH)
            rem4 = rem.rearrange("p (m n) -> p m n", n=CH)
            total = stats[:, 40:80]
            link(nc.vector.tensor_copy(total, cum4[:, :, CH - 1]))
            tot_b = stats[:, 40:80, None].to_broadcast([P, HEADS * CHUNKS, CH])
            link(nc.vector.tensor_tensor(cum4[DK:P], tot_b[DK:P], cum4[DK:P], ALU.subtract))
            nc.vector.tensor_tensor(cum4[DK:P], cum4[DK:P], z4[DK:P], ALU.add).then_inc(cum_ready, 1)
            dve.wait_ge(cum_ready, 1)
            nc.vector.tensor_tensor(rem4, tot_b, cum4, ALU.subtract).then_inc(rem_ready, 1)
            q2 = q.rearrange("p h n -> p (h n)")
            k2 = k.rearrange("p h n -> p (h n)")
            wait_stored(dve, JOB["qkP",])
            dve.wait_ge(exp_cum, 1)
            nc.vector.tensor_tensor(q2, q2, z, ALU.mult).then_inc(qe_ready, 1)
            dve.wait_ge(exp_rem, 1)
            nc.vector.tensor_tensor(rem, k2, rem, ALU.mult).then_inc(kdT_ready, 1)
            dve.wait_ge(exp_neg, 1)
            dve.wait_ge(kdT_ready, 1)
            nc.vector.tensor_tensor(k2, k2, cum, ALU.mult).then_inc(ke_ready, 1)
            store_mod(4, 8)
            dve.wait_ge(qe_ready, 1)
            dve.wait_ge(ke_ready, 1)
            link(nc.vector.memset(states[0:DK, SCH, :, :], 0.0))
            link(nc.vector.memset(states[DK:P, SCH + 1, :, :], 0.0))
            dve.wait_ge(s0_loaded, 32)
            dve.wait_ge(decay_ready, 1)
            for ck in range(CHUNKS):
                wait_stored(dve, JOB["ds", ck])

            def advance(rows, dst, src, ck):
                for hd in range(HEADS):
                    ins = nc.vector.scalar_tensor_tensor(dst[rows, hd, :], src[rows, hd, :], chunk_decay[rows, hd, ck:ck + 1],
                                                         dst[rows, hd, :], ALU.mult, ALU.add)
                return ins

            lower, upper = slice(0, DK), slice(DK, P)
            for i in range(SCH - 1):
                advance(lower, states[:, i + 1], states[:, i], i)
                link(advance(upper, states[:, SCH - 2 - i], states[:, SCH - 1 - i], SCH - 1 - i))
            advance(lower, fin, states[:, SCH + 1], SCH + 1)
            advance(upper, fin, states[:, SCH], SCH).then_inc(fin_ready, 1)
            store_mod(8, 10)
            for t in range(TILES):
                wait_stored(dve, JOB["sv", t])
                sv = s_vn(t)
                link(nc.vector.tensor_tensor(sgu_sq, sv, sv, ALU.mult))
                link(nc.vector.tensor_reduce(stats[:, 80:84], sgu_sq.rearrange("p (g n) -> p g n", g=GROUPS), AX_X, ALU.add))
                mean_recip(stats[:, 80:84], stats[:, 80:84], P, sgu_recip)
                dve.wait_ge(sgu_rs, t + 1)
                sv3 = sv.rearrange("p (g n) -> p g n", g=GROUPS)
                nc.vector.tensor_tensor(sv3, sv3, stats[:, 84:88, None].to_broadcast([P, GROUPS, P]), ALU.mult)\
                    .then_inc(sgu_vn_ready, 1)
            store_mod(10, 11)
            dve.wait_ge(sguw_loaded, 16)
            for t in range(TILES):
                n = JOB["mix", t]
                wait_filled(dve, n)
                stored(nc.vector.tensor_tensor(sgu_sq, bank(n), sgu_w, ALU.mult), n)
                wait_stored(dve, n)
                for gr in range(GROUPS):
                    cols = slice(gr * P, (gr + 1) * P)
                    ins = nc.vector.scalar_tensor_tensor(s[:, t, cols], sgu_sq[:, cols], vecs[:, V_BS + gr:V_BS + gr + 1],
                                                         s[:, t, cols], ALU.add, ALU.mult)
                ins.then_inc(s_ready, 1)
                dve.wait_ge(s_ready, t + 1)
            store_mod(11, 12)
            link(nc.vector.scalar_tensor_tensor(amp2, mod[:, SCALE2:SCALE2 + KT, :], 1.0,
                                                vecs[:, V_N2:V_N2 + KT, None].to_broadcast([P, KT, 2]), ALU.add, ALU.mult))
            dve.wait_ge(router_loaded, 16)
            for w in range(2):
                ins = nc.vector.tensor_tensor(router_amp[:, w], router, amp2[:, :, w:w + 1].to_broadcast([P, KT, EXPERTS]), ALU.mult)
            ins.then_inc(router_amp_ready, 1)

            def mask(t):
                for d, name, m in ((0, "attF", mask_f), (1, "attB", mask_b)):
                    n = JOB[name, t]
                    wait_filled(dve, n)
                    if t >= 2:
                        wait_filled(dve, JOB["o", t - 2])
                    stored(nc.vector.copy_predicated(att[:, t % 2, d, :, :], m[:, None, :].to_broadcast([P, HEADS, P]),
                                                     bank(n).rearrange("p (h n) -> p h n", h=HEADS)), n)

            def head_norm(t):
                ot = o_tok[:, t % 2, :]
                wait_stored(dve, JOB["o", t])
                link(nc.vector.tensor_tensor(o_sq, ot, ot, ALU.mult))
                link(nc.vector.tensor_reduce(stats[:, 104:108], o_sq.rearrange("p (g n) -> p g n", g=HEADS), AX_X, ALU.add))
                mean_recip(stats[:, 104:108], stats[:, 104:108], DV, o_recip)
                dve.wait_ge(o_rs, t + 1)
                o3 = ot.rearrange("p (g n) -> p g n", g=HEADS)
                link(nc.vector.tensor_tensor(o3, o3, stats[:, 108:112, None].to_broadcast([P, HEADS, P]), ALU.mult))
                nc.vector.tensor_tensor(ot, ot, g[:, t, :], ALU.mult).then_inc(o_ready, 1)

            def residual(t):
                w = 0 if t < ST else 1
                for half in range(2):
                    n = JOB["out", t, half]
                    cols = slice(half * 512, (half + 1) * 512)
                    wait_filled(dve, n)
                    stored(nc.vector.tensor_tensor(out_tmp[:, half, :], bank(n), gate1_rows[:, w, cols], ALU.mult), n)
                    wait_stored(dve, n)
                    ins = nc.vector.tensor_tensor(x[:, t, cols], x[:, t, cols], out_tmp[:, half, :], ALU.add)
                    if half == 1:
                        ins.then_inc(x1_ready, 1)
                dve.wait_ge(x1_squared, t + 1)
                mean_recip(stats[:, 97:98], stats[:, 96:97], D, x1_recip)
                dve.wait_ge(x1_rs, t + 1)
                nc.vector.tensor_scalar(xn2[:, t, :], x[:, t, :], stats[:, 98:99], None, ALU.mult).then_inc(xn2_ready, 1)

            dve.wait_ge(pool_zeroed, 1)
            for qd in range(4):
                wait_stored(dve, JOB["g1", qd])
            def store_route(t):
                n = JOB["hT", t, 1]
                wait_filled(dve, n)
                if t > 0:
                    wait_filled(dve, JOB["logit", t - 1])
                stored(nc.vector.tensor_copy(h2T[:, 4:8, :], bank(n).rearrange("p (k n) -> p k n", k=4)), n)
                n = JOB["logit", t]
                wait_filled(dve, n)
                stored(nc.vector.tensor_copy(logits[:, t, :], bank(n)[:, 0:EXPERTS]), n)

            for t in range(TILES + 3):
                if t < TILES:
                    mask(t)
                if 1 <= t <= TILES:
                    head_norm(t - 1)
                if 2 <= t < TILES + 2:
                    residual(t - 2)
                if t >= 3:
                    store_route(t - 3)
            wait_stored(dve, JOB["logit", TILES - 1])
            link(nc.vector.tensor_reduce(stats[:, 112:117], logits, AX_X, ALU.max))
            nc.vector.tensor_tensor(logits, logits, stats[:, 112:117, None].to_broadcast([P, TILES, EXPERTS]), ALU.subtract)\
                .then_inc(max_ready, 1)
            dve.wait_ge(exp_ready, 1)
            link(nc.vector.tensor_reduce(stats[:, 120:125], logits, AX_X, ALU.add))
            link(nc.vector.reciprocal(stats[:, 125:130], stats[:, 120:125]))
            nc.vector.tensor_tensor(probs[:, :, 0:EXPERTS], logits, stats[:, 125:130, None].to_broadcast([P, TILES, EXPERTS]), ALU.mult)\
                .then_inc(probs_ready, 1)
            for name, lo, hi, rounds in (("pS", 0, SAMPLE, CAP_S // 8), ("pP", SAMPLE, TOK, CAP_P // 8)):
                n = JOB[name,]
                wait_filled(dve, n)
                work = top_work[:, lo:hi]
                stored(nc.vector.tensor_copy(work, bank(n)[0:EXPERTS, 0:hi - lo]), n)
                wait_stored(dve, n)
                for _ in range(rounds):
                    link(nc.vector.max(top8, work))
                    link(nc.vector.match_replace(out=work, in_to_replace=top8, in_values=work, imm_value=-1.0))
                link(nc.vector.tensor_scalar(top_mask[:, lo:hi], work, 0.0, None, ALU.is_lt))
            link(nc.vector.memset(top_work, 1.0))
            link(nc.vector.tensor_tensor_scan(top_rank[:, 0:SAMPLE], top_work[:, 0:SAMPLE], top_mask[:, 0:SAMPLE], 0.0, ALU.mult, ALU.add))
            link(nc.vector.tensor_tensor_scan(top_rank[:, SAMPLE:TOK], top_work[:, SAMPLE:TOK], top_mask[:, SAMPLE:TOK], 0.0, ALU.mult, ALU.add))
            nc.vector.tensor_tensor(top_rank, top_rank, top_mask, ALU.mult).then_inc(rank_rows_ready, 1)
            n = JOB["rank",]
            wait_filled(dve, n)
            stored(nc.vector.tensor_scalar(rank[:, :, 0:EXPERTS], bank(n)[:, 0:TILES * EXPERTS].rearrange("p (t e) -> p t e", t=TILES),
                                           -1.0, None, ALU.add), n)
            wait_stored(dve, n)

            def one_hots(first, own):
                own(nc.vector.tensor_copy(comb_rk, rank[:, :, bass.ds(first, 2)]))
                own(nc.vector.tensor_copy(comb_pr, probs[:, :, bass.ds(first, 2)]))
                hs = hot_s.rearrange("p t e n -> p (t e) n")
                gs = gate_s.rearrange("p t e n -> p (t e) n")
                rk = comb_rk.rearrange("p t e -> p (t e)")
                pr = comb_pr.rearrange("p t e -> p (t e)")
                nc.vector.tensor_tensor(hs, iota[:, None, :].to_broadcast([P, 2 * ST, CAP_S]),
                                        rk[:, 0:2 * ST, None].to_broadcast([P, 2 * ST, CAP_S]), ALU.is_equal).then_inc(hot_ready, 1)
                nc.vector.tensor_tensor(hot_p, iota[:, None, 0:CAP_P].to_broadcast([P, 2, CAP_P]),
                                        rk[:, 2 * ST:2 * TILES, None].to_broadcast([P, 2, CAP_P]), ALU.is_equal).then_inc(hot_ready, 1)
                return hs, gs, pr

            def gates(hs, gs, pr):
                nc.vector.tensor_tensor(gs, hs, pr[:, 0:2 * ST, None].to_broadcast([P, 2 * ST, CAP_S]), ALU.mult).then_inc(hot_ready, 1)
                for e in range(2):
                    ins = nc.vector.tensor_scalar(gate_p[:, e, :], iota[:, 0:PART], comb_rk[:, ST, e:e + 1], comb_pr[:, ST, e:e + 1],
                                                  ALU.is_equal, ALU.mult)
                ins.then_inc(hot_ready, 1)

            parts = one_hots(0, link)
            dve.wait_ge(hot_ready, 2)
            gates(*parts)

            def modulate(job, own, pair=None):
                xe_k = xe.rearrange("p e k n -> p k e n")
                for half in range(2):
                    n = job("XT_S", half)
                    wait_filled(dve, n, pair)
                    ks = slice(4 * half, 4 * half + 4)
                    dst = xe_k[:, ks, :, 0:CAP_S]
                    own(nc.vector.tensor_tensor(dst, bank(n).rearrange("p (k e n) -> p k e n", k=4, e=2),
                                                amp2[:, ks, 0:1, None].to_broadcast([P, 4, 2, CAP_S]), ALU.mult))
                    stored(nc.vector.tensor_tensor(dst, dst, mod[:, SHIFT2 + 4 * half:SHIFT2 + 4 * half + 4, 0:1, None]
                                                   .to_broadcast([P, 4, 2, CAP_S]), ALU.add), n)
                n = job("XT_P")
                wait_filled(dve, n, pair)
                dst = xe_k[:, :, :, CAP_S:SLOTS]
                nc.vector.tensor_copy(gT_p, bank(n)[0:2 * PART, 256:256 + P])
                own(nc.vector.tensor_tensor(dst, bank(n)[:, 0:256].rearrange("p (k e n) -> p k e n", k=KT, e=2),
                                            amp2[:, :, 1:2, None].to_broadcast([P, KT, 2, CAP_P]), ALU.mult))
                stored(nc.vector.tensor_tensor(dst, dst, mod[:, SHIFT2:SHIFT2 + KT, 1:2, None].to_broadcast([P, KT, 2, CAP_P]),
                                               ALU.add), n)

            modulate(first_gather, link)

            def pair_work(pair, last=False):
                J = JOBS_TRUNK
                pair_steps = [0]
                PER_PAIR = 7

                def link_pair(ins):
                    pair_steps[0] += 1
                    ins.then_inc(vec_pair_step, 1)
                    dve.wait_ge(vec_pair_step, pair_steps[0] + pair * PER_PAIR)

                for e in range(2):
                    for r in range(3):
                        n = J + R3(e, r)
                        wait_stored(dve, J + R1(e, r), pair)
                        wait_filled(dve, n, pair)
                        stored(nc.vector.tensor_tensor(h_rows[:, r, :], silu_h[:, (3 * e + r) % 2, :], bank(n), ALU.mult), n)
                        if (e, r) == (0, 1) and not last:
                            wait_filled(dve, J + G_S, pair)
                            parts = one_hots(2 * pair + 2, link_pair)
                            dve.wait_ge(hot_ready, 6 + pair * 4)
                            gates(*parts)
                    rows_s, rows_p = slice(e * CAP_S, (e + 1) * CAP_S), slice(e * PART, (e + 1) * PART)
                    n = J + Y(e, 0)
                    wait_filled(dve, n, pair)
                    nc.vector.tensor_tensor(y_s[rows_s, 0:512], bank(n)[0:CAP_S], gate2_0[0:CAP_S], ALU.mult)
                    for half in range(2):
                        at = slice(CAP_S + half * PART, CAP_S + (half + 1) * PART)
                        ins = nc.vector.tensor_tensor(y_p[rows_p, half * 512:(half + 1) * 512], bank(n)[at], gate2_0[at], ALU.mult)
                    stored(ins, n)
                    n = J + Y(e, 1)
                    wait_filled(dve, n, pair)
                    link_pair(nc.vector.tensor_tensor(y_s[rows_s, 512:D], bank(n)[0:CAP_S], gate2_1[0:CAP_S], ALU.mult))
                    stored(nc.vector.tensor_tensor(y_half[rows_s], bank(n)[CAP_S:P], gate2_1[CAP_S:P], ALU.mult), n)
                    wait_stored(dve, n, pair)
                    nc.vector.tensor_tensor(y_s[rows_s, 512:D], y_s[rows_s, 512:D], y_half[rows_s], ALU.add).then_inc(y_added, 1)
                for i, t in enumerate(COMB_ORDER):
                    if i == COMB_AHEAD and not last:
                        modulate(next_gather, link_pair, pair)
                    for half in range(2):
                        n = J + COMB(t, half, last)
                        cols = slice(half * 512, (half + 1) * 512)
                        wait_filled(dve, n, pair)
                        stored(nc.vector.tensor_tensor(x[:, t, cols], x[:, t, cols], bank(n), ALU.add), n)
                assert last or pair_steps[0] == PER_PAIR

            with dve.Fori(0, PAIRS - 1) as pair:
                pair_work(pair)
            pair_work(PAIRS - 1, last=True)
            dve.wait_ge(final_loaded, 16)
            final_steps = [0]

            def link_final(ins):
                final_steps[0] += 1
                ins.then_inc(vec_final_step, 1)
                dve.wait_ge(vec_final_step, final_steps[0])

            for t in range(TILES):
                dve.wait_ge(y_squared, t + 1)
                mean_recip(stats[:, 131:132], stats[:, 130:131], D, y_recip, link_final)
                dve.wait_ge(y_rs, t + 1)
                nc.vector.scalar_tensor_tensor(y_out[:, t % 2, :], x[:, t, :], stats[:, 132:133], final_w, ALU.mult, ALU.mult)\
                    .then_inc(y_ready, 1)


_INS = ["x_prompt", "x_sample", "state_gla_fwd", "state_gla_bwd", "c", "c_ctx", "ada_w", "ada_b", "norm1_w", "w_in",
        "gla_wa2_f", "gla_ba_f", "gla_wa2_b", "gla_ba_b", "gla_norm_w", "sgu_norm_w", "sgu_ws", "sgu_bs", "w_out",
        "norm2_w", "router_w", "exp_w1", "exp_w3", "exp_w2", "final_norm_w"]
_OUTS = [(1, PROMPT, D), (1, SAMPLE, D), (1, 1, HEADS, DK, DV), (1, 1, HEADS, DK, DV)]


def kernel(**inputs):
    import numpy as _np
    import concourse.bacc as _bacc
    from concourse import mybir as _mybir
    from concourse.bass_utils import run_bass_kernel_spmd as _run

    nc = _bacc.Bacc("TRN2", target_bir_lowering=False, num_devices=1)
    arrays, args = {}, []
    named = [(name, _np.ascontiguousarray(inputs[name])) for name in _INS]
    named += list(zip(("table", "pos_row", "pos_col"), shape_constants()))
    for name, a in named:
        arrays[f"in_{name}_dram"] = a
        args.append(nc.dram_tensor(f"in_{name}_dram", a.shape, _mybir.dt.from_np(a.dtype), kind="ExternalInput").ap())
    for i, shape in enumerate(_OUTS):
        args.append(nc.dram_tensor(f"out_{i}_dram", shape, F32, kind="ExternalOutput").ap())
    trunk_kernel(nc, *args)
    r = _run(nc, [arrays], core_ids=[0])
    return tuple(r.results[0][f"out_{i}_dram"] for i in range(len(_OUTS)))
```

```python
from contextlib import ExitStack

import numpy as np

import concourse.bass as bass
from concourse import mybir

ALU = mybir.AluOpType
ACT = mybir.ActivationFunctionType
F32 = mybir.dt.float32
I32 = mybir.dt.int32
AX_X = mybir.AxisListType.X

P = 128
D = 1024
KT = D // P
SAMPLE, PROMPT = 512, 128
TILES = (SAMPLE + PROMPT) // P
ST = SAMPLE // P
TOK = SAMPLE + PROMPT
HEADS, DK, DV = 4, 64, 128
CH = 64
CHUNKS = TOK // CH
SCH = SAMPLE // CH
LOWRANK = 16
GATE_NORM = 16.0
GROUPS = 4
EXPERTS = 16
FE = 2048
CAP_S, CAP_P = 2 * SAMPLE // EXPERTS, 2 * PROMPT // EXPERTS
SLOTS = CAP_S + CAP_P
GRID_W = 64
EPS = 1e-6
PAIRS = EXPERTS // 2

COL_QK, COL_V, COL_G, COL_A, COL_U, COL_SV = 0, 512, 1024, 1536, 1568, 2080

BANKS = 8
CHUNK_F = 4096
RING = 6
TRUNK_RING = 3

V_ADAB, V_C, V_CCTX, V_N1, V_N2, V_BS, V_BA, V_GLAW, V_ROWS = 0, 48, 56, 64, 72, 80, 84, 88, 89
SHIFT1, SCALE1, GATE1, SHIFT2, SCALE2, GATE2 = 0, 8, 16, 24, 32, 40


def shape_constants():
    j = np.arange(P)[:, None]
    i = np.arange(P)[None, :]
    same = (j // CH) == (i // CH)
    ident = np.eye(P, dtype=np.float32)
    fwd = (same & (j <= i)).astype(np.float32)
    bwd = (same & (j >= i)).astype(np.float32)
    keep = np.broadcast_to((np.arange(TOK) % CH != 0).astype(np.float32), (P, TOK))
    iota = np.broadcast_to(np.arange(CAP_S, dtype=np.float32), (P, CAP_S))
    table = np.concatenate([ident, fwd, bwd, keep, iota], axis=1).astype(np.float32)
    nf = D // 4
    omega = (1.0 / (np.float32(10000.0) ** (np.arange(nf, dtype=np.float32) / np.float32(nf)))).astype(np.float32)

    def emb(n):
        a = np.arange(n, dtype=np.float32)[:, None] * omega[None, :]
        return np.concatenate([np.sin(a), np.cos(a)], axis=-1).astype(np.float32)

    return table, emb(SAMPLE // GRID_W), np.tile(emb(GRID_W), (P // GRID_W, 1))


XT_AHEAD = 5

GATHER_S, GATHER_P = 4, 2
GATHER_JOBS = [("S", i) for i in range(GATHER_S)] + [("P", i) for i in range(GATHER_P)] + [("G_P",)]


def job_numbers():
    names = [("vec",), ("wsT",)]
    names += [("adaR", 0), ("adaR", 1), ("adaT", 0), ("adaR", 2), ("adaT", 1)]
    names += [("xT", k) for k in range(XT_AHEAD)] + [("adaR", 3), ("adaT", 2), ("adaT", 3)]
    names += [("xT", k) for k in range(XT_AHEAD, KT)] + [("xTp", h) for h in range(2)]
    names += [("qkP",)] + [("qkS", m) for m in range(4)] + [("adaR", 4)]
    names += [("aS",), ("aP",)] + [("zS", h) for h in range(HEADS)] + [("zP",)]
    names += [("v", t) for t in range(TILES)] + [("adaT", 4), ("adaR", 5)]
    names += [("g", t) for t in range(TILES)] + [("adaT", 5), ("adaR", 6)]
    names += [("kd", t) for t in range(TILES)] + [("ds", n) for n in range(CHUNKS)]
    names += [("u", t) for t in range(TILES)] + [("adaT", 6), ("adaR", 7)]
    names += [("sv", t) for t in range(TILES)] + [("adaT", 7), ("adaR", 8), ("adaR", 9)]
    names += [("mix", t) for t in range(TILES)] + [("adaT", 8), ("adaT", 9), ("adaR", 10)]
    for t in range(TILES + 3):
        if t < TILES:
            names += [("attF", t), ("attB", t)]
        if t == 0:
            names += [("adaT", 10), ("adaR", 11)]
        if t == 1:
            names += [("adaT", 11)]
        if 1 <= t <= TILES:
            names += [("o", t - 1)]
        if t == 1:
            names += [("g1", q) for q in range(4)]
        if 2 <= t < TILES + 2:
            names += [("out", t - 2, 0)]
        if 1 <= t <= TILES:
            names += [("mT", t - 1, 0), ("mT", t - 1, 1)]
        if t == TILES + 2:
            names += [("g2", q) for q in range(4)]
        if t >= 3:
            names += [("hT", t - 3, 0), ("hT", t - 3, 1)]
        if 2 <= t < TILES + 2:
            names += [("out", t - 2, 1)]
        if t >= 3:
            names += [("logit", t - 3)]
    names += [("pS",), ("pP",), ("rank",)]
    names += GATHER_JOBS
    return {name: n for n, name in enumerate(names)}


JOB = job_numbers()
JOBS_TRUNK = len(JOB)

PAIR_JOBS = 40
R1 = lambda e, r: (0, 12)[e] + ((0, 2, 6), (0, 2, 5))[e][r]
R3 = lambda e, r: R1(e, r) + 1
T = lambda e, r: ((4, 8, 11), (16, 19, 22))[e][r]
G_S = 5
Y = lambda e, i: (9, 20)[e] + i
NEXT_GATHER = dict(zip(GATHER_JOBS, (23, 24, 25, 26, 27, 28, 31)))
COMB_ORDER = [ST] + list(range(ST))


def COMB(t, half, last):
    i = 2 * COMB_ORDER.index(t) + half
    return (23 if last else 29 if i < 2 else 30) + i


PART = 32
PADDED = 3 * PART
ROUNDS = [[(0, 0, 2), (0, 2, 1), (1, 2, 1)], [(1, 0, 2), (2, 0, 2)], [(3, 0, 2), (3, 2, 1), (2, 2, 1)]]
DOWN_0 = [(0, 0, 2), (0, 2, 1), (1, 2, 1)]
EXPERT_CHUNKS = [(0, 0), (0, 1), (1, 0), (1, 1), (0, 2), (1, 2), (0, 3), (1, 3)]
LAST_ROUND = [0, 1, 2, 2]

ADA = [("ada", 512 * c) for c in range(12)]
TRUNK_CHUNKS = (ADA[0:4] + [("in", COL_QK), ADA[4], ("in", COL_V), ADA[5], ("in", COL_G), ADA[6], ("in", COL_U), ADA[7],
                            ("in", COL_SV)] + ADA[8:12] + [("out", 0), ("out", 512)])
CHUNK_OF = {c: n for n, c in enumerate(TRUNK_CHUNKS)}
EXPERT_SLOT = [3, 4, 5, 1, 2, 0]
LOADS_BEFORE = [len([n for n in range(len(TRUNK_CHUNKS)) if n % TRUNK_RING == s]) if s < TRUNK_RING else 0
                for s in range(RING)]
PAIR_CHUNKS = 24

def trunk_kernel(nc, x_prompt, x_sample, s0_f, s0_b, c, c_ctx, ada_w, ada_b, norm1_w, w_in, wa2_f, ba_f,
                 wa2_b, ba_b, gla_norm_w, sgu_norm_w, sgu_ws, sgu_bs, w_out, norm2_w, router_w, w1, w3, w2,
                 final_norm_w, table, pos_row, pos_col, y_prompt, y_sample, new_f, new_b):
    with ExitStack() as ctx:
        def sb(name, cols):
            return ctx.enter_context(nc.sbuf_tensor(name, [P, cols], F32))

        def sem(name):
            return ctx.enter_context(nc.semaphore(name))

        ring = sb("ring", RING * CHUNK_F)
        consts = sb("consts", 3 * P + TOK + CAP_S)
        ident = consts[:, 0:P]
        mask_f = consts[:, P:2 * P].bitcast(I32)
        mask_b = consts[:, 2 * P:3 * P].bitcast(I32)
        keep = consts[:, 3 * P:3 * P + TOK]
        iota = consts[:, 3 * P + TOK:3 * P + TOK + CAP_S]
        vecs = sb("vecs", 96)
        silu_c = sb("silu_c", PART * KT)[:].rearrange("p (k w) -> p k w", w=PART)
        mod = sb("mod", 96)[:].rearrange("p (k w) -> p k w", w=2)
        amp1 = sb("amp1", 2 * KT)[:].rearrange("p (k w) -> p k w", w=2)
        amp2 = sb("amp2", 2 * KT)[:].rearrange("p (k w) -> p k w", w=2)
        router = sb("router", KT * EXPERTS)[:].rearrange("p (k e) -> p k e", e=EXPERTS)
        router_amp = sb("router_amp", 2 * KT * EXPERTS)[:].rearrange("p (w k e) -> p w k e", w=2, e=EXPERTS)
        x = sb("x", TILES * D)[:].rearrange("p (t d) -> p t d", t=TILES)
        feat = sb("feat", TILES * D)
        hT = feat[:].rearrange("p (k n) -> p k n", k=KT)
        xn2 = feat[:].rearrange("p (t d) -> p t d", t=TILES)
        probs = sb("probs", TILES * EXPERTS)[:].rearrange("p (t e) -> p t e", t=TILES)
        rank = sb("rank", TILES * EXPERTS)[:].rearrange("p (t e) -> p t e", t=TILES)
        stats = sb("stats", 160)
        logits = sb("logits", TILES * EXPERTS)[:].rearrange("p (t e) -> p t e", t=TILES)
        chunk_decay = sb("chunk_decay", HEADS * CHUNKS)[:].rearrange("p (h n) -> p h n", h=HEADS)

        up = TRUNK_RING * CHUNK_F
        q = ring[:, up:up + 2560].rearrange("p (h n) -> p h n", h=HEADS)
        k = ring[:, up + 2560:up + 5120].rearrange("p (h n) -> p h n", h=HEADS)
        v = ring[:, up + 5120:up + 7680].rearrange("p (t n) -> p t n", t=TILES)
        g = ring[:, up + 7680:up + 10240].rearrange("p (t n) -> p t n", t=TILES)
        att = ring[:, up + 10240:up + 12288].rearrange("p (b d h n) -> p b d h n", b=2, d=2, h=HEADS)
        pos_r = ring[:, up:up + 2048].rearrange("p (t n) -> p t n", t=ST)
        pos_c = ring[:, up + 2048:up + 2560]

        both = sb("both", 15872)
        z = both[:, 0:2560]
        cum = both[:, 2560:5120]
        rem = both[:, 5120:7680]
        states = both[:, 0:5120].rearrange("p (n h e) -> p n h e", n=CHUNKS, h=HEADS)
        xn = both[:, 0:5120].rearrange("p (t d) -> p t d", t=TILES)
        gate1_rows = both[:, 5120:7168].rearrange("p (w d) -> p w d", w=2)
        kd = both[:, 7680:10240].rearrange("p (t h d) -> p t h d", t=TILES, h=HEADS)
        a_up = both[:, 7680:8192].rearrange("p (h n) -> p h n", h=HEADS)
        aT = both[:, 8192:8832]
        w_a = both[:, 8832:9088].rearrange("p (k n) -> p k n", k=KT)
        vec_rows = both[:, 9088:9216]
        ws = both[:, 9216:9728].rearrange("p (g n) -> p g n", g=GROUPS)
        o_tok = both[:, 7680:8704].rearrange("p (b n) -> p b n", b=2)
        o_sq = both[:, 8704:9216]
        out_tmp = both[:, 9216:10240].rearrange("p (b n) -> p b n", b=2)
        s = both[:, 10240:12800].rearrange("p (t n) -> p t n", t=TILES)
        mixT = both[:, 12800:14848].rearrange("p (b k n) -> p b k n", b=2, k=KT)
        sgu_sq = both[:, 13824:14336]
        fin = both[:, 14336:14848].rearrange("p (h e) -> p h e", h=HEADS)
        ada_rows = both[:, 12800:13824].rearrange("p (b n) -> p b n", b=2)
        h2T = both[:, 14848:15872].rearrange("p (k n) -> p k n", k=KT)
        wsT = both[:, 14848:15360].rearrange("p (g n) -> p g n", g=GROUPS)
        sgu_w = both[:, 15360:15872]
        top_work = both[0:EXPERTS, 10240:10880]
        top_mask = both[0:EXPERTS, 10880:11520]
        top_rank = both[0:EXPERTS, 11520:12160]
        top8 = both[0:EXPERTS, 12160:12168]

        xe = both[:, 0:1536].rearrange("p (e k n) -> p e k n", e=2, k=KT)
        h_rows = both[:, 3584:5120].rearrange("p (r n) -> p r n", r=3)
        h = both[:, 5120:6656].rearrange("p (f n) -> p f n", f=FE // P)
        silu_h = both[:, 6656:7680].rearrange("p (b n) -> p b n", b=2)
        hot_s = both[:, 7680:8192].rearrange("p (t e n) -> p t e n", t=ST, e=2)
        hot_p = both[:, 8192:8224].rearrange("p (e n) -> p e n", e=2)
        gate_s = both[:, 8224:8736].rearrange("p (t e n) -> p t e n", t=ST, e=2)
        gate_p = both[:, 8736:8800].rearrange("p (e n) -> p e n", e=2)
        gT_s = both[:, 8800:9312]
        gT_p = both[:, 9312:9440]
        comb_rk = both[:, 9440:9450].rearrange("p (t e) -> p t e", e=2)
        comb_pr = both[:, 9450:9460].rearrange("p (t e) -> p t e", e=2)
        gate2_0 = both[:, 12800:13312]
        gate2_1 = both[:, 13312:13824]
        y_s = both[:, 13824:14848]
        y_p = both[:, 14848:15360]
        y_half = both[:, 9460:9972]
        final_w = both[:, 0:1024]
        y_out = ring[:, 0:TILES * D].rearrange("p (t d) -> p t d", t=TILES)

        def s_vn(t):
            return both[:, 7680 + 512 * t:8192 + 512 * t]

        psum = ctx.enter_context(nc.psum_tensor("psum", [P, BANKS, 512], F32))

        psum_filled = [sem(f"psum_filled{b}") for b in range(BANKS)]
        psum_stored = [sem(f"psum_stored{b}") for b in range(BANKS)]
        slot_loaded = [sem(f"slot_loaded{s}") for s in range(RING)]
        w2_read = sem("w2_read")
        silu_c_zeroed = sem("silu_c_zeroed")
        xe_zeroed = sem("xe_zeroed")
        mod_summed = sem("mod_summed")
        y_added = sem("y_added")
        ident_loaded = sem("ident_loaded")
        consts_loaded = sem("consts_loaded")
        vecs_loaded = sem("vecs_loaded")
        ws_loaded = sem("ws_loaded")
        x_loaded = [sem(f"x_loaded{t}") for t in range(TILES)]
        pos_loaded = sem("pos_loaded")
        wa_zeroed = sem("wa_zeroed")
        wa_loaded = sem("wa_loaded")
        router_loaded = sem("router_loaded")
        sguw_loaded = sem("sguw_loaded")
        s0_loaded = sem("s0_loaded")
        final_loaded = sem("final_loaded")
        pool_zeroed = sem("pool_zeroed")
        vec_step = sem("vec_step")
        act_step = sem("act_step")
        vec_pair_step = sem("vec_pair_step")
        vec_final_step = sem("vec_final_step")
        silu_c_ready = sem("silu_c_ready")
        x_pos_ready = sem("x_pos_ready")
        x_squared = sem("x_squared")
        x_recip = sem("x_recip")
        x_rs = sem("x_rs")
        xn_ready = sem("xn_ready")
        mod_ready = sem("mod_ready")
        z_ln = sem("z_ln")
        cum_ready = sem("cum_ready")
        rem_ready = sem("rem_ready")
        exp_cum = sem("exp_cum")
        exp_neg = sem("exp_neg")
        exp_rem = sem("exp_rem")
        decay_ready = sem("decay_ready")
        qe_ready = sem("qe_ready")
        kdT_ready = sem("kdT_ready")
        ke_ready = sem("ke_ready")
        ds_stored = sem("ds_stored")
        fin_ready = sem("fin_ready")
        sgu_recip = sem("sgu_recip")
        sgu_rs = sem("sgu_rs")
        sgu_vn_ready = sem("sgu_vn_ready")
        s_ready = sem("s_ready")
        o_recip = sem("o_recip")
        o_rs = sem("o_rs")
        o_ready = sem("o_ready")
        x1_ready = sem("x1_ready")
        x1_squared = sem("x1_squared")
        x1_recip = sem("x1_recip")
        x1_rs = sem("x1_rs")
        xn2_ready = sem("xn2_ready")
        router_amp_ready = sem("router_amp_ready")
        max_ready = sem("max_ready")
        exp_ready = sem("exp_ready")
        probs_ready = sem("probs_ready")
        rank_rows_ready = sem("rank_rows_ready")
        hot_ready = sem("hot_ready")
        y_squared = sem("y_squared")
        y_recip = sem("y_recip")
        y_rs = sem("y_rs")
        y_ready = sem("y_ready")
        y_saved = sem("y_saved")
        state_saved = sem("state_saved")

        def bank(n):
            return psum[:, n % BANKS, :]

        def wait_filled(eng, n, pair=None):
            eng.wait_ge(psum_filled[n % BANKS], n // BANKS + 1 + (0 if pair is None else pair * (PAIR_JOBS // BANKS)))

        def wait_stored(eng, n, pair=None):
            eng.wait_ge(psum_stored[n % BANKS], n // BANKS + 1 + (0 if pair is None else pair * (PAIR_JOBS // BANKS)))

        def wait_bank_free(pe, n, pair=None):
            if n >= BANKS:
                wait_stored(pe, n - BANKS, pair)

        def filled(ins, n):
            ins.then_inc(psum_filled[n % BANKS], 1)

        def stored(ins, n):
            ins.then_inc(psum_stored[n % BANKS], 1)

        def first_gather(*name):
            return JOB[name]

        def next_gather(*name):
            return JOBS_TRUNK + NEXT_GATHER[name]

        def chunk(slot):
            return ring[:, slot * CHUNK_F:(slot + 1) * CHUNK_F]

        def wait_trunk_chunk(pe, n):
            pe.wait_ge(slot_loaded[n % TRUNK_RING], 16 * (n // TRUNK_RING + 1))
            return chunk(n % TRUNK_RING).rearrange("p (k n) -> p k n", k=KT)

        def wait_expert_chunk(pe, m, pair):
            slot = EXPERT_SLOT[m % RING]
            pe.wait_ge(slot_loaded[slot], 16 * (LOADS_BEFORE[slot] + m // RING + 1) + pair * (16 * PAIR_CHUNKS // RING))
            return chunk(slot)

        def wait_trunk_chunk_read(sp, n):
            name, col = TRUNK_CHUNKS[n]
            if name == "ada":
                wait_filled(sp, JOB["adaR", col // 512])
            elif name == "in":
                last = {COL_QK: ("qkP",), COL_V: ("v", TILES - 1), COL_G: ("g", TILES - 1),
                        COL_U: ("u", TILES - 1), COL_SV: ("sv", TILES - 1)}[col]
                wait_filled(sp, JOB[last])
            else:
                wait_filled(sp, JOB["out", TILES - 1, col // 512])

        def wait_expert_chunk_read(sp, m, pair):
            back, m = (1, m + PAIR_CHUNKS) if m < 0 else (0, m)
            e, i = divmod(m, 12)
            when = pair - back
            if i < 8:
                which, f4 = EXPERT_CHUNKS[i]
                wait_filled(sp, JOBS_TRUNK + (R1, R3)[which](e, LAST_ROUND[f4]), when)
            elif i < 11:
                sp.wait_ge(w2_read, 3 * e + i - 7 + when * 6)
            else:
                wait_filled(sp, JOBS_TRUNK + Y(e, 1), when)

        sample_x = x_sample.rearrange("b (t p) d -> p (b t) d", p=P)
        prompt_x = x_prompt.rearrange("b p d -> p (b d)")
        ada_k = ada_w[0].rearrange("(k p) n -> p k n", p=P)
        in_k = w_in[0].rearrange("(k p) n -> p k n", p=P)
        out_k = w_out[0].rearrange("(k p) n -> p k n", p=P)

        vec_sources = [(V_C, c.rearrange("a (k n) -> (a k) n", n=P)), (V_CCTX, c_ctx.rearrange("(k n) -> k n", n=P)),
                       (V_ADAB, ada_b.rearrange("a (k n) -> (a k) n", n=P)), (V_N1, norm1_w.rearrange("a (k n) -> (a k) n", n=P)),
                       (V_N2, norm2_w.rearrange("a (k n) -> (a k) n", n=P)), (V_BS, sgu_bs[0]), (V_GLAW, gla_norm_w),
                       (V_BA, ba_f.rearrange("a (h n) -> (a h) n", n=DK))]

        block = ctx.enter_context(nc.Block())

        @block.sync
        def _(sp):
            sp.dma_start(ident, table[:, 0:P]).then_inc(ident_loaded, 16)
            for row, src in vec_sources[:4]:
                sp.dma_start(vec_rows[row:row + src.shape[0], 0:src.shape[1]], src).then_inc(vecs_loaded, 16)
            for n, (name, col) in enumerate(TRUNK_CHUNKS):
                if n >= TRUNK_RING:
                    wait_trunk_chunk_read(sp, n - TRUNK_RING)
                src = {"ada": ada_k, "in": in_k, "out": out_k}[name][:, :, col:col + 512]
                sp.dma_start(chunk(n % TRUNK_RING).rearrange("p (k n) -> p k n", k=KT), src)\
                    .then_inc(slot_loaded[n % TRUNK_RING], 16)
                if n == 0:
                    for t in range(ST):
                        sp.dma_start(x[:, t, :], sample_x[:, t, :]).then_inc(x_loaded[t], 16)
                    sp.dma_start(x[:, ST, :], prompt_x).then_inc(x_loaded[ST], 16)
                if n == 4:
                    sp.dma_start(consts[:, P:], table[:, P:]).then_inc(consts_loaded, 16)
                if n == 11:
                    sp.wait_ge(qe_ready, 1)
                    sp.wait_ge(ke_ready, 1)
                    sp.dma_start(states[0:DK, 0, :, :], s0_f[0, 0].rearrange("h d e -> d h e"))\
                        .then_inc(s0_loaded, 16)
                    sp.dma_start(states[DK:P, SCH - 1, :, :], s0_b[0, 0].rearrange("h d e -> d h e"))\
                        .then_inc(s0_loaded, 16)
                if n == 16:
                    sp.wait_ge(fin_ready, 1)
                    sp.dma_start(new_f[0, 0].rearrange("h d e -> d h e"), fin[0:DK, :, :]).then_inc(state_saved, 16)
                    sp.dma_start(new_b[0, 0].rearrange("h d e -> d h e"), fin[DK:P, :, :]).then_inc(state_saved, 16)

            def load_expert_chunk(m, pair):
                e, i = divmod(m, 12)
                slot = EXPERT_SLOT[m % RING]
                expert = 2 * pair + e
                if i < 8:
                    which, f4 = EXPERT_CHUNKS[i]
                    src = (w1, w3)[which][0, bass.ds(expert, 1)].rearrange("a (k p) n -> p (a k) n", p=P)[:, :, f4 * 512:f4 * 512 + 512]
                    dst = chunk(slot).rearrange("p (k n) -> p k n", k=KT)
                else:
                    src = w2[0, bass.ds(expert, 1)].rearrange("a (k p) n -> p (a k) n", p=P)[:, (i - 8) * 4:(i - 8) * 4 + 4, :]
                    dst = chunk(slot).rearrange("p (k n) -> p k n", k=4)
                sp.dma_start(dst, src).then_inc(slot_loaded[slot], 16)

            wait_filled(sp, JOB["mT", TILES - 1, 1])
            sp.wait_ge(o_ready, TILES)
            for m in range(RING):
                if m >= 3:
                    wait_trunk_chunk_read(sp, {3: 16, 4: 17, 5: 18}[m])
                load_expert_chunk(m, 0)
            for m in range(RING, PAIR_CHUNKS):
                wait_expert_chunk_read(sp, m - RING, 0)
                load_expert_chunk(m, 0)
            with sp.Fori(1, PAIRS) as pair:
                for m in range(PAIR_CHUNKS):
                    wait_expert_chunk_read(sp, m - RING, pair)
                    load_expert_chunk(m, pair)

            for i, t in enumerate(COMB_ORDER):
                sp.wait_ge(y_ready, i + 1)
                dst = (y_sample.rearrange("b (t p) d -> p (b t) d", p=P)[:, t, :] if t < ST
                       else y_prompt.rearrange("b p d -> p (b d)"))
                sp.dma_start(dst, y_out[:, t, :]).then_inc(y_saved, 16)
            sp.wait_ge(y_saved, 16 * TILES)
            sp.wait_ge(state_saved, 32)

        @block.gpsimd
        def _(pool):
            nc.gpsimd.memset(silu_c, 0.0).then_inc(silu_c_zeroed, 1)
            rows = pos_row.rearrange("(t h) n -> h t n", h=2)
            for half in range(2):
                pool.dma_start(pos_r[64 * half:64 * half + 64, :, :], rows[half:half + 1].to_broadcast([64, ST, 512]))\
                    .then_inc(pos_loaded, 16)
            pool.dma_start(pos_c, pos_col).then_inc(pos_loaded, 16)
            nc.gpsimd.memset(a_up, 0.0).then_inc(wa_zeroed, 1)
            nc.gpsimd.memset(att, 0.0).then_inc(pool_zeroed, 1)
            pool.wait_ge(wa_zeroed, 1)
            for gr in range(4):
                lo = gr * PART
                pool.dma_start(a_up[lo:lo + LOWRANK, :, 0:DK], wa2_f[0].rearrange("r (h n) -> r h n", n=DK)).then_inc(wa_loaded, 16)
                pool.dma_start(a_up[lo + LOWRANK:lo + 2 * LOWRANK, :, DK:P], wa2_b[0].rearrange("r (h n) -> r h n", n=DK))\
                    .then_inc(wa_loaded, 16)
            pool.dma_start(w_a, in_k[:, :, COL_A:COL_A + 2 * LOWRANK]).then_inc(wa_loaded, 16)
            pool.dma_start(router, router_w[0].rearrange("(k p) e -> p k e", p=P)).then_inc(router_loaded, 16)
            pool.dma_start(sgu_w, sgu_norm_w.to_broadcast([P, 512])).then_inc(sguw_loaded, 16)
            wait_filled(pool, JOB["rank",])
            nc.gpsimd.memset(xe[:, :, :, SLOTS:PADDED], 0.0).then_inc(xe_zeroed, 1)
            wait_filled(pool, JOBS_TRUNK + R3(1, 2) + PAIR_JOBS * (PAIRS - 1))
            pool.dma_start(final_w, final_norm_w.rearrange("(a n) -> a n", a=1).to_broadcast([P, D])).then_inc(final_loaded, 16)

        @block.tensor
        def _(pe):
            def ada_product(c5):
                w = wait_trunk_chunk(pe, CHUNK_OF["ada", 512 * c5])
                n = JOB["adaR", c5]
                wait_bank_free(pe, n)
                for i in range(2):
                    for gr in range(4):
                        kt = 4 * i + gr
                        mm = nc.tensor.matmul(bank(n)[gr * PART:(gr + 1) * PART, :], silu_c[:, kt, :], w[:, kt, :],
                                              start=(i == 0), stop=(i == 1))
                filled(mm, n)

            def ada_turn(c5):
                wait_stored(pe, JOB["adaR", c5])
                n = JOB["adaT", c5]
                wait_bank_free(pe, n)
                for j in range(4):
                    mm = nc.tensor.transpose(bank(n)[:, j * P:(j + 1) * P], ada_rows[:, c5 % 2, j * P:(j + 1) * P], ident)
                filled(mm, n)

            def project(name, col):
                w = wait_trunk_chunk(pe, CHUNK_OF["in", col])
                for t in range(TILES):
                    n = JOB[name, t]
                    wait_bank_free(pe, n)
                    for kt in range(KT):
                        mm = nc.tensor.matmul(bank(n), hT[:, kt, t * P:(t + 1) * P], w[:, kt, :],
                                              start=(kt == 0), stop=(kt == KT - 1))
                    filled(mm, n)

            pe.wait_ge(ident_loaded, 16)
            pe.wait_ge(vecs_loaded, 16 * 9)
            n = JOB["vec",]
            filled(nc.tensor.transpose(bank(n)[:, 0:V_ROWS], vec_rows[0:V_ROWS, :], ident[0:V_ROWS, 0:V_ROWS]), n)
            pe.wait_ge(ws_loaded, 16)
            n = JOB["wsT",]
            for gr in range(GROUPS):
                mm = nc.tensor.transpose(bank(n)[:, gr * P:(gr + 1) * P], ws[:, gr, :], ident)
            filled(mm, n)
            pe.wait_ge(silu_c_ready, 1)
            ada_product(0)
            ada_product(1)
            ada_turn(0)
            ada_product(2)
            ada_turn(1)

            def turn_x(first, end):
                for kt in range(first, end):
                    n = JOB["xT", kt]
                    wait_bank_free(pe, n)
                    for t in range(ST):
                        mm = nc.tensor.transpose(bank(n)[:, t * P:(t + 1) * P], xn[:, t, kt * P:(kt + 1) * P], ident)
                    filled(mm, n)

            pe.wait_ge(xn_ready, TILES)
            turn_x(0, XT_AHEAD)
            ada_product(3)
            ada_turn(2)
            ada_turn(3)
            turn_x(XT_AHEAD, KT)
            for half in range(2):
                n = JOB["xTp", half]
                wait_bank_free(pe, n)
                for j in range(4):
                    kt = 4 * half + j
                    mm = nc.tensor.transpose(bank(n)[:, j * P:(j + 1) * P], xn[:, ST, kt * P:(kt + 1) * P], ident)
                filled(mm, n)
            for kt in range(KT):
                wait_stored(pe, JOB["xT", kt])
            for half in range(2):
                wait_stored(pe, JOB["xTp", half])
            w = wait_trunk_chunk(pe, CHUNK_OF["in", COL_QK])
            nP = JOB["qkP",]
            wait_bank_free(pe, nP)
            for m in range(4):
                n = JOB["qkS", m]
                wait_bank_free(pe, n)
                for kt in range(KT):
                    mm = nc.tensor.matmul(bank(n), w[:, kt, m * P:(m + 1) * P], hT[:, kt, 0:SAMPLE],
                                          start=(kt == 0), stop=(kt == KT - 1))
                    mp = nc.tensor.matmul(bank(nP)[:, m * P:(m + 1) * P], w[:, kt, m * P:(m + 1) * P], hT[:, kt, SAMPLE:TOK],
                                          start=(kt == 0), stop=(kt == KT - 1))
                filled(mm, n)
            filled(mp, nP)
            ada_product(4)
            pe.wait_ge(wa_loaded, 16 * 9)
            for name, lo, hi in (("aS", 0, SAMPLE), ("aP", SAMPLE, TOK)):
                n = JOB[name,]
                wait_bank_free(pe, n)
                for i in range(2):
                    for gr in range(4):
                        kt = 4 * i + gr
                        mm = nc.tensor.matmul(bank(n)[gr * PART:(gr + 1) * PART, 0:hi - lo], w_a[:, kt, :], hT[:, kt, lo:hi],
                                              start=(i == 0), stop=(i == 1))
                filled(mm, n)
            wait_stored(pe, JOB["aS",])
            wait_stored(pe, JOB["aP",])
            for hd in range(HEADS):
                n = JOB["zS", hd]
                wait_bank_free(pe, n)
                filled(nc.tensor.matmul(bank(n), a_up[:, hd, :], aT[:, 0:SAMPLE], start=True, stop=True), n)
            n = JOB["zP",]
            wait_bank_free(pe, n)
            for hd in range(HEADS):
                mm = nc.tensor.matmul(bank(n)[:, hd * P:(hd + 1) * P], a_up[:, hd, :], aT[:, SAMPLE:TOK], start=True, stop=True)
            filled(mm, n)
            project("v", COL_V)
            ada_turn(4)
            ada_product(5)
            project("g", COL_G)
            ada_turn(5)
            ada_product(6)
            pe.wait_ge(kdT_ready, 1)
            kdT = rem.rearrange("p (h n) -> p h n", h=HEADS)
            for t in range(TILES):
                n = JOB["kd", t]
                wait_bank_free(pe, n)
                for hd in range(HEADS):
                    mm = nc.tensor.transpose(bank(n)[:, hd * P:(hd + 1) * P], kdT[:, hd, t * P:(t + 1) * P], ident)
                filled(mm, n)
            for t in range(TILES):
                jobs = (JOB["ds", 2 * t], JOB["ds", 2 * t + 1])
                wait_stored(pe, JOB["v", t])
                wait_stored(pe, JOB["kd", t])
                for n in jobs:
                    wait_bank_free(pe, n)
                for hd in range(HEADS):
                    for half, n in enumerate(jobs):
                        rows = slice(half * CH, (half + 1) * CH)
                        mm = nc.tensor.matmul(bank(n)[:, hd * P:(hd + 1) * P], kd[rows, t, hd, :],
                                              v[rows, t, hd * P:(hd + 1) * P], start=True, stop=True)
                        if hd == HEADS - 1:
                            filled(mm, n)
            project("u", COL_U)
            ada_turn(6)
            ada_product(7)
            project("sv", COL_SV)
            ada_turn(7)
            ada_product(8)
            ada_product(9)
            wait_stored(pe, JOB["wsT",])
            for t in range(TILES):
                n = JOB["mix", t]
                pe.wait_ge(sgu_vn_ready, t + 1)
                wait_bank_free(pe, n)
                for gr in range(GROUPS):
                    mm = nc.tensor.matmul(bank(n)[:, gr * P:(gr + 1) * P], wsT[:, gr, :],
                                          s_vn(t)[:, gr * P:(gr + 1) * P], start=True, stop=True)
                filled(mm, n)
            ada_turn(8)
            ada_turn(9)
            ada_product(10)

            def gate_rows(name, gate):
                for qd in range(4):
                    n = JOB[name, qd]
                    wait_bank_free(pe, n)
                    for j in range(4):
                        mm = nc.tensor.matmul(bank(n)[:, j * P:(j + 1) * P],
                                              mod[:, gate + 4 * (qd % 2) + j, qd // 2:qd // 2 + 1].to_broadcast([P, P]), ident,
                                              start=True, stop=True)
                    filled(mm, n)

            def attention(t):
                jobs = (JOB["attF", t], JOB["attB", t])
                for n in jobs:
                    wait_bank_free(pe, n)
                for hd in range(HEADS):
                    for d, n in enumerate(jobs):
                        mm = nc.tensor.matmul(bank(n)[:, hd * P:(hd + 1) * P], k[d * DK:(d + 1) * DK, hd, t * P:(t + 1) * P],
                                              q[d * DK:(d + 1) * DK, hd, t * P:(t + 1) * P], start=True, stop=True)
                        if hd == HEADS - 1:
                            filled(mm, n)

            def gla_out(t):
                n = JOB["o", t]
                wait_bank_free(pe, n)
                wait_stored(pe, JOB["attF", t])
                wait_stored(pe, JOB["attB", t])
                for hd in range(HEADS):
                    o = bank(n)[:, hd * P:(hd + 1) * P]
                    vh = v[:, t, hd * P:(hd + 1) * P]
                    nc.tensor.matmul(o, att[:, t % 2, 0, hd, :], vh, start=True, stop=False, skip_group_check=True)
                    nc.tensor.matmul(o, att[:, t % 2, 1, hd, :], vh, start=False, stop=False, skip_group_check=True)
                    for half in range(2):
                        ck = 2 * t + half
                        mm = nc.tensor.matmul(o[half * CH:(half + 1) * CH, :], q[:, hd, ck * CH:(ck + 1) * CH],
                                              states[:, ck, hd, :], start=False, stop=True, skip_group_check=True)
                filled(mm, n)

            def mix_turn(t):
                pe.wait_ge(o_ready, t + 1)
                pe.wait_ge(s_ready, TILES)
                for half in range(2):
                    n = JOB["mT", t, half]
                    wait_bank_free(pe, n)
                    src = o_tok[:, t % 2, :] if half == 0 else s[:, t, :]
                    for j in range(4):
                        mm = nc.tensor.transpose(bank(n)[:, j * P:(j + 1) * P], src[:, j * P:(j + 1) * P], ident)
                    filled(mm, n)

            def mix_out(t, half):
                wait_stored(pe, JOB["mT", t, 0])
                wait_stored(pe, JOB["mT", t, 1])
                w = wait_trunk_chunk(pe, CHUNK_OF["out", 512 * half])
                n = JOB["out", t, half]
                wait_bank_free(pe, n)
                for kt in range(KT):
                    mm = nc.tensor.matmul(bank(n), mixT[:, t % 2, kt, :], w[:, kt, :], start=(kt == 0), stop=(kt == KT - 1))
                filled(mm, n)

            pe.wait_ge(qe_ready, 1)
            pe.wait_ge(ke_ready, 1)
            pe.wait_ge(fin_ready, 1)

            def route_turn(t):
                pe.wait_ge(xn2_ready, t + 1)
                for half in range(2):
                    n = JOB["hT", t, half]
                    wait_bank_free(pe, n)
                    for j in range(4):
                        kt = 4 * half + j
                        mm = nc.tensor.transpose(bank(n)[:, j * P:(j + 1) * P], xn2[:, t, kt * P:(kt + 1) * P], ident)
                    filled(mm, n)

            def route(t):
                w = 0 if t < ST else 1
                n = JOB["logit", t]
                wait_bank_free(pe, n)
                for kt in range(KT):
                    nc.tensor.matmul(bank(n)[:, 0:EXPERTS], mod[:, SHIFT2 + kt, w:w + 1].to_broadcast([P, P]), router[:, kt, :],
                                     start=(kt == 0), stop=False)
                wait_stored(pe, JOB["hT", t, 0])
                wait_stored(pe, JOB["hT", t, 1])
                for kt in range(KT):
                    mm = nc.tensor.matmul(bank(n)[:, 0:EXPERTS], h2T[:, kt, :], router_amp[:, w, kt, :],
                                          start=False, stop=(kt == KT - 1))
                filled(mm, n)

            for t in range(TILES + 3):
                if t < TILES:
                    attention(t)
                if t == 0:
                    ada_turn(10)
                    ada_product(11)
                if t == 1:
                    ada_turn(11)
                if 1 <= t <= TILES:
                    gla_out(t - 1)
                if t == 1:
                    pe.wait_ge(mod_summed, 6)
                    gate_rows("g1", GATE1)
                if 2 <= t < TILES + 2:
                    mix_out(t - 2, 0)
                if 1 <= t <= TILES:
                    mix_turn(t - 1)
                if t == TILES + 2:
                    pe.wait_ge(mod_summed, 12)
                    gate_rows("g2", GATE2)
                if t >= 3:
                    route_turn(t - 3)
                if 2 <= t < TILES + 2:
                    mix_out(t - 2, 1)
                if t == 3:
                    pe.wait_ge(router_amp_ready, 1)
                if t >= 3:
                    route(t - 3)
            pe.wait_ge(probs_ready, 1)
            n = JOB["pS",]
            wait_bank_free(pe, n)
            for t in range(ST):
                mm = nc.tensor.transpose(bank(n)[0:EXPERTS, t * P:(t + 1) * P], probs[:, t, 0:EXPERTS], ident)
            filled(mm, n)
            n = JOB["pP",]
            wait_bank_free(pe, n)
            filled(nc.tensor.transpose(bank(n)[0:EXPERTS, 0:P], probs[:, ST, 0:EXPERTS], ident), n)
            pe.wait_ge(rank_rows_ready, 1)
            n = JOB["rank",]
            wait_bank_free(pe, n)
            for t in range(TILES):
                mm = nc.tensor.transpose(bank(n)[:, t * EXPERTS:(t + 1) * EXPERTS], top_rank[:, t * P:(t + 1) * P],
                                         ident[0:EXPERTS, 0:EXPERTS])
            filled(mm, n)

            def gather(job, pair=None):
                for i in range(GATHER_S):
                    n = job("S", i)
                    wait_bank_free(pe, n, pair)
                    for j in range(2):
                        kt = 2 * i + j
                        for t in range(ST):
                            mm = nc.tensor.matmul(bank(n)[:, j * P:(j + 1) * P], xn2[:, t, kt * P:(kt + 1) * P], hot_s[:, t, :, :],
                                                  start=(t == 0), stop=(t == ST - 1))
                    filled(mm, n)
                for i in range(GATHER_P):
                    n = job("P", i)
                    wait_bank_free(pe, n, pair)
                    for j in range(4):
                        kt = 4 * i + j
                        mm = nc.tensor.matmul(bank(n)[:, j * 2 * CAP_P:(j + 1) * 2 * CAP_P], xn2[:, ST, kt * P:(kt + 1) * P], hot_p,
                                              start=True, stop=True)
                    filled(mm, n)

                wait_bank_free(pe, job("G_P"), pair)

            def turn_prompt_gates(job, pair=None):
                n = job("G_P")
                filled(nc.tensor.transpose(bank(n)[0:2 * PART, 0:P], gate_p, ident), n)

            def wait_gathered(job, pair=None):
                for i in range(GATHER_S):
                    wait_stored(pe, job("S", i), pair)
                for i in range(GATHER_P):
                    wait_stored(pe, job("P", i), pair)
                wait_stored(pe, job("G_P"), pair)

            pe.wait_ge(hot_ready, 2)
            gather(first_gather)
            pe.wait_ge(hot_ready, 4)
            turn_prompt_gates(first_gather)
            wait_gathered(first_gather)
            pe.wait_ge(xe_zeroed, 1)

            def pair_products(pair, last=False):
                J = JOBS_TRUNK

                def rounds(e, r):
                    for which, job in ((0, R1), (1, R3)):
                        n = J + job(e, r)
                        w = {f4: wait_expert_chunk(pe, 12 * e + EXPERT_CHUNKS.index((which, f4)), pair)
                             .rearrange("p (k n) -> p k n", k=KT) for f4 in sorted({f4 for f4, _, _ in ROUNDS[r]})}
                        wait_bank_free(pe, n, pair)
                        for kt in range(KT):
                            at = 0
                            for f4, part, parts in ROUNDS[r]:
                                width = parts * PART
                                mm = nc.tensor.matmul(bank(n)[at:at + width, :], xe[:, e, kt, part * PART:part * PART + width],
                                                      w[f4][:, kt, :], start=(kt == 0), stop=(kt == KT - 1))
                                at += width
                        filled(mm, n)

                def turn_h(e, r):
                    n = J + T(e, r)
                    wait_bank_free(pe, n, pair)
                    wait_stored(pe, J + R3(e, r), pair)
                    for j in range(4):
                        mm = nc.tensor.transpose(bank(n)[:, j * P:(j + 1) * P], h_rows[:, r, j * P:(j + 1) * P], ident)
                    filled(mm, n)

                def down(e, i):
                    w = wait_expert_chunk(pe, 12 * e + 8 + i, pair).rearrange("p (k n) -> p k n", k=4)
                    n0, n1 = J + Y(e, 0), J + Y(e, 1)
                    for f in range(4):
                        ft = 4 * i + f
                        at = 0
                        for half, part, parts in DOWN_0:
                            width = parts * PART
                            m0 = nc.tensor.matmul(bank(n0)[at:at + width, :], h[:, ft, part * PART:part * PART + width],
                                                  w[:, f, half * 512:(half + 1) * 512], start=(ft == 0), stop=(ft == 15))
                            at += width
                    if i == 3:
                        filled(m0, n0)
                    for f in range(0, 4, 2):
                        for odd in range(2):
                            ft = 4 * i + f + odd
                            m1 = nc.tensor.matmul(bank(n1)[odd * CAP_S:(odd + 1) * CAP_S, :], h[:, ft, 0:CAP_S],
                                                  w[:, f + odd, 512:D], start=(ft < 2), stop=(ft >= 14))
                    if i == 3:
                        filled(m1, n1)
                    else:
                        m1.then_inc(w2_read, 1)

                for e in range(2):
                    rounds(e, 0)
                    rounds(e, 1)
                    turn_h(e, 0)
                    if e == 0:
                        n = J + G_S
                        wait_bank_free(pe, n, pair)
                        for t in range(ST):
                            mm = nc.tensor.transpose(bank(n)[:, t * P:(t + 1) * P], gate_s[:, t, :, :], ident)
                        filled(mm, n)
                    rounds(e, 2)
                    turn_h(e, 1)
                    wait_bank_free(pe, J + Y(e, 0), pair)
                    wait_bank_free(pe, J + Y(e, 1), pair)
                    wait_stored(pe, J + T(e, 0), pair)
                    down(e, 0)
                    turn_h(e, 2)
                    wait_stored(pe, J + T(e, 1), pair)
                    down(e, 1)
                    wait_stored(pe, J + T(e, 2), pair)
                    down(e, 2)
                    down(e, 3)
                if not last:
                    pe.wait_ge(hot_ready, 8 + pair * 4)
                    gather(next_gather, pair)
                wait_stored(pe, J + G_S, pair)
                wait_stored(pe, J + Y(1, 0), pair)
                pe.wait_ge(y_added, 2 + pair * 2)
                for i, t in enumerate(COMB_ORDER):
                    if i == 1 and not last:
                        turn_prompt_gates(next_gather, pair)
                    for half in range(2):
                        n = J + COMB(t, half, last)
                        cols = slice(half * 512, (half + 1) * 512)
                        wait_bank_free(pe, n, pair)
                        if t < ST:
                            mm = nc.tensor.matmul(bank(n), gT_s[:, t * P:(t + 1) * P], y_s[:, cols], start=True, stop=True)
                        else:
                            rows = slice(half * 2 * PART, (half + 1) * 2 * PART)
                            mm = nc.tensor.matmul(bank(n), gT_p[rows], y_p[rows], start=True, stop=True)
                        filled(mm, n)
                if not last:
                    wait_gathered(next_gather, pair)

            with pe.Fori(0, PAIRS - 1) as pair:
                pair_products(pair)
            pair_products(PAIRS - 1, last=True)

        @block.scalar
        def _(act):
            steps = [0]

            def link(ins):
                steps[0] += 1
                ins.then_inc(act_step, 1)
                act.wait_ge(act_step, steps[0])

            for row, src in vec_sources[4:]:
                act.dma_start(vec_rows[row:row + src.shape[0], 0:src.shape[1]], src).then_inc(vecs_loaded, 16)
            act.dma_start(vec_rows[V_BA:V_BA + HEADS, DK:P], ba_b.rearrange("a (h n) -> (a h) n", n=DK)).then_inc(vecs_loaded, 16)
            act.dma_start(ws, sgu_ws[0].rearrange("g p q -> p g q")).then_inc(ws_loaded, 16)
            wait_stored(act, JOB["vec",])
            act.wait_ge(silu_c_zeroed, 1)
            nc.scalar.activation(silu_c[:, :, 0:2], vecs[:, V_C:V_C + 16].rearrange("p (w k) -> p k w", w=2), ACT.Silu).then_inc(silu_c_ready, 1)
            n = JOB["wsT",]
            wait_filled(act, n)
            stored(nc.scalar.copy(wsT, bank(n).rearrange("p (g n) -> p g n", g=GROUPS)), n)

            def store_ada_rows(first, end):
                for c5 in range(first, end):
                    n = JOB["adaR", c5]
                    wait_filled(act, n)
                    if c5 >= 2:
                        wait_filled(act, JOB["adaT", c5 - 2])
                    stored(nc.scalar.copy(ada_rows[:, c5 % 2, :], bank(n)), n)

            store_ada_rows(0, 1)
            for t in range(TILES):
                if t < ST:
                    act.wait_ge(x_pos_ready, t + 1)
                else:
                    act.wait_ge(x_loaded[ST], 16)
                nc.scalar.activation(xn[:, t, :], x[:, t, :], ACT.Square, accum_out=stats[:, t:t + 1]).then_inc(x_squared, 1)
            act.wait_ge(x_recip, 1)
            nc.scalar.activation(stats[:, 10:15], stats[:, 5:10], ACT.Sqrt).then_inc(x_rs, 1)
            store_ada_rows(1, 4)
            act.wait_ge(mod_ready, 1)
            for kt in range(0, KT, 2):
                n = JOB["xT", kt]
                wait_filled(act, n)
                stored(nc.scalar.activation(hT[:, kt, 0:SAMPLE], bank(n), ACT.Identity, bias=mod[:, SHIFT1 + kt, 0:1],
                                            scale=amp1[:, kt, 0:1]), n)
            n = JOB["xTp", 0]
            wait_filled(act, n)
            for j in range(4):
                ins = nc.scalar.activation(hT[:, j, SAMPLE:TOK], bank(n)[:, j * P:(j + 1) * P], ACT.Identity,
                                           bias=mod[:, SHIFT1 + j, 1:2], scale=amp1[:, j, 1:2])
            stored(ins, n)
            for m in range(5):
                n = JOB["qkS", m] if m < 4 else JOB["qkP",]
                wait_filled(act, n)
                for mm in ([m] if m < 4 else range(4)):
                    dst, scale = (q, DK ** -0.5) if mm < 2 else (k, 1.0)
                    for hh in range(2):
                        for half in range(2):
                            src = bank(n)[hh * DK:(hh + 1) * DK, :] if m < 4 else bank(n)[hh * DK:(hh + 1) * DK, mm * P:(mm + 1) * P]
                            hd = 2 * (mm % 2) + hh
                            lo, hi = (0, SAMPLE) if m < 4 else (SAMPLE, TOK)
                            ins = nc.scalar.activation(dst[half * DK:(half + 1) * DK, hd, lo:hi], src, ACT.Copy, scale=scale)
                stored(ins, n)
            store_ada_rows(4, 5)
            wait_stored(act, JOB["zP",])
            link(nc.scalar.activation(rem, z, ACT.Abs))
            link(nc.scalar.activation(rem, rem, ACT.Exp, scale=-1.0))
            nc.scalar.activation(rem, rem, ACT.Ln, bias=1.0).then_inc(z_ln, 1)

            def store_v(t):
                n = JOB["v", t]
                wait_filled(act, n)
                stored(nc.scalar.copy(v[:, t, :], bank(n)), n)

            for t in range(TILES):
                store_v(t)
            store_ada_rows(5, 6)
            act.wait_ge(cum_ready, 1)
            nc.scalar.activation(z, cum, ACT.Exp, scale=1.0 / GATE_NORM).then_inc(exp_cum, 1)
            act.wait_ge(rem_ready, 1)
            nc.scalar.activation(rem, rem, ACT.Exp, scale=1.0 / GATE_NORM).then_inc(exp_rem, 1)
            act.wait_ge(exp_cum, 1)
            nc.scalar.activation(cum, cum, ACT.Exp, scale=-1.0 / GATE_NORM).then_inc(exp_neg, 1)
            nc.scalar.activation(chunk_decay, stats[:, 40:80].rearrange("p (h n) -> p h n", h=HEADS), ACT.Exp,
                                 scale=1.0 / GATE_NORM).then_inc(decay_ready, 1)
            for t in range(TILES):
                n = JOB["g", t]
                wait_filled(act, n)
                stored(nc.scalar.activation(g[:, t, :], bank(n), ACT.Silu), n)
            store_ada_rows(6, 7)
            for t in range(TILES):
                n = JOB["kd", t]
                wait_filled(act, n)
                stored(nc.scalar.copy(kd[:, t, :, :], bank(n).rearrange("p (h n) -> p h n", h=HEADS)), n)
            act.wait_ge(qe_ready, 1)
            act.wait_ge(ke_ready, 1)
            for ck in range(CHUNKS):
                n = JOB["ds", ck]
                wait_filled(act, n)
                src = bank(n).rearrange("p (h e) -> p h e", h=HEADS)
                if ck < SCH:
                    moves = [(slice(0, DK), ck + 1)] * (ck + 1 < SCH) + [(slice(DK, P), ck - 1)] * (ck > 0)
                    dsts = [(rows, states[rows, to, :, :]) for rows, to in moves]
                elif ck == SCH:
                    dsts = [(slice(0, DK), states[0:DK, SCH + 1, :, :]), (slice(DK, P), fin[DK:P, :, :])]
                else:
                    dsts = [(slice(0, DK), fin[0:DK, :, :]), (slice(DK, P), states[DK:P, SCH, :, :])]
                for rows, dst in dsts:
                    ins = nc.scalar.copy(dst, src[rows])
                stored(ins, n)
            for t in range(TILES):
                n = JOB["u", t]
                wait_filled(act, n)
                stored(nc.scalar.activation(s[:, t, :], bank(n), ACT.Gelu_apprx_tanh), n)
            store_ada_rows(7, 8)
            for t in range(TILES):
                n = JOB["sv", t]
                wait_filled(act, n)
                stored(nc.scalar.activation(s_vn(t), bank(n), ACT.Gelu_apprx_tanh), n)
                act.wait_ge(sgu_recip, t + 1)
                nc.scalar.activation(stats[:, 84:88], stats[:, 80:84], ACT.Sqrt).then_inc(sgu_rs, 1)
            store_ada_rows(8, 12)

            def mix_store(t):
                n = JOB["mT", t, 0]
                wait_filled(act, n)
                if t == 1:
                    act.wait_ge(state_saved, 32)
                if t >= 2:
                    wait_filled(act, JOB["out", t - 2, 1])
                stored(nc.scalar.activation(mixT[:, t % 2, 0:4, :], bank(n).rearrange("p (k n) -> p k n", k=4), ACT.Identity,
                                            bias=0.0, scale=vecs[:, V_GLAW:V_GLAW + 1]), n)
                n = JOB["mT", t, 1]
                wait_filled(act, n)
                stored(nc.scalar.copy(mixT[:, t % 2, 4:8, :], bank(n).rearrange("p (k n) -> p k n", k=4)), n)

            def norm2(t):
                act.wait_ge(x1_ready, t + 1)
                nc.scalar.activation(xn2[:, t, :], x[:, t, :], ACT.Square, accum_out=stats[:, 96:97]).then_inc(x1_squared, 1)
                act.wait_ge(x1_recip, t + 1)
                nc.scalar.activation(stats[:, 98:99], stats[:, 97:98], ACT.Sqrt).then_inc(x1_rs, 1)

            for t in range(TILES + 3):
                if 1 <= t <= TILES:
                    n = JOB["o", t - 1]
                    wait_filled(act, n)
                    if t - 1 >= 2:
                        wait_filled(act, JOB["mT", t - 3, 0])
                    stored(nc.scalar.copy(o_tok[:, (t - 1) % 2, :], bank(n)), n)
                    act.wait_ge(o_recip, t)
                    nc.scalar.activation(stats[:, 108:112], stats[:, 104:108], ACT.Sqrt).then_inc(o_rs, 1)
                    if t == 1:
                        for qd in range(4):
                            n = JOB["g1", qd]
                            wait_filled(act, n)
                            stored(nc.scalar.copy(gate1_rows[:, qd // 2, (qd % 2) * 512:(qd % 2) * 512 + 512], bank(n)), n)
                    mix_store(t - 1)
                if t == TILES + 2:
                    for qd, dst, rows in ((0, gate2_0, slice(0, CAP_S)), (1, gate2_1, slice(0, P)),
                                          (2, gate2_0, slice(CAP_S, CAP_S + PART)), (3, gate2_0, slice(CAP_S + PART, P))):
                        n = JOB["g2", qd]
                        wait_filled(act, n)
                        stored(nc.scalar.copy(dst[rows], bank(n)[rows]), n)
                if t >= 3:
                    n = JOB["hT", t - 3, 0]
                    wait_filled(act, n)
                    if t > 3:
                        wait_filled(act, JOB["logit", t - 4])
                    stored(nc.scalar.copy(h2T[:, 0:4, :], bank(n).rearrange("p (k n) -> p k n", k=4)), n)
                if 2 <= t < TILES + 2:
                    norm2(t - 2)
            act.wait_ge(max_ready, 1)
            nc.scalar.activation(logits, logits, ACT.Exp).then_inc(exp_ready, 1)

            def pair_work(pair, last=False):
                J = JOBS_TRUNK

                def store_h(e, r):
                    n = J + T(e, r)
                    wait_filled(act, n, pair)
                    src = bank(n).rearrange("p (j n) -> p j n", j=4)
                    moves = [[(0, 0, 0, PADDED), (PADDED, 1, 2 * PART, PART)],
                             [(0, 1, 0, 2 * PART), (2 * PART, 2, 0, 2 * PART)],
                             [(0, 3, 0, PADDED), (PADDED, 2, 2 * PART, PART)]][r]
                    for lo, f4, to, width in moves:
                        ins = nc.scalar.copy(h[:, 4 * f4:4 * f4 + 4, to:to + width], src[:, :, lo:lo + width])
                    stored(ins, n)

                def silu(e, r):
                    i = 3 * e + r
                    n = J + R1(e, r)
                    wait_filled(act, n, pair)
                    if i >= 2:
                        wait_stored(act, J + R3((i - 2) // 3, (i - 2) % 3), pair)
                    stored(nc.scalar.activation(silu_h[:, i % 2, :], bank(n), ACT.Silu), n)

                for e in range(2):
                    silu(e, 0)
                    silu(e, 1)
                    store_h(e, 0)
                    if e == 0:
                        n = J + G_S
                        wait_filled(act, n, pair)
                        stored(nc.scalar.copy(gT_s, bank(n)), n)
                    silu(e, 2)
                    store_h(e, 1)
                    store_h(e, 2)

            with act.Fori(0, PAIRS - 1) as pair:
                pair_work(pair)
            pair_work(PAIRS - 1, last=True)
            for i, t in enumerate(COMB_ORDER):
                wait_stored(act, JOBS_TRUNK + PAIR_JOBS * (PAIRS - 1) + COMB(t, 1, True))
                nc.scalar.activation(y_out[:, t, :], x[:, t, :], ACT.Square, accum_out=stats[:, 130 + i:131 + i]).then_inc(y_squared, 1)
                if i == TILES - 2:
                    act.wait_ge(y_recip, 1)
                    nc.scalar.activation(stats[:, 140:140 + TILES - 1], stats[:, 135:135 + TILES - 1], ACT.Sqrt).then_inc(y_rs, 1)
            act.wait_ge(y_recip, 2)
            nc.scalar.activation(stats[:, 139 + TILES:140 + TILES], stats[:, 134 + TILES:135 + TILES], ACT.Sqrt).then_inc(y_rs, 1)

        @block.vector
        def _(dve):
            steps = [0]

            def link(ins):
                steps[0] += 1
                ins.then_inc(vec_step, 1)
                dve.wait_ge(vec_step, steps[0])

            def mean_recip(out, sums, width, then, own=link):
                own(nc.vector.tensor_scalar(out, sums, 1.0 / width, EPS, ALU.mult, ALU.add))
                nc.vector.reciprocal(out, out).then_inc(then, 1)

            n = JOB["vec",]
            wait_filled(dve, n)
            stored(nc.vector.tensor_copy(vecs[:, 0:V_ROWS], bank(n)[:, 0:V_ROWS]), n)
            dve.wait_ge(pos_loaded, 48)
            for t in range(ST):
                dve.wait_ge(x_loaded[t], 16)
                nc.vector.tensor_tensor(x[:, t, 0:512], x[:, t, 0:512], pos_r[:, t, :], ALU.add)
                nc.vector.tensor_tensor(x[:, t, 512:D], x[:, t, 512:D], pos_c, ALU.add).then_inc(x_pos_ready, 1)
            dve.wait_ge(x_pos_ready, ST)
            dve.wait_ge(x_loaded[ST], 16)
            dve.wait_ge(x_squared, TILES)
            mean_recip(stats[:, 5:10], stats[:, 0:5], D, x_recip)
            dve.wait_ge(x_rs, 1)
            for t in range(TILES):
                nc.vector.tensor_scalar(xn[:, t, :], x[:, t, :], stats[:, 10 + t:11 + t], None, ALU.mult).then_inc(xn_ready, 1)

            def store_mod(first, end):
                for c5 in range(first, end):
                    n = JOB["adaT", c5]
                    wait_filled(dve, n)
                    dst = mod[:, 4 * c5:4 * c5 + 4, :]
                    quarters = bank(n).rearrange("p (j q c) -> p j c q", j=4, q=4)[:, :, 0:2, :]
                    stored(nc.vector.tensor_reduce(dst, quarters, AX_X, ALU.add), n)
                    wait_stored(dve, n)
                    nc.vector.tensor_tensor(dst, dst, vecs[:, V_ADAB + 4 * c5:V_ADAB + 4 * c5 + 4, None].to_broadcast([P, 4, 2]),
                                            ALU.add).then_inc(mod_summed, 1)
                dve.wait_ge(mod_summed, end)

            store_mod(0, 4)
            nc.vector.scalar_tensor_tensor(amp1, mod[:, SCALE1:SCALE1 + KT, :], 1.0,
                                           vecs[:, V_N1:V_N1 + KT, None].to_broadcast([P, KT, 2]), ALU.add, ALU.mult)\
                .then_inc(mod_ready, 1)
            dve.wait_ge(mod_ready, 1)
            for kt in range(1, KT, 2):
                n = JOB["xT", kt]
                wait_filled(dve, n)
                stored(nc.vector.tensor_scalar(hT[:, kt, 0:SAMPLE], bank(n), amp1[:, kt, 0:1], mod[:, SHIFT1 + kt, 0:1],
                                               ALU.mult, ALU.add), n)
            n = JOB["xTp", 1]
            wait_filled(dve, n)
            for j in range(4):
                ins = nc.vector.tensor_scalar(hT[:, 4 + j, SAMPLE:TOK], bank(n)[:, j * P:(j + 1) * P], amp1[:, 4 + j, 1:2],
                                              mod[:, SHIFT1 + 4 + j, 1:2], ALU.mult, ALU.add)
            stored(ins, n)
            for name, lo, hi in (("aS", 0, SAMPLE), ("aP", SAMPLE, TOK)):
                n = JOB[name,]
                wait_filled(dve, n)
                stored(nc.vector.tensor_copy(aT[:, lo:hi], bank(n)[:, 0:hi - lo]), n)
            z3 = z.rearrange("p (h n) -> p h n", h=HEADS)
            cum3 = cum.rearrange("p (h n) -> p h n", h=HEADS)
            for hd in range(HEADS):
                n = JOB["zS", hd]
                wait_filled(dve, n)
                stored(nc.vector.tensor_scalar(z3[:, hd, 0:SAMPLE], bank(n), vecs[:, V_BA + hd:V_BA + hd + 1], None, ALU.add), n)
            n = JOB["zP",]
            wait_filled(dve, n)
            for hd in range(HEADS):
                ins = nc.vector.tensor_scalar(z3[:, hd, SAMPLE:TOK], bank(n)[:, hd * P:(hd + 1) * P],
                                              vecs[:, V_BA + hd:V_BA + hd + 1], None, ALU.add)
            stored(ins, n)
            dve.wait_ge(consts_loaded, 16)
            dve.wait_ge(z_ln, 1)
            link(nc.vector.scalar_tensor_tensor(z, z, 0.0, rem, ALU.min, ALU.subtract))
            for hd in range(HEADS):
                ins = nc.vector.tensor_tensor_scan(cum3[:, hd, :], keep, z3[:, hd, :], 0.0, ALU.mult, ALU.add)
            link(ins)
            cum4 = cum.rearrange("p (m n) -> p m n", n=CH)
            z4 = z.rearrange("p (m n) -> p m n", n=CH)
            rem4 = rem.rearrange("p (m n) -> p m n", n=CH)
            total = stats[:, 40:80]
            link(nc.vector.tensor_copy(total, cum4[:, :, CH - 1]))
            tot_b = stats[:, 40:80, None].to_broadcast([P, HEADS * CHUNKS, CH])
            link(nc.vector.tensor_tensor(cum4[DK:P], tot_b[DK:P], cum4[DK:P], ALU.subtract))
            nc.vector.tensor_tensor(cum4[DK:P], cum4[DK:P], z4[DK:P], ALU.add).then_inc(cum_ready, 1)
            dve.wait_ge(cum_ready, 1)
            nc.vector.tensor_tensor(rem4, tot_b, cum4, ALU.subtract).then_inc(rem_ready, 1)
            q2 = q.rearrange("p h n -> p (h n)")
            k2 = k.rearrange("p h n -> p (h n)")
            wait_stored(dve, JOB["qkP",])
            dve.wait_ge(exp_cum, 1)
            nc.vector.tensor_tensor(q2, q2, z, ALU.mult).then_inc(qe_ready, 1)
            dve.wait_ge(exp_rem, 1)
            nc.vector.tensor_tensor(rem, k2, rem, ALU.mult).then_inc(kdT_ready, 1)
            dve.wait_ge(exp_neg, 1)
            dve.wait_ge(kdT_ready, 1)
            nc.vector.tensor_tensor(k2, k2, cum, ALU.mult).then_inc(ke_ready, 1)
            store_mod(4, 6)
            dve.wait_ge(qe_ready, 1)
            dve.wait_ge(ke_ready, 1)
            link(nc.vector.memset(states[0:DK, SCH, :, :], 0.0))
            link(nc.vector.memset(states[DK:P, SCH + 1, :, :], 0.0))
            dve.wait_ge(s0_loaded, 32)
            dve.wait_ge(decay_ready, 1)
            for ck in range(CHUNKS):
                wait_stored(dve, JOB["ds", ck])

            def advance(rows, dst, src, ck):
                for hd in range(HEADS):
                    ins = nc.vector.scalar_tensor_tensor(dst[rows, hd, :], src[rows, hd, :], chunk_decay[rows, hd, ck:ck + 1],
                                                         dst[rows, hd, :], ALU.mult, ALU.add)
                return ins

            lower, upper = slice(0, DK), slice(DK, P)
            for i in range(SCH - 1):
                advance(lower, states[:, i + 1], states[:, i], i)
                link(advance(upper, states[:, SCH - 2 - i], states[:, SCH - 1 - i], SCH - 1 - i))
            advance(lower, fin, states[:, SCH + 1], SCH + 1)
            advance(upper, fin, states[:, SCH], SCH).then_inc(fin_ready, 1)
            store_mod(6, 7)
            for t in range(TILES):
                wait_stored(dve, JOB["sv", t])
                sv = s_vn(t)
                link(nc.vector.tensor_tensor(sgu_sq, sv, sv, ALU.mult))
                link(nc.vector.tensor_reduce(stats[:, 80:84], sgu_sq.rearrange("p (g n) -> p g n", g=GROUPS), AX_X, ALU.add))
                mean_recip(stats[:, 80:84], stats[:, 80:84], P, sgu_recip)
                dve.wait_ge(sgu_rs, t + 1)
                sv3 = sv.rearrange("p (g n) -> p g n", g=GROUPS)
                nc.vector.tensor_tensor(sv3, sv3, stats[:, 84:88, None].to_broadcast([P, GROUPS, P]), ALU.mult)\
                    .then_inc(sgu_vn_ready, 1)
            store_mod(7, 8)
            dve.wait_ge(sguw_loaded, 16)
            for t in range(TILES):
                n = JOB["mix", t]
                wait_filled(dve, n)
                stored(nc.vector.tensor_tensor(sgu_sq, bank(n), sgu_w, ALU.mult), n)
                wait_stored(dve, n)
                for gr in range(GROUPS):
                    cols = slice(gr * P, (gr + 1) * P)
                    ins = nc.vector.scalar_tensor_tensor(s[:, t, cols], sgu_sq[:, cols], vecs[:, V_BS + gr:V_BS + gr + 1],
                                                         s[:, t, cols], ALU.add, ALU.mult)
                ins.then_inc(s_ready, 1)
                dve.wait_ge(s_ready, t + 1)
            store_mod(8, 10)

            def mask(t):
                for d, name, m in ((0, "attF", mask_f), (1, "attB", mask_b)):
                    n = JOB[name, t]
                    wait_filled(dve, n)
                    if t >= 2:
                        wait_filled(dve, JOB["o", t - 2])
                    stored(nc.vector.copy_predicated(att[:, t % 2, d, :, :], m[:, None, :].to_broadcast([P, HEADS, P]),
                                                     bank(n).rearrange("p (h n) -> p h n", h=HEADS)), n)

            def head_norm(t):
                ot = o_tok[:, t % 2, :]
                wait_stored(dve, JOB["o", t])
                link(nc.vector.tensor_tensor(o_sq, ot, ot, ALU.mult))
                link(nc.vector.tensor_reduce(stats[:, 104:108], o_sq.rearrange("p (g n) -> p g n", g=HEADS), AX_X, ALU.add))
                mean_recip(stats[:, 104:108], stats[:, 104:108], DV, o_recip)
                dve.wait_ge(o_rs, t + 1)
                o3 = ot.rearrange("p (g n) -> p g n", g=HEADS)
                link(nc.vector.tensor_tensor(o3, o3, stats[:, 108:112, None].to_broadcast([P, HEADS, P]), ALU.mult))
                nc.vector.tensor_tensor(ot, ot, g[:, t, :], ALU.mult).then_inc(o_ready, 1)

            def second_amps():
                link(nc.vector.scalar_tensor_tensor(amp2, mod[:, SCALE2:SCALE2 + KT, :], 1.0,
                                                    vecs[:, V_N2:V_N2 + KT, None].to_broadcast([P, KT, 2]), ALU.add, ALU.mult))
                dve.wait_ge(router_loaded, 16)
                for w in range(2):
                    ins = nc.vector.tensor_tensor(router_amp[:, w], router, amp2[:, :, w:w + 1].to_broadcast([P, KT, EXPERTS]), ALU.mult)
                ins.then_inc(router_amp_ready, 1)

            def residual(t, half):
                w = 0 if t < ST else 1
                n = JOB["out", t, half]
                cols = slice(half * 512, (half + 1) * 512)
                wait_filled(dve, n)
                stored(nc.vector.tensor_tensor(out_tmp[:, half, :], bank(n), gate1_rows[:, w, cols], ALU.mult), n)
                wait_stored(dve, n)
                ins = nc.vector.tensor_tensor(x[:, t, cols], x[:, t, cols], out_tmp[:, half, :], ALU.add)
                if half == 0:
                    return
                ins.then_inc(x1_ready, 1)
                dve.wait_ge(x1_squared, t + 1)
                mean_recip(stats[:, 97:98], stats[:, 96:97], D, x1_recip)
                dve.wait_ge(x1_rs, t + 1)
                nc.vector.tensor_scalar(xn2[:, t, :], x[:, t, :], stats[:, 98:99], None, ALU.mult).then_inc(xn2_ready, 1)

            dve.wait_ge(pool_zeroed, 1)

            def store_route(t):
                n = JOB["hT", t, 1]
                wait_filled(dve, n)
                if t > 0:
                    wait_filled(dve, JOB["logit", t - 1])
                stored(nc.vector.tensor_copy(h2T[:, 4:8, :], bank(n).rearrange("p (k n) -> p k n", k=4)), n)

            def store_logits(t):
                n = JOB["logit", t]
                wait_filled(dve, n)
                stored(nc.vector.tensor_copy(logits[:, t, :], bank(n)[:, 0:EXPERTS]), n)

            for t in range(TILES + 3):
                if t < TILES:
                    mask(t)
                if t == 0:
                    store_mod(10, 11)
                if t == 1:
                    store_mod(11, 12)
                    second_amps()
                if 1 <= t <= TILES:
                    head_norm(t - 1)
                if t == 2:
                    for qd in range(4):
                        wait_stored(dve, JOB["g1", qd])
                if 2 <= t < TILES + 2:
                    residual(t - 2, 0)
                if t >= 3:
                    store_route(t - 3)
                if 2 <= t < TILES + 2:
                    residual(t - 2, 1)
                if t >= 3:
                    store_logits(t - 3)
            wait_stored(dve, JOB["logit", TILES - 1])
            link(nc.vector.tensor_reduce(stats[:, 112:117], logits, AX_X, ALU.max))
            nc.vector.tensor_tensor(logits, logits, stats[:, 112:117, None].to_broadcast([P, TILES, EXPERTS]), ALU.subtract)\
                .then_inc(max_ready, 1)
            dve.wait_ge(exp_ready, 1)
            link(nc.vector.tensor_reduce(stats[:, 120:125], logits, AX_X, ALU.add))
            link(nc.vector.reciprocal(stats[:, 125:130], stats[:, 120:125]))
            nc.vector.tensor_tensor(probs[:, :, 0:EXPERTS], logits, stats[:, 125:130, None].to_broadcast([P, TILES, EXPERTS]), ALU.mult)\
                .then_inc(probs_ready, 1)
            for name, lo, hi, rounds in (("pS", 0, SAMPLE, CAP_S // 8), ("pP", SAMPLE, TOK, CAP_P // 8)):
                n = JOB[name,]
                wait_filled(dve, n)
                work = top_work[:, lo:hi]
                stored(nc.vector.tensor_copy(work, bank(n)[0:EXPERTS, 0:hi - lo]), n)
                wait_stored(dve, n)
                for _ in range(rounds):
                    link(nc.vector.max(top8, work))
                    link(nc.vector.match_replace(out=work, in_to_replace=top8, in_values=work, imm_value=-1.0))
                link(nc.vector.tensor_scalar(top_mask[:, lo:hi], work, 0.0, None, ALU.is_lt))
            link(nc.vector.memset(top_work, 1.0))
            link(nc.vector.tensor_tensor_scan(top_rank[:, 0:SAMPLE], top_work[:, 0:SAMPLE], top_mask[:, 0:SAMPLE], 0.0, ALU.mult, ALU.add))
            link(nc.vector.tensor_tensor_scan(top_rank[:, SAMPLE:TOK], top_work[:, SAMPLE:TOK], top_mask[:, SAMPLE:TOK], 0.0, ALU.mult, ALU.add))
            nc.vector.tensor_tensor(top_rank, top_rank, top_mask, ALU.mult).then_inc(rank_rows_ready, 1)
            n = JOB["rank",]
            wait_filled(dve, n)
            stored(nc.vector.tensor_scalar(rank[:, :, 0:EXPERTS], bank(n)[:, 0:TILES * EXPERTS].rearrange("p (t e) -> p t e", t=TILES),
                                           -1.0, None, ALU.add), n)
            wait_stored(dve, n)

            def one_hots(first, own):
                own(nc.vector.tensor_copy(comb_rk, rank[:, :, bass.ds(first, 2)]))
                own(nc.vector.tensor_copy(comb_pr, probs[:, :, bass.ds(first, 2)]))
                hs = hot_s.rearrange("p t e n -> p (t e) n")
                gs = gate_s.rearrange("p t e n -> p (t e) n")
                rk = comb_rk.rearrange("p t e -> p (t e)")
                pr = comb_pr.rearrange("p t e -> p (t e)")
                nc.vector.tensor_tensor(hs, iota[:, None, :].to_broadcast([P, 2 * ST, CAP_S]),
                                        rk[:, 0:2 * ST, None].to_broadcast([P, 2 * ST, CAP_S]), ALU.is_equal).then_inc(hot_ready, 1)
                nc.vector.tensor_tensor(hot_p, iota[:, None, 0:CAP_P].to_broadcast([P, 2, CAP_P]),
                                        rk[:, 2 * ST:2 * TILES, None].to_broadcast([P, 2, CAP_P]), ALU.is_equal).then_inc(hot_ready, 1)
                return hs, gs, pr

            def gates(hs, gs, pr):
                nc.vector.tensor_tensor(gs, hs, pr[:, 0:2 * ST, None].to_broadcast([P, 2 * ST, CAP_S]), ALU.mult).then_inc(hot_ready, 1)
                for e in range(2):
                    ins = nc.vector.tensor_scalar(gate_p[:, e, :], iota[:, 0:PART], comb_rk[:, ST, e:e + 1], comb_pr[:, ST, e:e + 1],
                                                  ALU.is_equal, ALU.mult)
                ins.then_inc(hot_ready, 1)

            parts = one_hots(0, link)
            dve.wait_ge(hot_ready, 2)
            gates(*parts)

            def modulate(job, own, pair=None):
                xe_k = xe.rearrange("p e k n -> p k e n")
                parts = [(job("S", i), 2 * i, 2, slice(0, CAP_S), 0) for i in range(GATHER_S)]
                parts += [(job("P", i), 4 * i, 4, slice(CAP_S, SLOTS), 1) for i in range(GATHER_P)]
                for n, kt, width, slots, w in parts:
                    wait_filled(dve, n, pair)
                    count = slots.stop - slots.start
                    shape = [P, width, 2, count]
                    dst = xe_k[:, kt:kt + width, :, slots]
                    src = bank(n)[:, 0:width * 2 * count].rearrange("p (k e n) -> p k e n", k=width, e=2)
                    own(nc.vector.tensor_tensor(dst, src, amp2[:, kt:kt + width, w:w + 1, None].to_broadcast(shape), ALU.mult))
                    stored(nc.vector.tensor_tensor(dst, dst, mod[:, SHIFT2 + kt:SHIFT2 + kt + width, w:w + 1, None].to_broadcast(shape),
                                                   ALU.add), n)

            def store_prompt_gates(job, pair=None):
                n = job("G_P")
                wait_filled(dve, n, pair)
                for half in range(2):
                    ins = nc.vector.tensor_copy(gT_p[half * 2 * PART:(half + 1) * 2 * PART], bank(n)[0:2 * PART, 0:P])
                stored(ins, n)

            modulate(first_gather, link)
            store_prompt_gates(first_gather)

            def pair_work(pair, last=False):
                J = JOBS_TRUNK
                pair_steps = [0]
                PER_PAIR = 4 + GATHER_S + GATHER_P

                def link_pair(ins):
                    pair_steps[0] += 1
                    ins.then_inc(vec_pair_step, 1)
                    dve.wait_ge(vec_pair_step, pair_steps[0] + pair * PER_PAIR)

                for e in range(2):
                    for r in range(3):
                        n = J + R3(e, r)
                        wait_stored(dve, J + R1(e, r), pair)
                        wait_filled(dve, n, pair)
                        stored(nc.vector.tensor_tensor(h_rows[:, r, :], silu_h[:, (3 * e + r) % 2, :], bank(n), ALU.mult), n)
                        if (e, r) == (0, 1) and not last:
                            wait_filled(dve, J + G_S, pair)
                            parts = one_hots(2 * pair + 2, link_pair)
                            dve.wait_ge(hot_ready, 6 + pair * 4)
                            gates(*parts)
                    rows_s = slice(e * CAP_S, (e + 1) * CAP_S)
                    n = J + Y(e, 0)
                    wait_filled(dve, n, pair)
                    nc.vector.tensor_tensor(y_s[rows_s, 0:512], bank(n)[0:CAP_S], gate2_0[0:CAP_S], ALU.mult)
                    for half in range(2):
                        at = slice(CAP_S + half * PART, CAP_S + (half + 1) * PART)
                        to = slice((2 * half + e) * PART, (2 * half + e + 1) * PART)
                        ins = nc.vector.tensor_tensor(y_p[to], bank(n)[at], gate2_0[at], ALU.mult)
                    stored(ins, n)
                    n = J + Y(e, 1)
                    wait_filled(dve, n, pair)
                    link_pair(nc.vector.tensor_tensor(y_s[rows_s, 512:D], bank(n)[0:CAP_S], gate2_1[0:CAP_S], ALU.mult))
                    stored(nc.vector.tensor_tensor(y_half[rows_s], bank(n)[CAP_S:P], gate2_1[CAP_S:P], ALU.mult), n)
                    wait_stored(dve, n, pair)
                    nc.vector.tensor_tensor(y_s[rows_s, 512:D], y_s[rows_s, 512:D], y_half[rows_s], ALU.add).then_inc(y_added, 1)
                if not last:
                    modulate(next_gather, link_pair, pair)
                for i, t in enumerate(COMB_ORDER):
                    if i == 1 and not last:
                        store_prompt_gates(next_gather, pair)
                    for half in range(2):
                        n = J + COMB(t, half, last)
                        cols = slice(half * 512, (half + 1) * 512)
                        wait_filled(dve, n, pair)
                        stored(nc.vector.tensor_tensor(x[:, t, cols], x[:, t, cols], bank(n), ALU.add), n)
                assert last or pair_steps[0] == PER_PAIR

            with dve.Fori(0, PAIRS - 1) as pair:
                pair_work(pair)
            pair_work(PAIRS - 1, last=True)
            dve.wait_ge(final_loaded, 16)
            final_steps = [0]

            def link_final(ins):
                final_steps[0] += 1
                ins.then_inc(vec_final_step, 1)
                dve.wait_ge(vec_final_step, final_steps[0])

            def scale_out(i):
                t = COMB_ORDER[i]
                nc.vector.scalar_tensor_tensor(y_out[:, t, :], x[:, t, :], stats[:, 140 + i:141 + i], final_w, ALU.mult, ALU.mult)\
                    .then_inc(y_ready, 1)

            dve.wait_ge(y_squared, TILES - 1)
            mean_recip(stats[:, 135:134 + TILES], stats[:, 130:129 + TILES], D, y_recip, link_final)
            dve.wait_ge(y_rs, 1)
            scale_out(0)
            scale_out(1)
            dve.wait_ge(y_squared, TILES)
            mean_recip(stats[:, 134 + TILES:135 + TILES], stats[:, 129 + TILES:130 + TILES], D, y_recip, link_final)
            for i in range(2, TILES - 1):
                scale_out(i)
            dve.wait_ge(y_rs, 2)
            scale_out(TILES - 1)


_INS = ["x_prompt", "x_sample", "state_gla_fwd", "state_gla_bwd", "c", "c_ctx", "ada_w", "ada_b", "norm1_w", "w_in",
        "gla_wa2_f", "gla_ba_f", "gla_wa2_b", "gla_ba_b", "gla_norm_w", "sgu_norm_w", "sgu_ws", "sgu_bs", "w_out",
        "norm2_w", "router_w", "exp_w1", "exp_w3", "exp_w2", "final_norm_w"]
_OUTS = [(1, PROMPT, D), (1, SAMPLE, D), (1, 1, HEADS, DK, DV), (1, 1, HEADS, DK, DV)]


def kernel(**inputs):
    import numpy as _np
    import concourse.bacc as _bacc
    from concourse import mybir as _mybir
    from concourse.bass_utils import run_bass_kernel_spmd as _run

    nc = _bacc.Bacc("TRN2", target_bir_lowering=False, num_devices=1)
    arrays, args = {}, []
    named = [(name, _np.ascontiguousarray(inputs[name])) for name in _INS]
    named += list(zip(("table", "pos_row", "pos_col"), shape_constants()))
    for name, a in named:
        arrays[f"in_{name}_dram"] = a
        args.append(nc.dram_tensor(f"in_{name}_dram", a.shape, _mybir.dt.from_np(a.dtype), kind="ExternalInput").ap())
    for i, shape in enumerate(_OUTS):
        args.append(nc.dram_tensor(f"out_{i}_dram", shape, F32, kind="ExternalOutput").ap())
    trunk_kernel(nc, *args)
    r = _run(nc, [arrays], core_ids=[0])
    return tuple(r.results[0][f"out_{i}_dram"] for i in range(len(_OUTS)))
```
